# Optimizing a Trainium2 kernel written in Bass

```python
import jax, jax.numpy as jnp
from jax import lax
import numpy as np

D_MODEL = 1024
BATCH = 1
SEQ = 512
DEPTH = 1

CHUNK = 64
QBLK = 128
N_MIXERS = 4
N_MEM = 256

ATT_HEADS = 16
ATT_HD = D_MODEL // ATT_HEADS
ML_HEADS = 4
ML_DK = D_MODEL // 2 // ML_HEADS
ML_DV = D_MODEL // ML_HEADS
GLA_HEADS = 4
GLA_DK = D_MODEL // 2 // GLA_HEADS
GLA_DV = D_MODEL // GLA_HEADS
GLA_RANK = 16
GLA_TAU = 16.0
XA_HEADS = 4
XA_HD = D_MODEL // XA_HEADS
D_FF = 2816
CONV_W = 3

DN_ALPHA = (2.0 * DEPTH) ** 0.25
DN_BETA = (8.0 * DEPTH) ** -0.25
LN_EPS = 1e-5
RMS_EPS = 1e-6
FOX_F_BIAS = 2.0
ML_F_BIAS = 3.0

SB_IN = 3 * D_MODEL
FOX_IN = 3 * D_MODEL + ATT_HEADS
ML_WIDTHS = [ML_HEADS * ML_DK, ML_HEADS * ML_DK, ML_HEADS * ML_DV, ML_HEADS * ML_DV, ML_HEADS, ML_HEADS]
GLA_WIDTHS = [GLA_HEADS * GLA_DK, GLA_HEADS * GLA_DK, GLA_HEADS * GLA_DV, GLA_HEADS * GLA_DV, GLA_RANK]


F32 = jnp.float32

def _split_cols(t, widths):
    idx = [int(i) for i in np.cumsum(widths)[:-1]]
    return jnp.split(t, idx, axis=-1)

def _heads(t, n):
    b, s, _ = t.shape
    return t.reshape(b, s, n, -1).transpose(0, 2, 1, 3)

def _merge(t):
    b, n, s, d = t.shape
    return t.transpose(0, 2, 1, 3).reshape(b, s, n * d)

def _to_chunks(t):
    b, hh, s = t.shape[:3]
    return jnp.moveaxis(t.reshape(b, hh, s // CHUNK, CHUNK, *t.shape[3:]), 2, 0)

def _from_chunks(t):
    t = jnp.moveaxis(t, 0, 2)
    return t.reshape(t.shape[0], t.shape[1], -1, *t.shape[4:])

def layer_norm(x, g, b):
    xf = x.astype(F32)
    mu = jnp.mean(xf, -1, keepdims=True)
    var = jnp.mean(jnp.square(xf - mu), -1, keepdims=True)
    return ((xf - mu) * lax.rsqrt(var + LN_EPS) * g + b).astype(x.dtype)

def stick_breaking_core(q, k, v):
    seq = q.shape[2]
    scale = q.shape[-1] ** -0.5
    qf, kf, vf = q.astype(F32), k.astype(F32), v.astype(F32)
    outs = []
    for start in range(0, seq, QBLK):
        end = start + QBLK
        z = jnp.einsum('bhtd,bhsd->bhts', qf[:, :, start:end], kf[:, :, :end]) * scale
        earlier = jnp.arange(end)[None, :] < jnp.arange(start, end)[:, None]
        log_keep = jnp.where(earlier, jax.nn.log_sigmoid(-z), 0.0)
        csum = jnp.cumsum(log_keep, axis=-1)
        log_w = jax.nn.log_sigmoid(z) + (csum[..., -1:] - csum)
        w = jnp.where(earlier, jnp.exp(log_w), 0.0)
        outs.append(jnp.einsum('bhts,bhsd->bhtd', w, vf[:, :, :end]))
    return jnp.concatenate(outs, axis=2).astype(v.dtype)

def mixer_stick_breaking(h, w_in):
    q, k, v = jnp.split(h @ w_in, 3, axis=-1)
    o = stick_breaking_core(_heads(q, ATT_HEADS), _heads(k, ATT_HEADS), _heads(v, ATT_HEADS))
    return _merge(o)

def forgetting_core(q, k, v, log_f):
    seq = q.shape[2]
    scale = q.shape[-1] ** -0.5
    qf, kf, vf = q.astype(F32), k.astype(F32), v.astype(F32)
    cum = jnp.cumsum(log_f.astype(F32), axis=-1)
    outs = []
    for start in range(0, seq, QBLK):
        end = start + QBLK
        z = jnp.einsum('bhtd,bhsd->bhts', qf[:, :, start:end], kf[:, :, :end]) * scale
        z = z + cum[:, :, start:end, None] - cum[:, :, None, :end]
        allowed = jnp.arange(end)[None, :] <= jnp.arange(start, end)[:, None]
        p = jax.nn.softmax(jnp.where(allowed, z, -jnp.inf), axis=-1)
        outs.append(jnp.einsum('bhts,bhsd->bhtd', p, vf[:, :, :end]))
    return jnp.concatenate(outs, axis=2).astype(v.dtype)

def mixer_forgetting(h, w_in, b_f):
    qkv, f_pre = _split_cols(h @ w_in, [3 * D_MODEL, ATT_HEADS])
    q, k, v = jnp.split(qkv, 3, axis=-1)
    log_f = jnp.swapaxes(jax.nn.log_sigmoid((f_pre + b_f).astype(F32)), 1, 2)
    o = forgetting_core(_heads(q, ATT_HEADS), _heads(k, ATT_HEADS), _heads(v, ATT_HEADS), log_f)
    return _merge(o)

def mlstm_core(q, k, v, i_pre, f_pre):
    b, nh, _, dk = q.shape
    dv = v.shape[-1]
    causal = jnp.tril(jnp.ones((CHUNK, CHUNK), dtype=bool))
    xs = (_to_chunks(q.astype(F32)), _to_chunks(k.astype(F32)), _to_chunks(v.astype(F32)),
          _to_chunks(i_pre.astype(F32)), _to_chunks(jax.nn.log_sigmoid(f_pre.astype(F32))))

    def step(carry, blk):
        c_st, n_st, m_st = carry
        qb, kb, vb, ib, lfb = blk
        bcum = jnp.cumsum(lfb, axis=-1)
        d = jnp.where(causal, bcum[..., :, None] - bcum[..., None, :] + ib[..., None, :], -jnp.inf)
        inter = bcum + m_st[..., None]
        m_t = jnp.maximum(inter, jnp.max(d, axis=-1))
        w_intra = jnp.exp(d - m_t[..., None])
        w_inter = jnp.exp(inter - m_t)
        qk = jnp.einsum('bhtd,bhsd->bhts', qb, kb) * w_intra
        num = w_inter[..., None] * jnp.einsum('bhtd,bhde->bhte', qb, c_st) + jnp.einsum('bhts,bhse->bhte', qk, vb)
        den = w_inter * jnp.einsum('bhtd,bhd->bht', qb, n_st) + jnp.sum(qk, axis=-1)
        h_out = num / jnp.maximum(jnp.abs(den), jnp.exp(-m_t))[..., None]
        m_new = m_t[..., -1]
        decay = jnp.exp(bcum[..., -1] + m_st - m_new)
        kw = kb * jnp.exp(bcum[..., -1:] - bcum + ib - m_new[..., None])[..., None]
        c_new = decay[..., None, None] * c_st + jnp.einsum('bhsd,bhse->bhde', kw, vb)
        n_new = decay[..., None] * n_st + jnp.sum(kw, axis=2)
        return (c_new, n_new, m_new), h_out

    init = (jnp.zeros((b, nh, dk, dv), F32), jnp.zeros((b, nh, dk), F32), jnp.zeros((b, nh), F32))
    _, hs = lax.scan(step, init, xs)
    return _from_chunks(hs).astype(v.dtype)

def mixer_mlstm(h, w_in, b_i, b_f):
    q, k, v, o, i_pre, f_pre = _split_cols(h @ w_in, ML_WIDTHS)
    i_pre = jnp.swapaxes((i_pre + b_i).astype(F32), 1, 2)
    f_pre = jnp.swapaxes((f_pre + b_f).astype(F32), 1, 2)
    hh = mlstm_core(_heads(q, ML_HEADS), _heads(k, ML_HEADS) * (ML_DK ** -0.5), _heads(v, ML_HEADS), i_pre, f_pre)
    return _merge(hh) * jax.nn.sigmoid(o)

def gla_core(q, k, v, log_a):
    b, nh, _, dk = q.shape
    dv = v.shape[-1]
    causal = jnp.tril(jnp.ones((CHUNK, CHUNK), dtype=bool))[:, :, None]
    xs = (_to_chunks(q.astype(F32)), _to_chunks(k.astype(F32)), _to_chunks(v.astype(F32)), _to_chunks(log_a.astype(F32)))

    def step(state, blk):
        qb, kb, vb, lab = blk
        bcum = jnp.cumsum(lab, axis=2)
        rel = jnp.where(causal, bcum[:, :, :, None, :] - bcum[:, :, None, :, :], -jnp.inf)
        att = jnp.einsum('bhtd,bhsd,bhtsd->bhts', qb, kb, jnp.exp(rel))
        o = jnp.einsum('bhts,bhse->bhte', att, vb) + jnp.einsum('bhtd,bhde->bhte', qb * jnp.exp(bcum), state)
        blast = bcum[:, :, -1:, :]
        new_state = jnp.exp(blast[:, :, 0, :])[..., None] * state + jnp.einsum('bhsd,bhse->bhde', kb * jnp.exp(blast - bcum), vb)
        return new_state, o

    _, os_ = lax.scan(step, jnp.zeros((b, nh, dk, dv), F32), xs)
    return _from_chunks(os_)

def mixer_gla(h, w_in, w_a2, b_a, norm_g):
    q, k, v, r, a_low = _split_cols(h @ w_in, GLA_WIDTHS)
    log_a = jax.nn.log_sigmoid((a_low @ w_a2 + b_a).astype(F32)) / GLA_TAU
    o = gla_core(_heads(q, GLA_HEADS) * (GLA_DK ** -0.5), _heads(k, GLA_HEADS), _heads(v, GLA_HEADS), _heads(log_a, GLA_HEADS))
    o = o * lax.rsqrt(jnp.mean(jnp.square(o), -1, keepdims=True) + RMS_EPS) * norm_g
    return _merge(o.astype(h.dtype)) * jax.nn.silu(r)

def mem_cross_attn(h, mem, w_q, w_kv, w_o):
    q = _heads(h @ w_q, XA_HEADS).astype(F32)
    k, v = jnp.split(mem @ w_kv, 2, axis=-1)
    k = _heads(k, XA_HEADS).astype(F32)
    v = _heads(v, XA_HEADS).astype(F32)
    p = jax.nn.softmax(jnp.einsum('bhtd,bhmd->bhtm', q, k) * (XA_HD ** -0.5), axis=-1)
    o = jnp.einsum('bhtm,bhmd->bhtd', p, v).astype(h.dtype)
    return _merge(o) @ w_o

def conv_ffn(h, w_up, conv_w, conv_b, w_down):
    u = h @ w_up
    ch = u.shape[-1]
    u = lax.conv_general_dilated(u, conv_w, window_strides=(1,), padding=((CONV_W - 1, 0),),
                                 dimension_numbers=('NWC', 'WIO', 'NWC'), feature_group_count=ch) + conv_b
    g, val = jnp.split(u, 2, axis=-1)
    return (jax.nn.gelu(g) * val) @ w_down

def _dense(key, shape, fan_in, gain=1.0):
    return jax.random.normal(key, shape, F32) * (gain * fan_in ** -0.5)

def first_inputs(seed: int = 0) -> dict:
    key = jax.random.key(seed)
    ks = iter(jax.random.split(key, 32))
    D = D_MODEL
    n_occ = [len(range(m, DEPTH, N_MIXERS)) for m in range(N_MIXERS)]
    nrm = lambda shape, s: jax.random.normal(next(ks), shape, F32) * s
    return {
        'x': jax.random.normal(next(ks), (BATCH, SEQ, D), F32),
        'mem': jax.random.normal(next(ks), (BATCH, N_MEM, D), F32),
        'ln_g': 1.0 + nrm((DEPTH, 3, D), 0.02),
        'ln_b': nrm((DEPTH, 3, D), 0.02),
        'mix_wo': _dense(next(ks), (DEPTH, D, D), D, DN_BETA),
        'sb_win': _dense(next(ks), (n_occ[0], D, SB_IN), D),
        'fox_win': _dense(next(ks), (n_occ[1], D, FOX_IN), D),
        'fox_bf': FOX_F_BIAS + nrm((n_occ[1], ATT_HEADS), 0.1),
        'ml_win': _dense(next(ks), (n_occ[2], D, sum(ML_WIDTHS)), D),
        'ml_bi': nrm((n_occ[2], ML_HEADS), 0.1),
        'ml_bf': ML_F_BIAS + nrm((n_occ[2], ML_HEADS), 0.1),
        'gla_win': _dense(next(ks), (n_occ[3], D, sum(GLA_WIDTHS)), D),
        'gla_wa2': _dense(next(ks), (n_occ[3], GLA_RANK, GLA_HEADS * GLA_DK), GLA_RANK),
        'gla_ba': nrm((n_occ[3], GLA_HEADS * GLA_DK), 0.1),
        'gla_norm_g': 1.0 + nrm((n_occ[3], GLA_DV), 0.02),
        'xa_wq': _dense(next(ks), (DEPTH, D, D), D),
        'xa_wkv': _dense(next(ks), (DEPTH, D, 2 * D), D),
        'xa_wo': _dense(next(ks), (DEPTH, D, D), D, DN_BETA),
        'ffn_up': _dense(next(ks), (DEPTH, D, 2 * D_FF), D),
        'ffn_conv': _dense(next(ks), (DEPTH, CONV_W, 1, 2 * D_FF), CONV_W),
        'ffn_conv_b': nrm((DEPTH, 2 * D_FF), 0.02),
        'ffn_down': _dense(next(ks), (DEPTH, D_FF, D), D_FF, DN_BETA),
    }

def first_block(x, mem, ln_g, ln_b, mix_wo, sb_win, fox_win, fox_bf, ml_win, ml_bi, ml_bf,
              gla_win, gla_wa2, gla_ba, gla_norm_g, xa_wq, xa_wkv, xa_wo,
              ffn_up, ffn_conv, ffn_conv_b, ffn_down):
    h = x
    for layer in range(DEPTH):
        kind = layer % N_MIXERS
        occ = layer // N_MIXERS
        if kind == 0:
            y = mixer_stick_breaking(h, sb_win[occ])
        elif kind == 1:
            y = mixer_forgetting(h, fox_win[occ], fox_bf[occ])
        elif kind == 2:
            y = mixer_mlstm(h, ml_win[occ], ml_bi[occ], ml_bf[occ])
        else:
            y = mixer_gla(h, gla_win[occ], gla_wa2[occ], gla_ba[occ], gla_norm_g[occ])
        h = layer_norm(DN_ALPHA * h + y @ mix_wo[layer], ln_g[layer, 0], ln_b[layer, 0])
        h = layer_norm(DN_ALPHA * h + mem_cross_attn(h, mem, xa_wq[layer], xa_wkv[layer], xa_wo[layer]),
                       ln_g[layer, 1], ln_b[layer, 1])
        h = layer_norm(DN_ALPHA * h + conv_ffn(h, ffn_up[layer], ffn_conv[layer], ffn_conv_b[layer], ffn_down[layer]),
                       ln_g[layer, 2], ln_b[layer, 2])
    return h


HEAD_A = 64
N_HEADS_A = 8
C_A = N_HEADS_A * HEAD_A
R_DECAY = 64
R_ICLR = 64
R_VRES = 32
GN_EPS = HEAD_A * 1e-5
C_B = 512
C_C = 512
POOL_WINDOWS = (2, 4, 8, 16)
N_POOL_GROUPS = 4
G_C = C_C // N_POOL_GROUPS
N_BRANCH = 3
BRANCH_W = 512
NORM_EPS = 1e-6

N_RWKV_IN = 4 * C_A + R_DECAY + R_ICLR
N_CONV_IN = 4 * C_B
N_POOL_IN = 2 * C_C
N_GATE_IN = N_BRANCH * D_MODEL
N_IN = N_RWKV_IN + N_CONV_IN + N_POOL_IN + N_GATE_IN


def rms_norm(x, g):
    xf = x.astype(jnp.float32)
    y = xf * lax.rsqrt(jnp.mean(xf * xf, axis=-1, keepdims=True) + NORM_EPS)
    return (y * g.astype(jnp.float32)).astype(x.dtype)

def token_shift(p, mu):
    p_prev = jnp.pad(p, ((0, 0), (1, 0), (0, 0)))[:, :-1]
    return p + (p_prev - p) * mu

def _rwkv7_step(state, inp):
    r_t, w_t, k_t, v_t, a_t, b_t = inp
    sa = jnp.einsum('bhvk,bhk->bhv', state, a_t)
    state = (state * w_t[:, :, None, :] + sa[..., None] * b_t[:, :, None, :]
             + v_t[..., None] * k_t[:, :, None, :])
    y_t = jnp.einsum('bhvk,bhk->bhv', state, r_t)
    return state, y_t

def rwkv7_branch(p_rwkv, w0, w_up, a0, a_up, k_k, k_a, r_k, gn_w, gn_b, v_first, vres):
    bsz, slen, _ = p_rwkv.shape
    dt = p_rwkv.dtype
    f32 = jnp.float32
    r, k, v, z, wd, ad = jnp.split(
        p_rwkv, [C_A, 2 * C_A, 3 * C_A, 4 * C_A, 4 * C_A + R_DECAY], axis=-1)
    w = -jax.nn.softplus(-(w0 + jnp.tanh(wd) @ w_up).astype(f32)) - 0.5
    v_layer = v
    if vres is not None:
        vd, v0, v_up = vres
        v = v + (v_first - v) * jax.nn.sigmoid(v0 + vd @ v_up)
    a = jax.nn.sigmoid(a0 + ad @ a_up)
    heads = lambda t: t.reshape(bsz, slen, N_HEADS_A, HEAD_A).astype(f32)
    kk = heads(k * k_k)
    kk = kk / jnp.maximum(jnp.sqrt(jnp.sum(kk * kk, axis=-1, keepdims=True)), 1e-12)
    k = k * (1 + (a - 1) * k_a)
    rh, kh, vh, ah = heads(r), heads(k), heads(v), heads(a)
    decay = heads(jnp.exp(-jnp.exp(w)))
    seq_major = lambda t: jnp.transpose(t, (1, 0, 2, 3))
    state0 = jnp.zeros((bsz, N_HEADS_A, HEAD_A, HEAD_A), f32)
    _, y = lax.scan(_rwkv7_step, state0,
                    (seq_major(rh), seq_major(decay), seq_major(kh), seq_major(vh),
                     seq_major(-kk), seq_major(kk * ah)))
    y = jnp.transpose(y, (1, 0, 2, 3))
    mean = jnp.mean(y, axis=-1, keepdims=True)
    var = jnp.mean(jnp.square(y - mean), axis=-1, keepdims=True)
    y = ((y - mean) * lax.rsqrt(var + GN_EPS)).reshape(bsz, slen, C_A)
    y = y * gn_w.astype(f32) + gn_b.astype(f32)
    bonus = jnp.sum(rh * kh * r_k.astype(f32), axis=-1, keepdims=True) * vh
    y = y + bonus.reshape(bsz, slen, C_A)
    out = y.astype(dt) * jax.nn.silu(z)
    return out, v_layer

def short_conv_branch(p_conv, conv_w):
    b, c, u, z = jnp.split(p_conv, 4, axis=-1)
    cu = c * u
    y = lax.conv_general_dilated(
        cu, conv_w[:, None, :], window_strides=(1,), padding=[(CONV_W - 1, 0)],
        dimension_numbers=('NWC', 'WIO', 'NWC'), feature_group_count=C_B)
    return b * y * jax.nn.silu(z)

def pool_branch(p_pool, pool_w, pool_scale):
    u, z = jnp.split(p_pool, 2, axis=-1)
    bsz, slen, _ = u.shape
    f32 = jnp.float32
    ug = u.reshape(bsz, slen, N_POOL_GROUPS, G_C).astype(f32)
    csum = jnp.cumsum(ug, axis=1)
    t = jnp.arange(1, slen + 1, dtype=f32)
    outs = []
    for gi, win in enumerate(POOL_WINDOWS):
        cg = csum[:, :, gi]
        prev = jnp.pad(cg, ((0, 0), (win, 0), (0, 0)))[:, :slen]
        cnt = jnp.minimum(t, float(win))[None, :, None]
        outs.append((cg - prev) / cnt - ug[:, :, gi])
    pooled = jnp.stack(outs, axis=2)
    mixed = jnp.einsum('bsgc,gcd->bsgd', pooled, pool_w.astype(f32)).reshape(bsz, slen, C_C)
    return (mixed * pool_scale.astype(f32)).astype(u.dtype) * jax.nn.silu(z)

def second_inputs(seed: int = 0) -> dict:
    key = jax.random.key(seed)
    ks = iter(jax.random.split(key, 32))
    nrm = lambda shape, scale: scale * jax.random.normal(next(ks), shape, jnp.float32)
    uni = lambda shape, lo, hi: jax.random.uniform(next(ks), shape, jnp.float32, lo, hi)
    L = DEPTH
    Lv = DEPTH - 1
    return {
        'x': nrm((BATCH, SEQ, D_MODEL), 1.0),
        'pre_norm_w': 1.0 + nrm((L, D_MODEL), 0.1),
        'post_norm_w': 1.0 + nrm((L, D_MODEL), 0.1),
        'w_in': nrm((L, D_MODEL, N_IN), D_MODEL ** -0.5),
        'mu_shift': uni((L, N_RWKV_IN), 0.0, 1.0),
        'rwkv_w0': uni((L, C_A), -6.0, -1.0),
        'rwkv_w_up': nrm((L, R_DECAY, C_A), 0.1 * R_DECAY ** -0.5),
        'rwkv_a0': nrm((L, C_A), 0.1),
        'rwkv_a_up': nrm((L, R_ICLR, C_A), R_ICLR ** -0.5),
        'rwkv_k_k': 0.85 + nrm((L, C_A), 0.05),
        'rwkv_k_a': 1.0 + nrm((L, C_A), 0.05),
        'rwkv_r_k': nrm((L, N_HEADS_A, HEAD_A), 0.1),
        'rwkv_gn_w': 1.0 + nrm((L, C_A), 0.1),
        'rwkv_gn_b': nrm((L, C_A), 0.02),
        'vres_down': nrm((Lv, D_MODEL, R_VRES), D_MODEL ** -0.5),
        'vres_mu': uni((Lv, R_VRES), 0.0, 1.0),
        'vres_v0': nrm((Lv, C_A), 0.1),
        'vres_up': nrm((Lv, R_VRES, C_A), R_VRES ** -0.5),
        'conv_w': nrm((L, CONV_W, C_B), CONV_W ** -0.5),
        'pool_w': nrm((L, N_POOL_GROUPS, G_C, G_C), G_C ** -0.5),
        'pool_scale': 1.0 + nrm((L, C_C), 0.1),
        'w_branch': nrm((L, N_BRANCH, BRANCH_W, D_MODEL), BRANCH_W ** -0.5),
        'w_out': nrm((L, D_MODEL, D_MODEL), D_MODEL ** -0.5),
    }

def second_block(x, pre_norm_w, post_norm_w, w_in, mu_shift, rwkv_w0, rwkv_w_up, rwkv_a0,
              rwkv_a_up, rwkv_k_k, rwkv_k_a, rwkv_r_k, rwkv_gn_w, rwkv_gn_b, vres_down,
              vres_mu, vres_v0, vres_up, conv_w, pool_w, pool_scale, w_branch, w_out):
    bsz, slen, _ = x.shape
    v_first = None
    for l in range(DEPTH):
        h = rms_norm(x, pre_norm_w[l])
        if l == 0:
            w_cat = w_in[l]
        else:
            w_cat = jnp.concatenate([w_in[l], vres_down[l - 1]], axis=1)
        p = h @ w_cat
        p_rwkv, p_conv, p_pool, p_gate = jnp.split(
            p[..., :N_IN],
            [N_RWKV_IN, N_RWKV_IN + N_CONV_IN, N_RWKV_IN + N_CONV_IN + N_POOL_IN], axis=-1)
        p_rwkv = token_shift(p_rwkv, mu_shift[l])
        if l == 0:
            vres = None
        else:
            vres = (token_shift(p[..., N_IN:], vres_mu[l - 1]), vres_v0[l - 1], vres_up[l - 1])
        y_a, v_layer = rwkv7_branch(p_rwkv, rwkv_w0[l], rwkv_w_up[l], rwkv_a0[l], rwkv_a_up[l],
                                    rwkv_k_k[l], rwkv_k_a[l], rwkv_r_k[l], rwkv_gn_w[l],
                                    rwkv_gn_b[l], v_first, vres)
        if l == 0:
            v_first = v_layer
        y_b = short_conv_branch(p_conv, conv_w[l])
        y_c = pool_branch(p_pool, pool_w[l], pool_scale[l])
        ys = jnp.stack([y_a, y_b, y_c], axis=0)
        proj = jnp.einsum('nbsc,ncd->nbsd', ys, w_branch[l])
        gates = jax.nn.sigmoid(p_gate.reshape(bsz, slen, N_BRANCH, D_MODEL))
        merged = jnp.einsum('bsnd,nbsd->bsd', gates, proj)
        out = merged @ w_out[l]
        x = x + rms_norm(out, post_norm_w[l])
    return x


def setup_inputs(seed=0):
    out = dict(first_inputs(seed))
    for name, value in second_inputs(seed + 1).items():
        if name != "x":
            out[name + "_2"] = value
    return out


def reference(
    x, mem, ln_g, ln_b, mix_wo, sb_win, fox_win, fox_bf, ml_win, ml_bi, ml_bf, gla_win, gla_wa2,
    gla_ba, gla_norm_g, xa_wq, xa_wkv, xa_wo, ffn_up, ffn_conv, ffn_conv_b, ffn_down,
    pre_norm_w_2, post_norm_w_2, w_in_2, mu_shift_2, rwkv_w0_2, rwkv_w_up_2, rwkv_a0_2,
    rwkv_a_up_2, rwkv_k_k_2, rwkv_k_a_2, rwkv_r_k_2, rwkv_gn_w_2, rwkv_gn_b_2, vres_down_2,
    vres_mu_2, vres_v0_2, vres_up_2, conv_w_2, pool_w_2, pool_scale_2, w_branch_2, w_out_2,
):
    x = first_block(
        x, mem, ln_g, ln_b, mix_wo, sb_win, fox_win, fox_bf, ml_win, ml_bi, ml_bf, gla_win,
        gla_wa2, gla_ba, gla_norm_g, xa_wq, xa_wkv, xa_wo, ffn_up, ffn_conv, ffn_conv_b,
        ffn_down,
    )
    return second_block(
        x, pre_norm_w_2, post_norm_w_2, w_in_2, mu_shift_2, rwkv_w0_2, rwkv_w_up_2, rwkv_a0_2,
        rwkv_a_up_2, rwkv_k_k_2, rwkv_k_a_2, rwkv_r_k_2, rwkv_gn_w_2, rwkv_gn_b_2, vres_down_2,
        vres_mu_2, vres_v0_2, vres_up_2, conv_w_2, pool_w_2, pool_scale_2, w_branch_2, w_out_2,
    )


_drawn_inputs = setup_inputs


def setup_inputs(seed=0):
    import zlib

    import numpy as np

    out = dict(_drawn_inputs(seed))
    spreads = {}
    factors = {'ffn_conv_b': 4.148,
     'rwkv_w_up_2': 28.766,
     'rwkv_a0_2': 4.333,
     'rwkv_k_k_2': 13.595,
     'rwkv_gn_b_2': 7.606,
     'rwkv_k_a_2': 2.693}
    for name, (base, spread) in spreads.items():
        noise = np.random.default_rng([zlib.crc32(name.encode()), seed]).standard_normal(out[name].shape)
        drawn = base * np.exp(spread * noise) if base else spread * noise
        out[name] = __import__('jax').numpy.asarray(drawn.astype(out[name].dtype))
    for name, factor in factors.items():
        out[name] = (out[name] * factor).astype(out[name].dtype)
    return out
```

```python
import numpy as np
from contextlib import ExitStack

import concourse.bass as bass
from concourse import mybir

F32 = mybir.dt.float32
F32R = mybir.dt.float32r
ALU = mybir.AluOpType
ACT = mybir.ActivationFunctionType

P = 128
SEQ = 512
MEM = 256
D = 1024
KB = D // P
HD_A = 64
PAIRS = D // P
XA_HEADS = 4
D_FF = 2816
FFB = D_FF // P
NS = SEQ // P
CA = 4
CH = P
ALPHA = 2.0 ** 0.25
LN_EPS = 1e-5
RMS_EPS = 1e-6
GN_EPS = HD_A * 1e-5
DECAY = -float(np.exp(-0.5))

UNIT = 8 * P
STAGE_UNITS = [("mem_kv", 16), ("sb", 24), ("wo", 8), ("xq", 8), ("xo", 8), ("up", 44), ("down", 24),
               ("rwkv", 17), ("conv", 16), ("pool", 8), ("branch", 36), ("out", 8)]
U0, _u = {}, 0
for _name, _n in STAGE_UNITS:
    U0[_name] = _u
    _u += _n
UNITS = _u
DOWN_UNITS = 3

VEC_WIDTHS = [("ln_g", 24), ("ln_b", 24), ("ffn_conv", 3 * 2 * FFB), ("ffn_conv_b", 2 * FFB), ("pre", 8), ("post", 8),
              ("mu", 17), ("w0", 4), ("a0", 4), ("k_k", 4), ("k_a", 4), ("r_k", 4), ("gn_w", 4), ("gn_b", 4),
              ("conv_w", 12), ("pool_scale", 4)]
V0, _v = {}, 0
for _name, _n in VEC_WIDTHS:
    V0[_name] = _v
    _v += _n
VEC = _v

LEVELS = [1, 2, 4, 8, 16, 32, 64]
CONST_WIDTHS = [("ident", P), ("mean", P), ("heads", P), ("suffix", P), ("all", P), ("never", P), ("strict", P),
                ("levels", len(LEVELS) * P), ("scan", SEQ)]
C0, _c = {}, 0
for _name, _n in CONST_WIDTHS:
    C0[_name] = _c
    _c += _n
CONST = _c
POOL_WINDOWS = (2, 4, 8, 16)

REGION = {0: (0, 512), 1: (512, 384), 3: (896, 128), 2: (1024, 256)}
SCORES = 1280


def build_block(nc, w, xT, memT, vec, const, small, pool_count, outT):
    ctx = ExitStack()
    with ctx:
        def sem(name):
            return ctx.enter_context(nc.semaphore(name))

        def at(name, shape, kb, dt=F32):
            assert 0 <= kb and BASE + int(kb * 1024) + 4 * int(np.prod(shape[1:])) <= nc.sbuf_usable_end, name
            return nc.alloc_sbuf_tensor_at(name, shape, dt, offset=BASE + int(kb * 1024))

        BASE = 17408
        stage = at("stage", [P, 2, UNIT], 0)
        w_hi = at("w_hi", [P, 2, UNIT], 8, F32R)
        w_lo = at("w_lo", [P, 2, UNIT], 16, F32R)
        H = at("H", [P, KB, SEQ], 32)
        x_hi = at("x_hi", [P, KB, SEQ], 48, F32R)
        x_lo = at("x_lo", [P, KB, SEQ], 64, F32R)
        Y = at("Y", [P, KB, SEQ], 80)
        con = at("con", [P, C0["levels"]], 96)
        vcol = at("vcol", [P, VEC], 99.5)
        suffix = at("suffix", [P, P], 24, F32R)
        every = at("every", [P, P], 24.5, F32R)
        never = at("never", [P, P], 25, F32R)
        ident_r = at("ident_r", [P, P], 25.5, F32R)
        tmp = at("tmp", [P, 2, SEQ], 101.5)
        acc = at("acc", [P, SEQ], 105.5)
        acc2 = at("acc2", [P, SEQ], 107.5)
        square = at("square", [P, SEQ], 109.5)
        mean = at("mean", [P, SEQ], 111.5)
        rstd = at("rstd", [P, SEQ], 113.5)
        A0 = 115.5
        o_hi = at("o_hi", [P, KB, SEQ], A0, F32R)
        o_lo = at("o_lo", [P, KB, SEQ], A0 + 16, F32R)
        mem_k = at("mem_k", [P, KB, MEM], A0 + 32)
        mem_v = at("mem_v", [P, MEM // P, D], A0 + 40)
        m_hi = at("m_hi", [P, KB, MEM], A0 + 48, F32R)
        m_lo = at("m_lo", [P, KB, MEM], A0 + 56, F32R)
        mem = at("mem", [P, KB, MEM], A0 + 64)
        mem_vT = at("mem_vT", [P, 2, MEM], A0 + 72)
        q_sb = at("q_sb", [P, SEQ], A0 + 48)
        k_sb = at("k_sb", [P, SEQ], A0 + 50)
        vT_sb = at("vT_sb", [P, SEQ], A0 + 52)
        v_sb = at("v_sb", [P, NS, P], A0 + 54)
        soft = [at(f"soft{h}", [P, SCORES], 80 + 5 * h) for h in range(2)]
        keep = [at("keep0", [P, SCORES], 90), at("keep1", [P, SCORES], A0 + 56)]
        keep_hi = [at(f"keep_hi{h}", [P, SCORES], A0 + 61 + 5 * h, F32R) for h in range(2)]
        keep_lo = [at(f"keep_lo{h}", [P, SCORES], A0 + 71 + 5 * h, F32R) for h in range(2)]
        xq = at("xq", [P, KB, SEQ], A0 + 48)
        prob = at("prob", [P, 2, NS, MEM], A0 + 64)
        probT = at("probT", [P, 2, MEM // P, SEQ], A0 + 72)
        soft_max = at("soft_max", [P, XA_HEADS, NS], A0 + 80)
        soft_sum = at("soft_sum", [P, XA_HEADS, NS], A0 + 80.25)
        f_hi = at("f_hi", [P, FFB, SEQ], A0, F32R)
        f_lo = at("f_lo", [P, FFB, SEQ], A0 + 44, F32R)
        raw = at("raw", [P, 4, SEQ], 80)
        conv = at("conv", [P, 4, SEQ], 88)
        gate_t = at("gate_t", [P, 2, SEQ], 105.5)

        levels = at("levels", [P, len(LEVELS), P], 26)
        scan_keep = at("scan_keep", [P, SEQ], 29.5)
        sq2 = at("sq2", [P, 2, SEQ], 107.5)
        rw_a = at("rw_a", [P, CA, SEQ], A0)
        rw_rk = at("rw_rk", [P, 2 * CA, SEQ], A0 + 8)
        rw_r, rw_k = rw_rk[:, 0:CA, :], rw_rk[:, CA:2 * CA, :]
        rw_kk = at("rw_kk", [P, CA, SEQ], A0 + 24)
        rw_vz = at("rw_vz", [P, 2 * CA, SEQ], A0 + 32)
        rw_v, rw_z = rw_vz[:, 0:CA, :], rw_vz[:, CA:2 * CA, :]
        rw_L = at("rw_L", [P, CA, SEQ], A0 + 48)
        w_small = at("w_small", [P, 2, SEQ], A0 + 56)
        rw_e = at("rw_e", [P, CA, SEQ], A0 + 60)
        rw_t = at("rw_t", [P, CA, SEQ], A0 + 68)
        lora = at("lora", [P, SEQ], A0 + 84)
        rw_ld = at("rw_ld", [P, CA, SEQ], 80)
        rw_n = at("rw_n", [P, CA, SEQ], 88)
        omm = at("omm", [P, 17], A0 + 88.5)
        cen = at("cen", [P, CA, NS], A0 + 88.75)
        gfac = at("gfac", [P, CA, NS], A0 + 89)
        M = at("M", [P, 8, 4, P], 80)
        tok = at("tok", [P, 3, CA, P], 105.5)
        rh = at("rh", [P, SEQ], 111.5)
        sa = at("sa", [P, SEQ], 113.5)
        AR = at("AR", [P, CA, 2, P], A0 + 60)
        bkv = at("bkv", [P, 3, CA, P], A0 + 64)
        X = at("X", [P, 8, P], A0 + 70)
        Tt = at("Tt", [P, 8, P], A0 + 74)
        R1 = at("R1", [P, 8, P], A0 + 78)
        Mk = at("Mk", [P, 8, P], A0 + 82)
        Sz = at("Sz", [P, 8, HD_A], A0 + 86)
        scr = at("scr", [P, 12], A0 + 89.25)
        g_sq = at("g_sq", [P, CA, SEQ], 80)
        g_mu = at("g_mu", [P, CA, SEQ], 88)
        g_rs = at("g_rs", [P, CA, SEQ], A0 + 60)
        g_sz = at("g_sz", [P, CA, SEQ], A0 + 68)
        ys_hi = at("ys_hi", [P, 3 * CA, SEQ], A0, F32R)
        ys_lo = at("ys_lo", [P, 3 * CA, SEQ], A0 + 24, F32R)
        cb = at("cb", [P, 2, 4, SEQ], 80)
        sg = at("sg", [P, 2, SEQ], A0 + 60)
        pool_n = at("pool_n", [P, 4, SEQ], A0 + 64)
        pt = at("pt", [P, 2, SEQ], A0 + 72)
        pld = at("pld", [P, 2, SEQ], A0 + 76)
        mg_hi = at("mg_hi", [P, KB, SEQ], A0 + 48, F32R)
        mg_lo = at("mg_lo", [P, KB, SEQ], A0 + 64, F32R)
        gates = at("gates", [P, 4, SEQ], A0 + 80)
        bt = at("bt", [P, 4, SEQ], 105.5)

        ps = ctx.enter_context(nc.psum_tensor("ps", [P, 8, 512], F32))

        def scores(h):
            return ps[:, 2 + 3 * h:5 + 3 * h, :].rearrange("p b n -> p (b n)")

        def C(name, n=P):
            return con[:, C0[name]:C0[name] + n]

        def V(name, j=0):
            return vcol[:, bass.ds(V0[name] + j, 1)]

        ident = C("ident")

        landed = [sem(f"landed{j}") for j in range(2)]
        params_in = sem("params_in")
        x_in = sem("x_in")
        mem_in = sem("mem_in")
        whi_made = sem("whi_made")
        wlo_made = sem("wlo_made")
        unit_done = sem("unit_done")
        evac = sem("evac")
        mask_made = sem("mask_made")
        h_split = sem("h_split")
        m_hi_made = sem("m_hi_made")
        m_split = sem("m_split")
        mv_turned = sem("mv_turned")
        mv_taken = sem("mv_taken")
        out_sent = sem("out_sent")

        EV0 = {}
        n_ev = 0
        for name, n in (("mem_kv", 16), ("sb", 24), ("wo", 8), ("xq", 8), ("xo", 8), ("up", 44), ("down", 8),
                        ("rwkv", 17), ("conv", 16), ("pool", 8), ("branch", 24), ("out", 8)):
            EV0[name] = n_ev
            n_ev += n
        CREDIT = 2

        EACH = {"mean_made": dict(wo=1, xo=1, down=1), "var_made0": dict(wo=2, xo=2, down=2),
                "centred": dict(wo=KB, xo=KB, down=KB), "h_made": dict(wo=KB, xo=KB, down=KB),
                "ln_made": dict(wo=1, xo=1, down=1, pre=1, out=1), "rstd_made": dict(wo=1, xo=1, down=1, pre=1, out=1),
                "var_made": dict(wo=1, xo=1, down=1, pre=1, out=1),
                "y_made": dict(wo=KB + CREDIT, xo=KB + CREDIT, down=KB + CREDIT),
                "acc_made": dict(wo=KB + 1, xo=KB + 1, down=KB + 1),
                "acc2_made": dict(wo=KB + 1, xo=KB + 1, down=KB + 1, out=KB + 1),
                "sq_made": dict(wo=KB, xo=KB, down=KB, pre=KB, out=KB),
                "sums_done": dict(wo=2, xo=2, down=2, pre=KB, out=1),
                "normed": dict(wo=KB, xo=KB, down=KB, pre=KB), "xhi_made": dict(wo=KB, xo=KB, pre=KB),
                "x_ready": dict(wo=KB, xo=KB, pre=KB)}
        BEFORE = {s: {n: sum(list(c.values())[:k]) for k, n in enumerate(c)} for s, c in EACH.items()}

        NORMS = {"wo": 0, "xo": 1, "down": 2}
        xin_hi = sem("xin_hi")
        mean_made = sem("mean_made")
        var_made0 = sem("var_made0")
        centred = sem("centred")
        ln_made = sem("ln_made")
        rstd_made = sem("rstd_made")
        y_made = sem("y_made")
        acc_made = sem("acc_made")
        sq_made = sem("sq_made")
        acc2_made = sem("acc2_made")
        sums_done = sem("sums_done")
        var_made = sem("var_made")
        normed = sem("normed")
        h_made = sem("h_made")
        xhi_made = sem("xhi_made")
        x_ready = sem("x_ready")

        sb_scored = sem("sb_scored")
        sb_abs = sem("sb_abs")
        sb_exp = sem("sb_exp")
        sb_ln = sem("sb_ln")
        sb_keep = sem("sb_keep")
        sb_khi = sem("sb_khi")
        sb_klo = sem("sb_klo")
        sb_summed = sem("sb_summed")
        sb_w = sem("sb_w")
        sb_vturn = sem("sb_vturn")
        sb_v = sem("sb_v")
        sb_pv = sem("sb_pv")
        sb_ohi = sem("sb_ohi")
        sb_o = sem("sb_o")

        xa_scored = sem("xa_scored")
        xa_max = sem("xa_max")
        xa_nmax = sem("xa_nmax")
        xa_exp = sem("xa_exp")
        xa_rec = sem("xa_rec")
        xa_prob = sem("xa_prob")
        xa_turned = sem("xa_turned")
        xa_pT0 = sem("xa_pT0")
        xa_pT1 = sem("xa_pT1")
        xa_pv = sem("xa_pv")
        xa_ohi = sem("xa_ohi")
        xa_o = sem("xa_o")

        ff_conv = sem("ff_conv")
        ff_tap = sem("ff_tap")
        ff_sq = sem("ff_sq")
        ff_poly = sem("ff_poly")
        ff_arg = sem("ff_arg")
        ff_sig = sem("ff_sig")
        ff_vg = sem("ff_vg")
        ff_f = sem("ff_f")
        ff_hi = sem("ff_hi")
        ff_made = sem("ff_made")

        rw_shift0_s = sem("rw_shift0")
        rw_shifted_s = sem("rw_shifted")
        rw_tanh_s = sem("rw_tanh")
        rw_lora_mm_s = sem("rw_lora_mm")
        rw_sig_s = sem("rw_sig")
        rw_scan_s = sem("rw_scan")
        rw_kksq_s = sem("rw_kksq")
        rw_ss_mm_s = sem("rw_ss_mm")
        rw_max_s = sem("rw_max")
        rw_sqrt_s = sem("rw_sqrt")
        rw_lc_s = sem("rw_lc")
        rw_e_s = sem("rw_e")
        rw_barg_s = sem("rw_barg")
        rw_bmm_s = sem("rw_bmm")
        rw_bonus_s = sem("rw_bonus")
        rw_prep_s = sem("rw_prep")
        small_in_s = sem("small_in")
        levels_in_s = sem("levels_in")
        pooln_in_s = sem("pooln_in")
        ch_ar_s = sem("ch_ar")
        ch_bkv_s = sem("ch_bkv")
        ch_turned_s = sem("ch_turned")
        ch_b_s = sem("ch_b")
        ch_k_s = sem("ch_k")
        ch_vt_s = sem("ch_vt")
        ch_scored_s = sem("ch_scored")
        ch_ab_s = sem("ch_ab")
        ch_m_s = sem("ch_m")
        ch_mask_s = sem("ch_mask")
        ch_y1_s = sem("ch_y1")
        ch_t1_s = sem("ch_t1")
        ch_tt0_s = sem("ch_tt0")
        ch_x0_s = sem("ch_x0")
        ch_mk_s = sem("ch_mk")
        ch_r_s = sem("ch_r")
        ch_rb_s = sem("ch_rb")
        ch_xmm_s = sem("ch_xmm")
        ch_ymm_s = sem("ch_ymm")
        ch_xn_s = sem("ch_xn")
        ch_yn_s = sem("ch_yn")
        ch_rh_mm_s = sem("ch_rh_mm")
        ch_rh_s = sem("ch_rh")
        ch_sa_mm_s = sem("ch_sa_mm")
        ch_sa_s = sem("ch_sa")
        ch_y_mm_s = sem("ch_y_mm")
        ch_s_mm_s = sem("ch_s_mm")
        ch_y_s = sem("ch_y")
        ch_s0_s = sem("ch_s0")
        ch_s_s = sem("ch_s")
        ch_wait_s = sem("ch_wait")
        gn_sq_s = sem("gn_sq")
        gn_mm_s = sem("gn_mm")
        gn_mu_s = sem("gn_mu")
        gn_v_s = sem("gn_v")
        gn_v2_s = sem("gn_v2")
        gn_ln_s = sem("gn_ln")
        gn_rs_s = sem("gn_rs")
        gn_out_s = sem("gn_out")
        gn_hi_s = sem("gn_hi")
        gn_lo_s = sem("gn_lo")
        gn_sig_s = sem("gn_sig")
        cv_sig_s = sem("cv_sig")
        cv_out_s = sem("cv_out")
        cv_hi_s = sem("cv_hi")
        cv_lo_s = sem("cv_lo")
        cv_link_s = sem("cv_link")
        pl_sig_s = sem("pl_sig")
        pl_pooled_s = sem("pl_pooled")
        pl_mm_s = sem("pl_mm")
        pl_out_s = sem("pl_out")
        pl_hi_s = sem("pl_hi")
        pl_lo_s = sem("pl_lo")
        br_taken_s = sem("br_taken")
        br_sum_s = sem("br_sum")
        mg_hi_made_s = sem("mg_hi_made")
        mg_ready_s = sem("mg_ready")
        fin_s = sem("fin")
        fin0_s = sem("fin0")
        rw_link_s = sem("rw_link")

        block = ctx.enter_context(nc.Block())

        @block.sync
        def _(sp):
            sp.dma_start(mem[:], memT).then_inc(mem_in, 16)
            for u in range(2):
                sp.dma_start(stage[:, u, :], w[u]).then_inc(landed[u], 16)
            sp.dma_start(H[:], xT).then_inc(x_in, 16)
            with sp.Fori(1, UNITS // 2) as i:
                for j in range(2):
                    sp.wait_ge(wlo_made, 2 * i + (j - 1))
                    sp.dma_start(stage[:, j, :], w[2 * i + j]).then_inc(landed[j], 16)
            for u in range(UNITS // 2 * 2, UNITS):
                sp.wait_ge(wlo_made, u - 1)
                sp.dma_start(stage[:, u % 2, :], w[u]).then_inc(landed[u % 2], 16)
            with sp.Fori(0, KB) as k:
                sp.wait_ge(fin_s, k + 1)
                sp.dma_start(outT[:, k, :], H[:, k, :]).then_inc(out_sent, 16)
            sp.wait_ge(out_sent, 16 * KB)

        @block.tensor
        def _(pe):
            pe.sem_inc(unit_done, CREDIT)
            pe.sem_inc(mv_turned, CREDIT)

            def product(out, u, slot, hi, lo, ready=None, blocks=8, k0=0, last_k=None, done=True):
                pe.wait_ge(wlo_made, u + 1)
                for k in range(blocks):
                    if ready is not None:
                        pe.wait_ge(*ready(k))
                    wh, wl = w_hi[:, slot, k * P:(k + 1) * P], w_lo[:, slot, k * P:(k + 1) * P]
                    first = k0 + k == 0
                    end = k0 + k == (blocks - 1 if last_k is None else last_k)
                    pe.matmul(out, wl, hi(k), start=first, stop=False)
                    pe.matmul(out, wh, lo(k), start=False, stop=False)
                    mm = pe.matmul(out, wh, hi(k), start=False, stop=end)
                if done:
                    mm.then_inc(unit_done, 1)

            def x_rows(k):
                return x_hi[:, k, :]

            def x_rows_lo(k):
                return x_lo[:, k, :]

            pe.wait_ge(m_split, 1)
            with pe.Fori(0, 2) as i:
                for j in range(4):
                    u = 4 * i + j
                    pe.wait_ge(evac, u + 1)
                    product(ps[:, j % 2, 0:MEM], u, j % 2, lambda k: m_hi[:, k, :], lambda k: m_lo[:, k, :])

            def turn_mem_v(n, b):
                pe.wait_ge(evac, n + (8 + CREDIT + 1))
                pe.wait_ge(mv_taken, n + 1)
                for t in range(MEM // P):
                    mm = pe.transpose(ps[:, 2 + b, t * P:(t + 1) * P], mem_vT[:, b, t * P:(t + 1) * P], ident)
                mm.then_inc(mv_turned, 1)

            with pe.Fori(0, 2) as i:
                for j in range(4):
                    u = 4 * i + (8 + j)
                    pe.wait_ge(evac, u + 1)
                    product(ps[:, j % 2, 0:MEM], u, j % 2, lambda k: m_hi[:, k, :], lambda k: m_lo[:, k, :])
                    turn_mem_v(4 * i + j, j % 2)

            E = EV0["sb"] + CREDIT
            pe.wait_ge(mask_made, 4)
            pe.wait_ge(mv_taken, 8 + CREDIT)
            pe.wait_ge(h_split, 1)

            def pv(g, h, bank=0):
                pe.wait_ge(sb_w, 2 * g + (h + 1))
                for i in range(NS):
                    o, n = REGION[i]
                    mm = pe.matmul(ps[64 * h:64 * h + 64, bank, SEQ - n:SEQ], v_sb[:, i, 64 * h:64 * h + 64],
                                   soft[h][:, o:o + n], start=(i == 0), stop=(i == NS - 1), skip_group_check=True)
                mm.then_inc(sb_pv, 1)

            def pair(g, b, base, first=False):
                u = base
                if not first:
                    pe.wait_ge(sb_v, g)
                product(ps[:, 0, :], u, b, x_rows, x_rows_lo)
                pe.wait_ge(evac, 3 * g + E)
                product(ps[:, 1, :], u + 1, 1 - b, x_rows, x_rows_lo)
                if not first:
                    pe.wait_ge(evac, 3 * g + (E + 1))
                    pv(g - 1, 0)
                pe.wait_ge(evac, 3 * g + (E + 2))
                for h in range(2):
                    if h and not first:
                        pe.wait_ge(sb_w, 2 * g)
                    for i in (0, 1, 3, 2):
                        o, n = REGION[i]
                        pe.matmul(scores(h)[:, o:o + n], k_sb[64 * h:64 * h + 64, i * P:(i + 1) * P],
                                  q_sb[64 * h:64 * h + 64, SEQ - n:SEQ], start=(i != 3), stop=False,
                                  skip_group_check=True)
                        mm = pe.matmul(scores(h)[:, o:o + P], ident_r[:], never[:], start=False, stop=False,
                                       skip_group_check=True)
                    mm.then_inc(sb_scored, 1)
                if not first:
                    pv(g - 1, 1)
                product(ps[:, 1, :], u + 2, b, x_rows, x_rows_lo)
                pe.wait_ge(evac, 3 * g + (E + 3))
                if not first:
                    pe.wait_ge(sb_o, g)
                for i in range(NS):
                    mm = pe.transpose(ps[:, 0, i * P:(i + 1) * P], vT_sb[:, i * P:(i + 1) * P], ident)
                mm.then_inc(sb_vturn, 1)
                for h in range(2):
                    pe.wait_ge(sb_klo, 2 * g + (h + 1))
                    for i in range(NS):
                        o, n = REGION[i]
                        for s in range(i, NS):
                            so, sn = REGION[s]
                            m = suffix if s == i else every
                            for part in (keep_hi, keep_lo):
                                mm = pe.matmul(scores(h)[:, o + n - sn:o + n], m[:], part[h][:, so:so + sn],
                                               start=False, stop=(s == NS - 1 and part is keep_lo),
                                               skip_group_check=True)
                    mm.then_inc(sb_summed, 1)

            pair(0, 0, U0["sb"], first=True)
            pair(1, 1, U0["sb"] + 3)
            with pe.Fori(1, PAIRS // 2) as i:
                pair(2 * i, 0, 6 * i + U0["sb"])
                pair(2 * i + 1, 1, 6 * i + (U0["sb"] + 3))
            pe.wait_ge(sb_v, PAIRS)
            for h in range(2):
                pv(PAIRS - 1, h, 2)

            def sums(n, both=True):
                if both:
                    pe.wait_ge(acc_made, KB + 1 + BEFORE["acc_made"][n])
                    pe.matmul(ps[:, 2, :], C("mean"), acc[:], start=True, stop=True).then_inc(sums_done, 1)
                pe.wait_ge(acc2_made, KB + 1 + BEFORE["acc2_made"][n])
                pe.matmul(ps[:, 3, :], C("mean"), acc2[:], start=True, stop=True).then_inc(sums_done, 1)

            def tiles(n, hi, lo, ready, free=None):
                with pe.Fori(0, 2) as i:
                    for j in range(4):
                        u = 4 * i + (U0[n] + j)
                        b = (U0[n] + j) % 2
                        pe.wait_ge(evac, 4 * i + (EV0[n] + j + CREDIT - 1))
                        product(ps[:, b, :], u, b, hi, lo, ready if j == 0 else None)

            def o_rows(k):
                return o_hi[:, k, :]

            def o_rows_lo(k):
                return o_lo[:, k, :]

            tiles("wo", o_rows, o_rows_lo, lambda k: (sb_o, k + 1))
            sums("wo")

            def xa_scores(h):
                if h >= 1:
                    pe.wait_ge(xa_exp, NS * h)
                pe.wait_ge(evac, EV0["xq"] + CREDIT + 2 * h + 2)
                for t in range(NS):
                    for d in range(2):
                        mm = pe.matmul(ps[:, 2 + t // 2, (t % 2) * MEM:(t % 2 + 1) * MEM],
                                       xq[:, 2 * h + d, t * P:(t + 1) * P], mem_k[:, 2 * h + d, :],
                                       start=(d == 0), stop=(d == 1))
                mm.then_inc(xa_scored, 1)

            def xa_out(h):
                pe.wait_ge(xa_prob, h + 1)
                if h >= 1:
                    pe.wait_ge(xa_pT0, h)
                    pe.wait_ge(xa_pT1, h)
                for m in range(MEM // P):
                    for t in range(NS):
                        mm = pe.transpose(ps[:, 4 + m, t * P:(t + 1) * P], prob[:, h % 2, t, m * P:(m + 1) * P], ident)
                    mm.then_inc(xa_turned, 1)
                pe.wait_ge(xa_pT0, h + 1)
                pe.wait_ge(xa_pT1, h + 1)
                if h >= 1:
                    pe.wait_ge(xa_o, 2 * h)
                for d in range(2):
                    for m in range(MEM // P):
                        mm = pe.matmul(ps[:, 6 + d, :], mem_v[:, m, (2 * h + d) * P:(2 * h + d + 1) * P],
                                       probT[:, h % 2, m, :], start=(m == 0), stop=(m == MEM // P - 1))
                    mm.then_inc(xa_pv, 1)

            pe.wait_ge(mv_taken, 8 + CREDIT)
            for h in range(XA_HEADS):
                for d in range(2):
                    u = U0["xq"] + 2 * h + d
                    pe.wait_ge(evac, EV0["xq"] + 2 * h + d + CREDIT - 1)
                    product(ps[:, u % 2, :], u, u % 2, x_rows, x_rows_lo,
                            (lambda k: (x_ready, k + 1 + BEFORE["x_ready"]["wo"])) if h == d == 0 else None)
                if h:
                    xa_out(h - 1)
                xa_scores(h)
            xa_out(XA_HEADS - 1)
            tiles("xo", o_rows, o_rows_lo, lambda k: (xa_o, k + 1))
            sums("xo")

            with pe.Fori(0, 2 * FFB // 4) as i:
                for j in range(4):
                    u = 4 * i + (U0["up"] + j)
                    b = (U0["up"] + j) % 2
                    pe.wait_ge(evac, 4 * i + (EV0["up"] + j + CREDIT - 1))
                    product(ps[:, b, :], u, b, x_rows, x_rows_lo, (lambda k: (x_ready, k + 1 + BEFORE["x_ready"]["xo"])) if j == 0 else None)
            with pe.Fori(0, 2) as i:
                for j in range(4):
                    pe.wait_ge(evac, 4 * i + (EV0["down"] + j + CREDIT - 1))
                    for c in range(DOWN_UNITS):
                        u = 12 * i + (U0["down"] + 3 * j + c)
                        product(ps[:, j % 2, :], u, (U0["down"] + 3 * j + c) % 2,
                                lambda k: f_hi[:, 8 * c + k, :], lambda k: f_lo[:, 8 * c + k, :],
                                (lambda k: (ff_made, 8 * c + k + 3)) if j == 0 else None,
                                blocks=min(8, FFB - 8 * c), k0=8 * c, last_k=FFB - 1)
            sums("down")

            for k in range(KB):
                pe.wait_ge(sq_made, k + 1 + BEFORE["sq_made"]["pre"])
                pe.matmul(ps[:, 4, :], C("mean"), sq2[:, k % 2, :], start=(k == 0),
                          stop=(k == KB - 1)).then_inc(sums_done, 1)

            def shifted(t0, n):
                with pe.Fori(0, n // 2) as i:
                    for j in range(2):
                        b = U0["rwkv"] + t0 + j
                        pe.wait_ge(evac, 2 * i + (EV0["rwkv"] + t0 + j + CREDIT - 1))
                        product(ps[:, b % 2, :], 2 * i + b, b % 2, x_rows, x_rows_lo)

            u = U0["rwkv"]
            pe.wait_ge(evac, EV0["rwkv"] + CREDIT - 1)
            product(ps[:, u % 2, :], u, u % 2, x_rows, x_rows_lo, lambda k: (x_ready, k + 1 + BEFORE["x_ready"]["pre"]))
            shifted(1, 4)
            pe.wait_ge(small_in_s, 16)
            pe.wait_ge(rw_tanh_s, 1)
            for part in range(2):
                for j in range(CA):
                    if part and j >= 2:
                        pe.wait_ge(rw_sig_s, j - 1)
                    bank = 2 + (4 * part + j) % 6
                    pe.matmul(ps[:, bank, :], w_small[64 * part:64 * part + 64, 0, j * P:(j + 1) * P],
                              lora[64 * part:64 * part + 64, :], start=True, stop=True).then_inc(rw_lora_mm_s, 1)
            shifted(5, 4)
            shifted(9, 4)
            pe.wait_ge(rw_kksq_s, 1)
            pe.wait_ge(rw_sig_s, 8)
            for j in range(CA):
                pe.matmul(ps[:, 4 + j, :], C("heads"), rw_t[:, j, :], start=True, stop=True).then_inc(rw_ss_mm_s, 1)
            shifted(13, 4)
            pe.wait_ge(rw_max_s, 1)
            for j in range(CA):
                pe.wait_ge(rw_barg_s, j + 1)
                pe.matmul(ps[:, 4 + j, :], C("heads"), rw_t[:, j, :], start=True, stop=True).then_inc(rw_bmm_s, 1)
            pe.wait_ge(rw_bonus_s, CA)

            pe.sem_inc(ch_scored_s, 1)
            RB, XB, YB = (3, 4), (5, 6), (7, 0)

            def heads_of(q):
                return range(4 * q, 4 * q + 4)

            def bank_of(b, h):
                return ps[:, b, (h % 4) * P:(h % 4 + 1) * P]

            with pe.Fori(0, NS) as c:
                pe.wait_ge(ch_y_s, c + 1)
                pe.wait_ge(ch_s_s, 2 * c + 2)
                for n in range(3):
                    pe.wait_ge(ch_bkv_s, 3 * c + (n + 1))
                    for j in range(CA):
                        mm = pe.transpose(ps[:, n, j * P:(j + 1) * P], bkv[:, n, j, :], ident)
                    mm.then_inc(ch_turned_s, 1)
                pe.wait_ge(ch_ar_s, 2 * c + 2)
                for h in range(8):
                    r0 = 64 * (h % 2)
                    if h >= 4:
                        pe.wait_ge(ch_m_s, 8 * c + (h - 3))
                    for n in range(2):
                        mm = pe.matmul(ps[:, 3 + h % 4, 256 * n:256 * n + 256], bkv[r0:r0 + 64, n, h // 2, :],
                                       AR[r0:r0 + 64, h // 2, :, :], start=True, stop=True)
                    mm.then_inc(ch_scored_s, 1)
                pe.wait_ge(ch_k_s, c + 1)
                pe.wait_ge(ch_vt_s, c + 1)
                for h in range(8):
                    pe.wait_ge(ch_mask_s, 8 * c + (h + 1))
                    o = ps[:, 1, h * HD_A:(h + 1) * HD_A]
                    pe.matmul(o, AR[:, h // 2, 0, :], Sz[:, h, :], start=True, stop=False)
                    mm = pe.matmul(o, M[:, h, 2, :], tok[:, 2, h // 2, 64 * (h % 2):64 * (h % 2) + 64],
                                   start=False, stop=True)
                mm.then_inc(ch_rh_mm_s, 1)
                pe.wait_ge(ch_m_s, 8 * c + 8)
                pe.wait_ge(ch_b_s, c + 1)
                for q in range(2):
                    pe.wait_ge(ch_y1_s, 2 * c + (q + 1))
                    for h in heads_of(q):
                        mm = pe.transpose(bank_of(XB[q], h), Tt[:, h, :], ident)
                    mm.then_inc(ch_t1_s, 1)

                def level(idx, x_idx, with_x):
                    for q in range(2):
                        pe.wait_ge(ch_mk_s, 2 * idx + (q + 1))
                        pe.wait_ge(ch_x0_s, 2 * c + (q + 1))
                        pe.wait_ge(ch_xn_s, 2 * x_idx + (q + 1))
                        for h in heads_of(q):
                            mm = pe.matmul(bank_of(RB[q], h), Mk[:, h, :], X[:, h, :], start=True, stop=True)
                        mm.then_inc(ch_r_s, 1)
                    for q in range(2):
                        pe.wait_ge(ch_rb_s, 2 * idx + (q + 1))
                        pe.wait_ge(ch_yn_s, 2 * idx + (q + 1))
                        if with_x:
                            for h in heads_of(q):
                                mm = pe.matmul(bank_of(XB[q], h), Tt[:, h, :], R1[:, h, :], start=True, stop=True)
                            mm.then_inc(ch_xmm_s, 1)
                        for h in heads_of(q):
                            mm = pe.matmul(bank_of(YB[q], h), R1[:, h, :], Tt[:, h, :], start=True, stop=True)
                        mm.then_inc(ch_ymm_s, 1)

                NL = len(LEVELS) - 1

                with pe.Fori(0, NL - 1) as lv:
                    level(NL * c + lv, (NL - 1) * c + lv, True)
                level(NL * c + (NL - 1), (NL - 1) * c + (NL - 1), False)
                pe.wait_ge(ch_rh_s, c + 1)
                pe.wait_ge(ch_vt_s, c + 1)
                pe.wait_ge(ch_yn_s, 2 * NL * (c + 1) + 2 * 1)
                for h in range(8):
                    mm = pe.matmul(ps[:, 2, h * HD_A:(h + 1) * HD_A], Tt[:, h, :], rh[:, h * HD_A:(h + 1) * HD_A],
                                   start=True, stop=True)
                mm.then_inc(ch_sa_mm_s, 1)
                pe.wait_ge(ch_sa_s, c + 1)
                for h in range(8):
                    r0 = 64 * (h % 2)
                    v_h = tok[:, 2, h // 2, r0:r0 + 64]
                    sa_h = sa[:, h * HD_A:(h + 1) * HD_A]
                    o = ps[r0:r0 + 64, 4, (h // 2) * HD_A:(h // 2 + 1) * HD_A]
                    pe.matmul(o, tok[:, 0, h // 2, r0:r0 + 64], sa_h, start=True, stop=False)
                    mm = pe.matmul(o, tok[:, 1, h // 2, r0:r0 + 64], v_h, start=False, stop=True)
                mm.then_inc(ch_s_mm_s, 1)
                for h in range(8):
                    r0 = 64 * (h % 2)
                    v_h = tok[:, 2, h // 2, r0:r0 + 64]
                    sa_h = sa[:, h * HD_A:(h + 1) * HD_A]
                    o = ps[r0:r0 + 64, 3, (h // 2) * P:(h // 2 + 1) * P]
                    pe.matmul(o, Sz[:, h, :], AR[:, h // 2, 1, :], start=True, stop=False)
                    pe.matmul(o, sa_h, M[:, h, 1, :], start=False, stop=False)
                    mm = pe.matmul(o, v_h, M[:, h, 3, :], start=False, stop=True)
                mm.then_inc(ch_y_mm_s, 1)

            pe.wait_ge(ch_y_s, NS + 1)
            pe.wait_ge(ch_s_s, 2 * NS + 2)
            pe.wait_ge(gn_sq_s, 1)
            for j in range(CA):
                pe.matmul(ps[:, j, :], C("heads"), rw_r[:, j, :], start=True, stop=True)
            for j in range(CA):
                mm = pe.matmul(ps[:, 4 + j, :], C("heads"), g_sq[:, j, :], start=True, stop=True)
            mm.then_inc(gn_mm_s, 1)
            pe.wait_ge(gn_mu_s, 1)
            with pe.Fori(0, 2) as i:
                for j in range(8):
                    b = U0["conv"] + j
                    pe.wait_ge(evac, 8 * i + (EV0["conv"] + j + CREDIT - 1))
                    product(ps[:, b % 2, :], 8 * i + b, b % 2, x_rows, x_rows_lo)

            def mix(j):
                pe.wait_ge(pl_pooled_s, j + 1)
                if j >= 2:
                    pe.wait_ge(pl_out_s, j - 1)
                pe.matmul(ps[:, 2 + j % 2, :], w_small[:, 1, j * P:(j + 1) * P], pld[:, j % 2, :],
                          start=True, stop=True).then_inc(pl_mm_s, 1)

            pe.wait_ge(gn_v_s, 1)
            for j in range(CA):
                for c in range(2):
                    b = U0["pool"] + 2 * j + c
                    pe.wait_ge(evac, EV0["pool"] + 2 * j + c + CREDIT - 1)
                    product(ps[:, b % 2, :], b, b % 2, x_rows, x_rows_lo)
                if j:
                    mix(j - 1)

            def step(n, m, b, i=0, first=False):
                for d in range(2):
                    pe.wait_ge(evac, 8 * i + (EV0["branch"] + 2 * ((b - U0["branch"]) // 3) + d + CREDIT - 1))
                    product(ps[:, (b + d) % 2, :], 12 * i + (b + d), (b + d) % 2, x_rows, x_rows_lo)
                if first:
                    mix_late()
                st = (b - U0["branch"]) // 3
                pe.wait_ge(br_taken_s, 8 * i + (2 * st + 1))
                pe.wait_ge(br_taken_s, 8 * i + (2 * st + 2))
                pe.wait_ge(wlo_made, 12 * i + (b + 3))
                slot = b % 2
                for d in range(2):
                    for k in range(4):
                        kk = 4 * d + k
                        wh, wl = w_hi[:, slot, kk * P:(kk + 1) * P], w_lo[:, slot, kk * P:(kk + 1) * P]
                        hi, lo = ys_hi[:, CA * n + k, :], ys_lo[:, CA * n + k, :]
                        o = ps[:, 4 + 2 * (m % 2) + d, :]
                        pe.matmul(o, wl, hi, start=(k == 0), stop=False)
                        pe.matmul(o, wh, lo, start=False, stop=False)
                        mm = pe.matmul(o, wh, hi, start=False, stop=(k == 3))
                mm.then_inc(unit_done, 1)

            def mix_late():
                mix(CA - 1)
                pe.wait_ge(pl_lo_s, CA)

            for m in range(4):
                step(0, m, U0["branch"] + 3 * m, first=m == 0)
            with pe.Fori(1, 3) as i:
                for m in range(4):
                    step(i, m, U0["branch"] + 3 * m, i)
            for j in range(KB):
                b = U0["out"] + j
                pe.wait_ge(evac, EV0["out"] + j + CREDIT - 1)
                product(ps[:, b % 2, :], b, b % 2, lambda k: mg_hi[:, k, :], lambda k: mg_lo[:, k, :],
                        (lambda k: (mg_ready_s, k + 1)) if j == 0 else None)
            sums("out", both=False)

        @block.scalar
        def _(act):
            act.dma_start(con[:], const[:, 0:C0["levels"]]).then_inc(params_in, 16)
            act.dma_start(vcol[:], vec).then_inc(params_in, 16)
            act.dma_start(levels[:], const[:, C0["levels"]:C0["scan"]].rearrange("p (l n) -> p l n", n=P)).then_inc(levels_in_s, 16)
            act.dma_start(scan_keep[:], const[:, C0["scan"]:CONST]).then_inc(levels_in_s, 16)
            act.preload_act_table_set("natural_log_exp_and_others")
            act.sem_inc(evac, CREDIT)

            def split_hi(b, i=0, step=0):
                act.wait_ge(landed[b % 2], 8 * step * i + 16 * (b // 2 + 1))
                act.activation(w_hi[:, b % 2, :], stage[:, b % 2, :], ACT.Copy).then_inc(whi_made, 1)

            def take(dst, bank, n, width=SEQ, scale=1.0):
                act.wait_ge(unit_done, n)
                act.activation(dst, ps[:, bank, 0:width], ACT.Copy, scale=scale).then_inc(evac, 1)

            act.wait_ge(mem_in, 16)
            act.activation(m_hi[:], mem[:], ACT.Copy).then_inc(m_hi_made, 1)
            split_hi(0)
            split_hi(1)
            act.wait_ge(params_in, 32)
            act.activation(suffix[:], C("suffix"), ACT.Copy).then_inc(mask_made, 1)
            act.activation(every[:], C("all"), ACT.Copy).then_inc(mask_made, 1)
            act.activation(ident_r[:], ident, ACT.Copy).then_inc(mask_made, 1)
            act.activation(never[:], C("never"), ACT.Copy).then_inc(mask_made, 1)
            act.wait_ge(x_in, 16)
            act.activation(x_hi[:], H[:], ACT.Copy).then_inc(xin_hi, 1)
            with act.Fori(0, 4) as i:
                for j in range(2):
                    take(mem_k[:, 2 * i + j, :], j, 2 * i + (j + CREDIT + 1), MEM)
                    split_hi(2 + j, i, 2)
            with act.Fori(0, 4) as i:
                for j in range(2):
                    act.wait_ge(mv_turned, 2 * i + (j + 1))
                    take(mem_vT[:, j, :], j, 2 * i + (8 + j + CREDIT + 1), MEM)
                    split_hi(10 + j, i, 2)

            def pair(g, i, b, first=False):
                n = 6 * i + (b + CREDIT)
                if not first:
                    act.wait_ge(sb_scored, 2 * g)
                take(q_sb[:], 0, n + 1, scale=float(HD_A) ** -0.5)
                split_hi(b + 2, i, 6)
                take(k_sb[:], 1, n + 2)
                split_hi(b + 3, i, 6)
                for h in range(2):
                    act.wait_ge(sb_scored, 2 * g + (h + 1))
                    if not first:
                        act.wait_ge(sb_pv, 2 * g + (h - 1))
                    act.activation(soft[h][:], scores(h)[:, 0:SCORES], ACT.Abs).then_inc(sb_abs, 1)
                    act.wait_ge(sb_abs, 2 * g + (h + 1))
                    act.activation(soft[h][:], soft[h][:], ACT.Exp, scale=-1.0).then_inc(sb_exp, 1)
                    act.wait_ge(sb_exp, 2 * g + (h + 1))
                    act.activation(soft[h][:], soft[h][:], ACT.Ln, bias=1.0).then_inc(sb_ln, 1)
                if not first:
                    outputs(g - 1)
                    act.wait_ge(sb_vturn, g)
                take(vT_sb[:], 1, n + 3)
                split_hi(b + 4, i, 6)
                for h in range(2):
                    act.wait_ge(sb_summed, 2 * g + (h + 1))
                    act.activation(soft[h][:], scores(h)[:, 0:SCORES], ACT.Exp).then_inc(sb_w, 1)

            def outputs(g, bank=0):
                act.wait_ge(sb_pv, 2 * g + 2)
                act.activation(o_hi[:, g, :], ps[:, bank, :], ACT.Copy).then_inc(sb_ohi, 1)

            pair(0, 0, U0["sb"], first=True)
            pair(1, 0, U0["sb"] + 3)
            with act.Fori(1, PAIRS // 2) as i:
                pair(2 * i, i, U0["sb"])
                pair(2 * i + 1, i, U0["sb"] + 3)
            outputs(PAIRS - 1, 2)

            def tiles(n):
                with act.Fori(0, 4) as i:
                    for j in range(2):
                        act.wait_ge(y_made, 2 * i + (j + 1) + BEFORE["y_made"][n])
                        take(tmp[:, j, :], j, 2 * i + (U0[n] + j + CREDIT + 1))
                        split_hi(U0[n] + j + 2, i, 2)

            def statistics(n, both=True):
                if both:
                    act.wait_ge(sums_done, 1 + BEFORE["sums_done"][n])
                    act.activation(mean[:], ps[:, 2, :], ACT.Copy).then_inc(mean_made, 1)
                act.wait_ge(var_made, 1 + BEFORE["var_made"][n])
                act.activation(rstd[:], rstd[:], ACT.Ln).then_inc(ln_made, 1)
                act.wait_ge(ln_made, 1 + BEFORE["ln_made"][n])
                act.activation(rstd[:], rstd[:], ACT.Exp, scale=-0.5).then_inc(rstd_made, 1)

            def scale_shift(n):
                v = KB * NORMS[n]
                with act.Fori(0, KB) as k:
                    act.wait_ge(normed, k + 1 + BEFORE["normed"][n])
                    g, s = V("ln_g", v + k), V("ln_b", v + k)
                    act.activation(H[:, k, :], Y[:, k, :], ACT.Identity, bias=s, scale=g).then_inc(h_made, 1)
                    if n != "down":
                        act.activation(x_hi[:, k, :], Y[:, k, :], ACT.Identity, bias=s, scale=g).then_inc(xhi_made, 1)

            tiles("wo")
            statistics("wo")
            scale_shift("wo")

            def xa_soft(h):
                act.wait_ge(xa_nmax, h + 1)
                if h >= 2:
                    act.wait_ge(xa_turned, 2 * (h - 1))
                for t in range(NS):
                    act.activation(prob[:, h % 2, t, :], ps[:, 2 + t // 2, (t % 2) * MEM:(t % 2 + 1) * MEM], ACT.Exp,
                                   bias=soft_max[:, h, t:t + 1], scale=float(D // XA_HEADS) ** -0.5,
                                   accum_out=soft_sum[:, h, t:t + 1]).then_inc(xa_exp, 1)

            def xa_take(h):
                act.wait_ge(xa_turned, 2 * h + 1)
                if h >= 2:
                    act.wait_ge(xa_pv, 2 * (h - 1))
                act.activation(probT[:, h % 2, 0, :], ps[:, 4, :], ACT.Copy).then_inc(xa_pT0, 1)
                for d in range(2):
                    act.wait_ge(xa_pv, 2 * h + d + 1)
                    act.activation(o_hi[:, 2 * h + d, :], ps[:, 6 + d, :], ACT.Copy).then_inc(xa_ohi, 1)

            for h in range(XA_HEADS):
                for d in range(2):
                    u = U0["xq"] + 2 * h + d
                    take(xq[:, 2 * h + d, :], u % 2, u + CREDIT + 1)
                    split_hi(u + 2)
                if h:
                    xa_take(h - 1)
                xa_soft(h)
            xa_take(XA_HEADS - 1)
            tiles("xo")
            statistics("xo")
            scale_shift("xo")

            with act.Fori(0, FFB // 2) as i:
                for j in range(4):
                    p = 2 * i + j // 2
                    act.wait_ge(ff_conv, 4 * i + (j + 1))
                    take(raw[:, j, :], j % 2, 4 * i + (U0["up"] + j + CREDIT + 1))
                    split_hi(U0["up"] + j + 2, i, 4)
                    if j % 2 == 0:
                        act.wait_ge(ff_conv, 4 * i + (j + 1 + 4))
                        act.wait_ge(ff_f, p + 1)
                        act.activation(gate_t[:, j // 2, :], conv[:, j, :], ACT.Square).then_inc(ff_sq, 1)
                    else:
                        act.wait_ge(ff_arg, p + 1)
                        act.activation(gate_t[:, j // 2, :], gate_t[:, j // 2, :], ACT.Sigmoid).then_inc(ff_sig, 1)
                        act.wait_ge(ff_f, p + 3)
                        act.activation(f_hi[:, p, :], conv[:, j - 1, :], ACT.Copy).then_inc(ff_hi, 1)
            with act.Fori(0, 4) as i:
                for j in range(2):
                    for c in range(DOWN_UNITS):
                        b = U0["down"] + DOWN_UNITS * j + c
                        if c < DOWN_UNITS - 1:
                            act.wait_ge(unit_done, 6 * i + (b + CREDIT + 1))
                        else:
                            act.wait_ge(y_made, 2 * i + (j + 1) + BEFORE["y_made"]["down"])
                            take(tmp[:, j, :], j, 6 * i + (b + CREDIT + 1))
                        split_hi(b + 2, i, 6)
            act.dma_start(w_small[:], small.rearrange("p (a n) -> p a n", n=SEQ)).then_inc(small_in_s, 16)
            statistics("down")
            scale_shift("down")
            statistics("pre", both=False)
            with act.Fori(0, KB) as k:
                act.wait_ge(normed, k + 1 + BEFORE["normed"]["pre"])
                act.activation(x_hi[:, k, :], Y[:, k, :], ACT.Copy).then_inc(xhi_made, 1)

            u = U0["rwkv"]
            take(tmp[:, u % 2, :], u % 2, u + CREDIT + 1)
            split_hi(u + 2)
            act.wait_ge(rw_shifted_s, 1 + CREDIT)
            act.activation(lora[0:64, :], lora[0:64, :], ACT.Tanh).then_inc(rw_tanh_s, 1)

            def shifted(t0, n):
                with act.Fori(0, n // 2) as i:
                    for j in range(2):
                        b = U0["rwkv"] + t0 + j
                        act.wait_ge(rw_shifted_s, 2 * i + (t0 + j + 1))
                        take(tmp[:, b % 2, :], b % 2, 2 * i + (b + CREDIT + 1))
                        split_hi(b + 2, i, 2)

            shifted(1, 4)
            for part, (dst, bias) in enumerate(((rw_ld, "w0"), (rw_a, "a0"))):
                for j in range(CA):
                    act.wait_ge(rw_lora_mm_s, 4 * part + j + 1)
                    act.activation(dst[:, j, :], ps[:, 2 + (4 * part + j) % 6, :], ACT.Sigmoid,
                                   bias=V(bias, j)).then_inc(rw_sig_s, 1)
            shifted(5, 4)
            shifted(9, 4)
            shifted(13, 2)
            act.wait_ge(rw_max_s, 1)
            act.activation(rw_n[:], rw_n[:], ACT.Sqrt).then_inc(rw_sqrt_s, 1)
            for j in range(2, 4):
                b = U0["rwkv"] + 13 + j
                act.wait_ge(rw_shifted_s, 13 + j + 1)
                take(tmp[:, b % 2, :], b % 2, b + CREDIT + 1)
                split_hi(b + 2)
            act.wait_ge(rw_shifted_s, 17 + CREDIT)
            act.wait_ge(rw_lc_s, 2)
            act.activation(rw_e[:], rw_L[:], ACT.Exp, scale=-1.0).then_inc(rw_e_s, 1)
            act.wait_ge(rw_e_s, 1)
            act.activation(rw_L[:], rw_L[:], ACT.Exp).then_inc(rw_e_s, 1)
            act.activation(rw_ld[:], rw_ld[:], ACT.Exp).then_inc(rw_e_s, 1)
            act.activation(gfac[:], gfac[:], ACT.Exp).then_inc(rw_e_s, 1)

            act.sem_inc(ch_y_s, 1)
            act.wait_ge(rw_prep_s, 1)
            with act.Fori(0, NS) as c:
                act.wait_ge(ch_y_s, c + 1)
                act.activation(AR[:, :, 0, :], rw_kk[:, :, bass.ds(c * CH, CH)], ACT.Copy).then_inc(ch_ar_s, 1)
                act.activation(AR[:, :, 1, :], rw_r[:, :, bass.ds(c * CH, CH)], ACT.Copy).then_inc(ch_ar_s, 1)
                act.wait_ge(ch_turned_s, 3 * c + 1)
                act.activation(tok[:, 0, :, :], ps[:, 0, :].rearrange("p (j n) -> p j n", n=P), ACT.Copy).then_inc(ch_b_s, 1)
                act.wait_ge(ch_turned_s, 3 * c + 2)
                act.activation(tok[:, 1, :, :], ps[:, 1, :].rearrange("p (j n) -> p j n", n=P), ACT.Copy).then_inc(ch_k_s, 1)
                for h in range(8):
                    act.wait_ge(ch_ab_s, 8 * c + (h + 1))
                    act.activation(M[:, h, 1:4, :], ps[:, 3 + h % 4, P:4 * P].rearrange("p (a n) -> p a n", n=P),
                                   ACT.Copy).then_inc(ch_m_s, 1)
                act.wait_ge(ch_rh_mm_s, c + 1)
                act.activation(rh[:], ps[:, 1, :], ACT.Copy).then_inc(ch_rh_s, 1)
                NL = len(LEVELS) - 1
                for q in range(2):
                    act.wait_ge(ch_t1_s, 2 * c + (q + 1))
                    act.activation(X[:, 4 * q:4 * q + 4, :], ps[:, 5 + q, :].rearrange("p (h n) -> p h n", n=P),
                                   ACT.Copy).then_inc(ch_x0_s, 1)

                def level(idx):
                    for q in range(2):
                        act.wait_ge(ch_r_s, 2 * idx + (q + 1))
                        act.activation(R1[:, 4 * q:4 * q + 4, :], ps[:, 3 + q, :].rearrange("p (h n) -> p h n", n=P),
                                       ACT.Copy).then_inc(ch_rb_s, 1)

                with act.Fori(0, NL) as lv:
                    level(NL * c + lv)
                act.wait_ge(ch_sa_mm_s, c + 1)
                act.activation(sa[:], ps[:, 2, :], ACT.Copy).then_inc(ch_sa_s, 1)
                act.wait_ge(ch_y_mm_s, c + 1)
                act.activation(rw_r[:, :, bass.ds((c + 1) * CH - CH, CH)], ps[:, 3, :].rearrange("p (j n) -> p j n", n=P), ACT.Copy).then_inc(ch_y_s, 1)

            act.wait_ge(gn_mm_s, 1)
            act.activation(g_mu[:], ps[:, 0:4, :], ACT.Copy, scale=1.0 / HD_A).then_inc(gn_mu_s, 1)
            act.wait_ge(gn_v2_s, 1)
            act.activation(g_rs[:], g_rs[:], ACT.Ln).then_inc(gn_ln_s, 1)
            act.wait_ge(gn_ln_s, 1)
            act.activation(g_rs[:], g_rs[:], ACT.Exp, scale=-0.5).then_inc(gn_rs_s, 1)
            act.activation(g_sz[:], rw_z, ACT.Sigmoid).then_inc(gn_sig_s, 1)
            act.wait_ge(gn_out_s, 1)
            act.activation(ys_hi[:, 0:CA, :], rw_r, ACT.Copy).then_inc(gn_hi_s, 1)

            with act.Fori(0, 2) as i:
                for j in range(8):
                    p, c = j // 4, j % 4
                    b = U0["conv"] + j
                    if c == 0:
                        act.wait_ge(cv_lo_s, 2 * i + (p + 1))
                    take(cb[:, p, c, :], b % 2, 8 * i + (b + CREDIT + 1))
                    split_hi(b + 2, i, 8)
                    if c == 3:
                        act.wait_ge(evac, 8 * i + (EV0["conv"] + j + CREDIT + 1))
                        act.activation(sg[:, p, :], cb[:, p, 3, :], ACT.Sigmoid).then_inc(cv_sig_s, 1)
                        act.wait_ge(cv_out_s, 2 * i + (p + 1))
                        act.activation(ys_hi[:, CA + 2 * i + p, :], cb[:, p, 2, :], ACT.Copy).then_inc(cv_hi_s, 1)
            act.wait_ge(cv_lo_s, CA + 2)
            act.dma_start(pool_n[:], pool_count).then_inc(pooln_in_s, 16)

            def pool_hi(j):
                act.wait_ge(pl_out_s, j + 1)
                act.activation(ys_hi[:, 2 * CA + j, :], cb[:, j % 2, 2, :], ACT.Copy).then_inc(pl_hi_s, 1)

            for j in range(CA):
                if j >= 2:
                    act.wait_ge(pl_lo_s, j - 1)
                for c in range(2):
                    b = U0["pool"] + 2 * j + c
                    take(cb[:, j % 2, c, :], b % 2, b + CREDIT + 1)
                    split_hi(b + 2)
                act.wait_ge(evac, EV0["pool"] + 2 * j + 2 + CREDIT)
                act.activation(sg[:, j % 2, :], cb[:, j % 2, 1, :], ACT.Sigmoid).then_inc(pl_sig_s, 1)
                if j:
                    pool_hi(j - 1)

            def step(m, b, i=0, first=False):
                st = (b - U0["branch"]) // 3
                for d in range(2):
                    act.wait_ge(br_taken_s, 8 * i + (2 * st + d + 1))
                    act.wait_ge(unit_done, 12 * i + (b + d + CREDIT + 1))
                    act.activation(gates[:, 2 * (m % 2) + d, :], ps[:, (b + d) % 2, :], ACT.Sigmoid).then_inc(evac, 1)
                    split_hi(b + d + 2, i, 12)
                if first:
                    pool_hi(CA - 1)
                act.wait_ge(unit_done, 12 * i + (b + 2 + CREDIT + 1))
                split_hi(b + 4, i, 12)

            for m in range(4):
                step(m, U0["branch"] + 3 * m, first=m == 0)
            with act.Fori(1, 3) as i:
                for m in range(4):
                    step(m, U0["branch"] + 3 * m, i)
            with act.Fori(0, KB) as k:
                act.wait_ge(br_sum_s, k + (2 * KB + 2))
                act.activation(mg_hi[:, k, :], Y[:, k, :], ACT.Copy).then_inc(mg_hi_made_s, 1)
            for j in range(KB):
                b = U0["out"] + j
                take(Y[:, j, :], b % 2, b + CREDIT + 1)
                if b + 2 < UNITS:
                    split_hi(b + 2)
            statistics("out", both=False)

        @block.gpsimd
        def _(pool):
            def split_lo(b, i=0, step=0):
                pool.wait_ge(whi_made, step * i + (b + 1))
                pool.tensor_tensor(w_lo[:, b % 2, :], stage[:, b % 2, :], w_hi[:, b % 2, :].bitcast(F32),
                                   ALU.subtract).then_inc(wlo_made, 1)

            split_lo(0)
            split_lo(1)
            with pool.Fori(0, 8) as i:
                for j in range(2):
                    split_lo(2 + j, i, 2)

            with pool.Fori(0, PAIRS // 2) as i:
                for c in range(6):
                    split_lo(U0["sb"] + 2 + c, i, 6)

            def squares(k, n, src):
                pool.wait_ge(acc2_made, k + 1 + BEFORE["acc2_made"][n])
                pool.tensor_tensor(square[:], src, src, ALU.mult).then_inc(sq_made, 1)
                pool.wait_ge(sq_made, k + 1 + BEFORE["sq_made"][n])
                pool.tensor_tensor(acc2[:], acc2[:], square[:], ALU.add).then_inc(acc2_made, 1)

            def tiles(n, units=1):
                pool.memset(acc2[:], 0.0).then_inc(acc2_made, 1)
                with pool.Fori(0, 4) as i:
                    for j in range(2):
                        for c in range(units):
                            split_lo(U0[n] + 2 + units * j + c, i, 2 * units)
                        pool.wait_ge(y_made, 2 * i + (j + 1 + CREDIT) + BEFORE["y_made"][n])
                        squares(2 * i + j, n, Y[:, 2 * i + j, :])

            def split_x(n):
                with pool.Fori(0, KB) as k:
                    pool.wait_ge(h_made, k + 1 + BEFORE["h_made"][n])
                    pool.wait_ge(xhi_made, k + 1 + BEFORE["xhi_made"][n])
                    pool.tensor_tensor(x_lo[:, k, :], H[:, k, :], x_hi[:, k, :].bitcast(F32),
                                       ALU.subtract).then_inc(x_ready, 1)

            tiles("wo")
            split_x("wo")
            with pool.Fori(0, 4) as i:
                for j in range(2):
                    split_lo(U0["xq"] + 2 + j, i, 2)
            tiles("xo")
            split_x("xo")
            pool.sem_inc(ff_made, 2)
            with pool.Fori(0, FFB // 2) as i:
                for j in range(4):
                    p = 2 * i + j // 2
                    split_lo(U0["up"] + 2 + j, i, 4)
                    if j % 2:
                        pool.wait_ge(ff_conv, 4 * i + (j + 1 + 4))
                        pool.tensor_tensor(conv[:, j, :], conv[:, j, :], conv[:, j - 1, :], ALU.mult).then_inc(ff_vg, 1)
                        pool.wait_ge(ff_hi, p + 1)
                        pool.tensor_tensor(f_lo[:, p, :], conv[:, j - 1, :], f_hi[:, p, :].bitcast(F32),
                                           ALU.subtract).then_inc(ff_made, 1)
            tiles("down", DOWN_UNITS)
            for k in range(KB):
                pool.wait_ge(h_made, k + 1 + BEFORE["h_made"]["down"])
                if k >= 2:
                    pool.wait_ge(sums_done, k - 1 + BEFORE["sums_done"]["pre"])
                pool.tensor_tensor(sq2[:, k % 2, :], H[:, k, :], H[:, k, :], ALU.mult).then_inc(sq_made, 1)
            with pool.Fori(0, KB) as k:
                pool.wait_ge(xhi_made, k + 1 + BEFORE["xhi_made"]["pre"])
                pool.tensor_tensor(x_lo[:, k, :], Y[:, k, :], x_hi[:, k, :].bitcast(F32),
                                   ALU.subtract).then_inc(x_ready, 1)
            split_lo(U0["rwkv"] + 2)
            with pool.Fori(0, 8) as i:
                for j in range(2):
                    split_lo(U0["rwkv"] + 3 + j, i, 2)
            pool.wait_ge(rw_prep_s, 1)
            pool.memset(Sz[:], 0.0).then_inc(ch_s_s, 1)
            pool.sem_inc(ch_s_s, 1)
            pool.memset(scr[:], 0.0).then_inc(ch_wait_s, 1)
            pool.wait_ge(ch_wait_s, 1)
            with pool.Fori(0, NS) as c:
                at_c = bass.ds(c * CH, CH)
                pool.wait_ge(ch_scored_s, 8 * c + 1)
                pool.tensor_tensor(scr[:, 9:10], scr[:, 0:1], scr[:, 0:1], ALU.mult)
                pool.tensor_copy(bkv[:, 0, :, :], rw_a[:, :, at_c]).then_inc(ch_bkv_s, 1)
                pool.tensor_copy(bkv[:, 1, :, :], rw_k[:, :, at_c]).then_inc(ch_bkv_s, 1)
                pool.tensor_copy(bkv[:, 2, :, :], rw_v[:, :, at_c]).then_inc(ch_bkv_s, 1)
                for h in range(8):
                    pool.wait_ge(ch_m_s, 8 * c + (h + 1))
                    pool.tensor_tensor(scr[:, h + 1:h + 2], scr[:, 0:1], scr[:, 0:1], ALU.mult)
                    pool.affine_select(M[:, h, 1, :], M[:, h, 1, :], pattern=[[1, P]], compare_op=ALU.is_ge,
                                       fill=0.0, base=0, channel_multiplier=-1)
                    pool.affine_select(M[:, h, 2:4, :], M[:, h, 2:4, :], pattern=[[1, 2], [1, P]], compare_op=ALU.is_gt,
                                       fill=0.0, base=0, channel_multiplier=-1).then_inc(ch_mask_s, 1)
            pool.wait_ge(gn_hi_s, 1)
            pool.tensor_tensor(ys_lo[:, 0:CA, :], rw_r, ys_hi[:, 0:CA, :].bitcast(F32), ALU.subtract).then_inc(gn_lo_s, 1)
            pool.sem_inc(cv_lo_s, 2)
            with pool.Fori(0, 2) as i:
                for j in range(8):
                    split_lo(U0["conv"] + 2 + j, i, 8)
                    if j % 4 == 3:
                        p = j // 4
                        pool.wait_ge(cv_hi_s, 2 * i + (p + 1))
                        pool.tensor_tensor(scr[:, 10 + p:11 + p], scr[:, 0:1], scr[:, 0:1], ALU.mult)
                        pool.tensor_tensor(ys_lo[:, CA + 2 * i + p, :], cb[:, p, 2, :], ys_hi[:, CA + 2 * i + p, :].bitcast(F32),
                                           ALU.subtract).then_inc(cv_lo_s, 1)

            def pool_lo(j):
                pool.wait_ge(pl_hi_s, j + 1)
                pool.tensor_tensor(ys_lo[:, 2 * CA + j, :], cb[:, j % 2, 2, :], ys_hi[:, 2 * CA + j, :].bitcast(F32),
                                   ALU.subtract).then_inc(pl_lo_s, 1)

            for j in range(CA):
                for c in range(2):
                    split_lo(U0["pool"] + 2 * j + c + 2)
                if j:
                    pool_lo(j - 1)
            for c in range(12):
                split_lo(U0["branch"] + 2 + c)
                if c == 1:
                    pool_lo(CA - 1)
            with pool.Fori(1, 3) as i:
                for c in range(12):
                    split_lo(U0["branch"] + 2 + c, i, 12)
            for k in range(KB):
                pool.wait_ge(mg_hi_made_s, k + 1)
                pool.tensor_tensor(mg_lo[:, k, :], Y[:, k, :], mg_hi[:, k, :].bitcast(F32),
                                   ALU.subtract).then_inc(mg_ready_s, 1)
            pool.wait_ge(mg_ready_s, KB)
            pool.memset(acc2[:], 0.0).then_inc(acc2_made, 1)
            for j in range(KB):
                if U0["out"] + j + 2 < UNITS:
                    split_lo(U0["out"] + j + 2)
                pool.wait_ge(evac, EV0["out"] + j + 1 + CREDIT)
                squares(j, "out", Y[:, j, :])

        @block.vector
        def _(dve):
            dve.sem_inc(mv_taken, CREDIT)
            dve.wait_ge(m_hi_made, 1)
            dve.tensor_tensor(m_lo[:], mem[:], m_hi[:].bitcast(F32), ALU.subtract).then_inc(m_split, 1)
            dve.wait_ge(xin_hi, 1)
            dve.tensor_tensor(x_lo[:], H[:], x_hi[:].bitcast(F32), ALU.subtract).then_inc(h_split, 1)
            with dve.Fori(0, 4) as i:
                for j in range(2):
                    dve.wait_ge(mv_turned, 2 * i + (j + 1 + CREDIT))
                    dve.tensor_copy(mem_v[:, :, bass.ds((2 * i + j) * P, P)],
                                    ps[:, 2 + j, 0:MEM].rearrange("p (t n) -> p t n", t=2)).then_inc(mv_taken, 1)

            def pair(g, first=False):
                for h in range(2):
                    dve.wait_ge(sb_ln, 2 * g + (h + 1))
                    dve.scalar_tensor_tensor(out=keep[h][:], in0=scores(h)[:, 0:SCORES], scalar=0.0, in1=soft[h][:],
                                             op0=ALU.max, op1=ALU.add).then_inc(sb_keep, 1)
                    dve.wait_ge(sb_keep, 2 * g + (h + 1))
                    dve.tensor_copy(keep_hi[h][:], keep[h][:]).then_inc(sb_khi, 1)
                    dve.wait_ge(sb_khi, 2 * g + (h + 1))
                    dve.tensor_tensor(keep_lo[h][:], keep[h][:], keep_hi[h][:].bitcast(F32),
                                      ALU.subtract).then_inc(sb_klo, 1)
                    if h == 0 and not first:
                        outputs(g - 1)
                dve.wait_ge(sb_vturn, g + 1)
                dve.tensor_copy(v_sb[:], ps[:, 0, :].rearrange("p (t n) -> p t n", t=NS)).then_inc(sb_v, 1)

            def outputs(g, bank=0):
                dve.wait_ge(sb_ohi, g + 1)
                dve.tensor_tensor(o_lo[:, g, :], ps[:, bank, :], o_hi[:, g, :].bitcast(F32), ALU.subtract).then_inc(sb_o, 1)

            pair(0, first=True)
            pair(1)
            with dve.Fori(1, PAIRS // 2) as i:
                pair(2 * i)
                pair(2 * i + 1)
            outputs(PAIRS - 1, 2)

            def tiles(n):
                dve.sem_inc(y_made, CREDIT)
                dve.memset(acc[:], 0.0).then_inc(acc_made, 1)
                with dve.Fori(0, KB // 2) as i:
                    for j in range(2):
                        k = 2 * i + j
                        dve.wait_ge(evac, 2 * i + (EV0[n] + j + CREDIT + 1))
                        dve.scalar_tensor_tensor(out=Y[:, k, :], in0=H[:, k, :], scalar=ALPHA, in1=tmp[:, j, :],
                                                 op0=ALU.mult, op1=ALU.add).then_inc(y_made, 1)
                        dve.wait_ge(y_made, 2 * i + (j + 1 + CREDIT) + BEFORE["y_made"][n])
                        dve.wait_ge(acc_made, 2 * i + (j + 1) + BEFORE["acc_made"][n])
                        dve.tensor_tensor(acc[:], acc[:], Y[:, k, :], ALU.add).then_inc(acc_made, 1)

            def statistics(n, eps):
                dve.wait_ge(mean_made, 1 + BEFORE["mean_made"][n])
                dve.tensor_tensor(rstd[:], mean[:], mean[:], ALU.mult).then_inc(var_made0, 1)
                dve.wait_ge(var_made0, 1 + BEFORE["var_made0"][n])
                dve.wait_ge(sums_done, 2 + BEFORE["sums_done"][n])
                dve.tensor_tensor(rstd[:], ps[:, 3, :], rstd[:], ALU.subtract).then_inc(var_made0, 1)
                dve.wait_ge(var_made0, 2 + BEFORE["var_made0"][n])
                dve.tensor_scalar(rstd[:], rstd[:], 0.0, eps, ALU.max, ALU.add).then_inc(var_made, 1)

            def norm(n):
                dve.wait_ge(acc2_made, KB + 1 + BEFORE["acc2_made"][n])
                with dve.Fori(0, KB) as k:
                    dve.tensor_tensor(Y[:, k, :], Y[:, k, :], mean[:], ALU.subtract).then_inc(centred, 1)
                    dve.wait_ge(rstd_made, 1 + BEFORE["rstd_made"][n])
                    dve.wait_ge(centred, k + 1 + BEFORE["centred"][n])
                    dve.tensor_tensor(Y[:, k, :], Y[:, k, :], rstd[:], ALU.mult).then_inc(normed, 1)

            tiles("wo")
            statistics("wo", LN_EPS)
            norm("wo")

            def xa_soft(h):
                dve.wait_ge(xa_scored, h + 1)
                for b in range(2):
                    dve.tensor_reduce(soft_max[:, h, 2 * b:2 * b + 2],
                                      ps[:, 2 + b, :].rearrange("p (t n) -> p t n", t=2), mybir.AxisListType.X,
                                      ALU.max).then_inc(xa_max, 1)
                dve.wait_ge(xa_max, 2 * h + 2)
                dve.tensor_scalar(soft_max[:, h, :], soft_max[:, h, :], -float(D // XA_HEADS) ** -0.5, None,
                                  ALU.mult).then_inc(xa_nmax, 1)
                dve.wait_ge(xa_exp, NS * (h + 1))
                dve.reciprocal(soft_sum[:, h, :], soft_sum[:, h, :]).then_inc(xa_rec, 1)
                dve.wait_ge(xa_rec, h + 1)
                dve.tensor_tensor(prob[:, h % 2, :, :], prob[:, h % 2, :, :],
                                  soft_sum[:, h, :].unsqueeze(2).to_broadcast([P, NS, MEM]), ALU.mult).then_inc(xa_prob, 1)

            def xa_take(h):
                dve.wait_ge(xa_turned, 2 * h + 2)
                if h >= 2:
                    dve.wait_ge(xa_pv, 2 * (h - 1))
                dve.tensor_copy(probT[:, h % 2, 1, :], ps[:, 5, :]).then_inc(xa_pT1, 1)
                for d in range(2):
                    dve.wait_ge(xa_ohi, 2 * h + d + 1)
                    dve.tensor_tensor(o_lo[:, 2 * h + d, :], ps[:, 6 + d, :], o_hi[:, 2 * h + d, :].bitcast(F32),
                                      ALU.subtract).then_inc(xa_o, 1)

            for h in range(XA_HEADS):
                if h:
                    xa_take(h - 1)
                xa_soft(h)
            xa_take(XA_HEADS - 1)
            tiles("xo")
            statistics("xo", LN_EPS)
            norm("xo")

            C_GELU = 2.0 * float(np.sqrt(2.0 / np.pi))
            dve.sem_inc(ff_conv, 4)
            dve.sem_inc(ff_f, 2)
            with dve.Fori(0, FFB // 2) as i:
                for j in range(4):
                    p = 2 * i + j // 2
                    tap = lambda c: V("ffn_conv", (2 * c + j % 2) * FFB + p)
                    dve.wait_ge(evac, 4 * i + (EV0["up"] + j + CREDIT + 1))
                    dve.wait_ge(ff_made, p + 1)
                    dve.tensor_scalar(conv[:, j, :], raw[:, j, :], tap(2), V("ffn_conv_b", (j % 2) * FFB + p),
                                      ALU.mult, ALU.add).then_inc(ff_tap, 1)
                    dve.wait_ge(ff_tap, 8 * i + (2 * j + 1))
                    dve.scalar_tensor_tensor(out=conv[:, j, 1:SEQ], in0=raw[:, j, 0:SEQ - 1], scalar=tap(1),
                                             in1=conv[:, j, 1:SEQ], op0=ALU.mult, op1=ALU.add).then_inc(ff_tap, 1)
                    dve.wait_ge(ff_tap, 8 * i + (2 * j + 2))
                    dve.scalar_tensor_tensor(out=conv[:, j, 2:SEQ], in0=raw[:, j, 0:SEQ - 2], scalar=tap(0),
                                             in1=conv[:, j, 2:SEQ], op0=ALU.mult, op1=ALU.add).then_inc(ff_conv, 1)
                    if j % 2:
                        gt = gate_t[:, j // 2, :]
                        dve.wait_ge(ff_sq, p + 1)
                        dve.tensor_scalar(gt, gt, 0.044715 * C_GELU, C_GELU, ALU.mult, ALU.add).then_inc(ff_poly, 1)
                        dve.wait_ge(ff_poly, p + 1)
                        dve.tensor_tensor(gt, gt, conv[:, j - 1, :], ALU.mult).then_inc(ff_arg, 1)
                        dve.wait_ge(ff_sig, p + 1)
                        dve.wait_ge(ff_vg, p + 1)
                        dve.tensor_tensor(conv[:, j - 1, :], conv[:, j, :], gt, ALU.mult).then_inc(ff_f, 1)
            tiles("down")
            statistics("down", LN_EPS)
            norm("down")
            chain = [0]

            def link(ins):
                chain[0] += 1
                ins.then_inc(rw_link_s, 1)
                dve.wait_ge(rw_link_s, chain[0])

            dve.wait_ge(sums_done, KB + BEFORE["sums_done"]["pre"])
            dve.tensor_scalar(rstd[:], ps[:, 4, :], RMS_EPS, None, ALU.add).then_inc(var_made, 1)
            dve.wait_ge(rstd_made, 1 + BEFORE["rstd_made"]["pre"])
            with dve.Fori(0, KB) as k:
                dve.scalar_tensor_tensor(out=Y[:, k, :], in0=H[:, k, :], scalar=V("pre", k), in1=rstd[:],
                                         op0=ALU.mult, op1=ALU.mult).then_inc(normed, 1)

            link(dve.tensor_scalar(omm[:], vcol[:, V0["mu"]:V0["mu"] + 17], -1.0, 1.0, ALU.mult, ALU.add))
            dve.sem_inc(rw_shifted_s, CREDIT)

            def shift(dst, t, m, n):
                dve.wait_ge(evac, t + (EV0["rwkv"] + CREDIT + 1))
                dve.tensor_scalar(dst, tmp[:, n, :], omm[:, bass.ds(m, 1)], None, ALU.mult).then_inc(rw_shift0_s, 1)
                dve.wait_ge(rw_shift0_s, t + 1)
                dve.scalar_tensor_tensor(out=dst[:, 1:SEQ], in0=tmp[:, n, 0:SEQ - 1], scalar=V("mu", m), in1=dst[:, 1:SEQ],
                                         op0=ALU.mult, op1=ALU.add).then_inc(rw_shifted_s, 1)

            def shifts(buf, first, t0, n):
                with dve.Fori(0, n // 2) as i:
                    for j in range(2):
                        shift(buf[:, 2 * i + (first + j), :], 2 * i + (t0 + j), 2 * i + (t0 + j - 1),
                              (U0["rwkv"] + t0 + j) % 2)

            shift(lora[:], 0, 16, U0["rwkv"] % 2)
            shifts(rw_rk, 0, 1, 4)
            dve.wait_ge(rw_sig_s, 4)
            link(dve.tensor_scalar(rw_ld[:], rw_ld[:], DECAY, None, ALU.mult))
            dve.wait_ge(levels_in_s, 32)
            for j in range(CA):
                dve.tensor_tensor_scan(rw_L[:, j, :], scan_keep[:], rw_ld[:, j, :], 0.0, ALU.mult, ALU.add).then_inc(rw_scan_s, 1)
            shifts(rw_rk, 4, 5, 4)
            dve.wait_ge(rw_shifted_s, 9 + CREDIT)
            for j in range(CA):
                link(dve.tensor_scalar(rw_kk[:, j, :], rw_k[:, j, :], V("k_k", j), None, ALU.mult))
            dve.tensor_tensor(rw_t[:], rw_kk[:], rw_kk[:], ALU.mult).then_inc(rw_kksq_s, 1)
            shifts(rw_vz, 0, 9, 4)
            dve.wait_ge(rw_scan_s, CA)
            L = rw_L[:].rearrange("p j (c n) -> p j c n", n=CH)
            link(dve.tensor_scalar(cen[:], L[:, :, :, CH - 1], 0.5, None, ALU.mult))
            Lf = rw_L[:].rearrange("p j (c n) -> p (j c) n", n=CH)
            dve.tensor_tensor(Lf, Lf, cen[:].rearrange("p j c -> p (j c)").unsqueeze(2).to_broadcast([P, CA * NS, CH]),
                              ALU.subtract).then_inc(rw_lc_s, 1)
            dve.wait_ge(rw_lc_s, 1)
            link(dve.tensor_tensor(gfac[:, :, 0:NS - 1], cen[:, :, 0:NS - 1], cen[:, :, 1:NS], ALU.add))
            link(dve.tensor_copy(gfac[:, :, NS - 1:NS], cen[:, :, NS - 1:NS]))
            dve.tensor_tensor(rw_ld[:], rw_L[:], rw_ld[:], ALU.subtract).then_inc(rw_lc_s, 1)
            dve.wait_ge(rw_ss_mm_s, CA)
            dve.tensor_scalar(rw_n[:], ps[:, 4:8, :], 1e-24, None, ALU.max).then_inc(rw_max_s, 1)
            shifts(rw_vz, 4, 13, 2)
            dve.wait_ge(rw_sig_s, 8)
            for j in range(CA):
                link(dve.tensor_scalar(rw_t[:, j, :], rw_a[:, j, :], V("k_a", j), V("k_a", j), ALU.mult, ALU.subtract))
                link(dve.scalar_tensor_tensor(out=rw_k[:, j, :], in0=rw_t[:, j, :], scalar=1.0, in1=rw_k[:, j, :],
                                              op0=ALU.add, op1=ALU.mult))
            shifts(rw_vz, 6, 15, 2)
            dve.wait_ge(rw_shifted_s, 17 + CREDIT)
            for j in range(CA):
                link(dve.tensor_scalar(rw_t[:, j, :], rw_r[:, j, :], V("r_k", j), None, ALU.mult))
                dve.tensor_tensor(rw_t[:, j, :], rw_t[:, j, :], rw_k[:, j, :], ALU.mult).then_inc(rw_barg_s, 1)
            dve.wait_ge(rw_barg_s, CA)
            dve.wait_ge(rw_sqrt_s, 1)
            link(dve.reciprocal(rw_n[:], rw_n[:]))
            link(dve.tensor_tensor(rw_kk[:], rw_kk[:], rw_n[:], ALU.mult))
            link(dve.tensor_tensor(rw_a[:], rw_a[:], rw_kk[:], ALU.mult))
            dve.wait_ge(rw_e_s, 4)
            link(dve.tensor_tensor(rw_a[:], rw_a[:], rw_e[:], ALU.mult))
            link(dve.tensor_tensor(rw_k, rw_k, rw_e[:], ALU.mult))
            link(dve.tensor_tensor(rw_r, rw_r, rw_L[:], ALU.mult))
            link(dve.scalar_tensor_tensor(out=rw_kk[:], in0=rw_kk[:], scalar=-1.0, in1=rw_ld[:], op0=ALU.mult, op1=ALU.mult))
            dve.wait_ge(rw_bmm_s, CA)
            for j in range(CA):
                dve.tensor_tensor(rw_L[:, j, :], ps[:, 4 + j, :], rw_v[:, j, :], ALU.mult).then_inc(rw_bonus_s, 1)
            dve.wait_ge(rw_bonus_s, CA)
            dve.tensor_copy(omm[:, 0:1], omm[:, 1:2]).then_inc(rw_prep_s, 1)

            dve.sem_inc(ch_xn_s, 2)
            dve.sem_inc(ch_yn_s, 2)
            NL = len(LEVELS) - 1
            strict = C("strict")
            by_head = lambda m: m.unsqueeze(1).to_broadcast([P, 4, P])
            with dve.Fori(0, NS) as c:
                dve.wait_ge(ch_turned_s, 3 * c + 3)
                dve.tensor_copy(tok[:, 2, :, :], ps[:, 2, :].rearrange("p (j n) -> p j n", n=P)).then_inc(ch_vt_s, 1)
                for h in range(8):
                    dve.wait_ge(ch_scored_s, 8 * c + (h + 2))
                    dve.tensor_tensor(M[:, h, 0, :], ps[:, 3 + h % 4, 0:P], strict, ALU.mult).then_inc(ch_ab_s, 1)
                for q in range(2):
                    hs = slice(4 * q, 4 * q + 4)
                    dve.wait_ge(ch_ab_s, 8 * c + 4 * q + 4)
                    dve.tensor_tensor(Tt[:, hs, :], M[:, hs, 0, :], by_head(levels[:, 0, :]), ALU.mult).then_inc(ch_tt0_s, 1)
                    dve.wait_ge(ch_tt0_s, 2 * c + (q + 1))
                    dve.tensor_tensor(Tt[:, hs, :], Tt[:, hs, :], by_head(ident), ALU.add).then_inc(ch_y1_s, 1)

                def masks(idx, lv):
                    for q in range(2):
                        hs = slice(4 * q, 4 * q + 4)
                        dve.tensor_tensor(Mk[:, hs, :], M[:, hs, 0, :], by_head(levels[:, lv, :]), ALU.mult).then_inc(ch_mk_s, 1)

                def update(idx, x_idx, with_x):
                    for q in range(2):
                        hs = slice(4 * q, 4 * q + 4)
                        view = lambda b: ps[:, b, :].rearrange("p (h n) -> p h n", n=P)
                        if with_x:
                            dve.wait_ge(ch_xmm_s, 2 * x_idx + (q + 1))
                            dve.tensor_tensor(X[:, hs, :], X[:, hs, :], view(5 + q), ALU.add).then_inc(ch_xn_s, 1)
                        dve.wait_ge(ch_ymm_s, 2 * idx + (q + 1))
                        dve.tensor_tensor(Tt[:, hs, :], Tt[:, hs, :], view((7, 0)[q]), ALU.add).then_inc(ch_yn_s, 1)

                with dve.Fori(0, NL - 1) as lv:
                    idx = NL * c + lv
                    masks(idx, lv + 1)
                    update(idx, (NL - 1) * c + lv, True)
                masks(NL * c + (NL - 1), NL)
                update(NL * c + (NL - 1), None, False)
                dve.wait_ge(ch_s_mm_s, c + 1)
                for r in range(2):
                    rows = slice(64 * r, 64 * r + 64)
                    S = Sz[rows, r::2, :]
                    dve.wait_ge(ch_y_mm_s, c + 1)
                    dve.tensor_tensor(S, S, ps[rows, 4, 0:CA * HD_A].rearrange("p (j n) -> p j n", n=HD_A),
                                      ALU.add).then_inc(ch_s0_s, 1)
                    dve.wait_ge(ch_s0_s, 2 * c + (r + 1))
                    dve.tensor_tensor(S, S, gfac[rows, :, bass.ds(c, 1)].to_broadcast([64, CA, HD_A]),
                                      ALU.mult).then_inc(ch_s_s, 1)

            dve.wait_ge(ch_y_s, NS + 1)
            dve.tensor_tensor(g_sq[:], rw_r, rw_r, ALU.mult).then_inc(gn_sq_s, 1)
            dve.wait_ge(gn_mu_s, 1)
            dve.wait_ge(gn_sq_s, 1)
            link(dve.tensor_tensor(rw_r, rw_r, g_mu[:], ALU.subtract))
            link(dve.tensor_tensor(g_mu[:], g_mu[:], g_mu[:], ALU.mult))
            dve.scalar_tensor_tensor(out=g_rs[:], in0=ps[:, 4:8, :], scalar=1.0 / HD_A, in1=g_mu[:], op0=ALU.mult,
                                     op1=ALU.subtract).then_inc(gn_v_s, 1)
            dve.wait_ge(gn_v_s, 1)
            dve.tensor_scalar(g_rs[:], g_rs[:], 0.0, GN_EPS, ALU.max, ALU.add).then_inc(gn_v2_s, 1)
            dve.wait_ge(gn_rs_s, 1)
            link(dve.tensor_tensor(rw_r, rw_r, g_rs[:], ALU.mult))
            for j in range(CA):
                link(dve.tensor_scalar(rw_r[:, j, :], rw_r[:, j, :], V("gn_w", j), V("gn_b", j), ALU.mult, ALU.add))
            link(dve.tensor_tensor(rw_r, rw_r, rw_L[:], ALU.add))
            dve.wait_ge(gn_sig_s, 1)
            link(dve.tensor_tensor(rw_r, rw_r, rw_z, ALU.mult))
            dve.tensor_tensor(rw_r, rw_r, g_sz[:], ALU.mult).then_inc(gn_out_s, 1)

            with dve.Fori(0, 2) as i:
                for p in range(2):
                    B, Cc, Uu, Z = (cb[:, p, n, :] for n in range(4))
                    at_0 = 14 * i + 7 * p
                    n_link = [0]

                    def step(ins):
                        n_link[0] += 1
                        ins.then_inc(cv_link_s, 1)
                        dve.wait_ge(cv_link_s, 12 * i + (6 * p + n_link[0]))

                    tap = lambda n: V("conv_w", 2 * i + (n * CA + p))
                    dve.wait_ge(evac, 8 * i + (EV0["conv"] + 4 * p + 3 + CREDIT))
                    step(dve.tensor_tensor(Cc, Cc, Uu, ALU.mult))
                    step(dve.tensor_scalar(Uu, Cc, tap(2), None, ALU.mult))
                    step(dve.scalar_tensor_tensor(out=Uu[:, 1:SEQ], in0=Cc[:, 0:SEQ - 1], scalar=tap(1), in1=Uu[:, 1:SEQ],
                                                  op0=ALU.mult, op1=ALU.add))
                    step(dve.scalar_tensor_tensor(out=Uu[:, 2:SEQ], in0=Cc[:, 0:SEQ - 2], scalar=tap(0), in1=Uu[:, 2:SEQ],
                                                  op0=ALU.mult, op1=ALU.add))
                    step(dve.tensor_tensor(Uu, Uu, B, ALU.mult))
                    dve.wait_ge(evac, 8 * i + (EV0["conv"] + 4 * p + 4 + CREDIT))
                    dve.wait_ge(cv_sig_s, 2 * i + (p + 1))
                    step(dve.tensor_tensor(Uu, Uu, Z, ALU.mult))
                    dve.tensor_tensor(Uu, Uu, sg[:, p, :], ALU.mult).then_inc(cv_out_s, 1)

            dve.sem_inc(br_taken_s, 4)

            def pool_out(j):
                B = cb[:, j % 2, :, :]
                dve.wait_ge(pl_mm_s, j + 1)
                dve.wait_ge(pl_sig_s, j + 1)
                link(dve.scalar_tensor_tensor(out=B[:, 2, :], in0=ps[:, 2 + j % 2, :], scalar=V("pool_scale", j),
                                              in1=B[:, 1, :], op0=ALU.mult, op1=ALU.mult))
                dve.tensor_tensor(B[:, 2, :], B[:, 2, :], sg[:, j % 2, :], ALU.mult).then_inc(pl_out_s, 1)

            dve.wait_ge(pooln_in_s, 16)
            for j in range(CA):
                src = cb[:, j % 2, 0, :]
                dve.wait_ge(evac, EV0["pool"] + 2 * j + 1 + CREDIT)
                if j >= 2:
                    dve.wait_ge(pl_mm_s, j - 1)
                width, cur, n = 1, src, 0
                while width < POOL_WINDOWS[j]:
                    nxt = pt[:, n % 2, :]
                    link(dve.tensor_copy(nxt[:, 0:width], cur[:, 0:width]))
                    link(dve.tensor_tensor(nxt[:, width:SEQ], cur[:, width:SEQ], cur[:, 0:SEQ - width], ALU.add))
                    cur, width, n = nxt, 2 * width, n + 1
                link(dve.tensor_tensor(pld[:, j % 2, :], cur, pool_n[:, j, :], ALU.mult))
                dve.tensor_tensor(pld[:, j % 2, :], pld[:, j % 2, :], src, ALU.subtract).then_inc(pl_pooled_s, 1)
                if j:
                    pool_out(j - 1)
            pool_out(CA - 1)

            dve.wait_ge(pl_lo_s, CA)
            dve.memset(Y[:], 0.0).then_inc(br_sum_s, 1)

            def step(m, b, i=0, first=False):
                st = (b - U0["branch"]) // 3
                dve.wait_ge(unit_done, 12 * i + (b + 2 + CREDIT + 1))
                for d in range(2):
                    g = 2 * (m % 2) + d
                    dve.wait_ge(evac, 8 * i + (EV0["branch"] + 2 * st + d + 1 + CREDIT))
                    dve.tensor_tensor(bt[:, g, :], gates[:, g, :], ps[:, 4 + g, :], ALU.mult).then_inc(br_taken_s, 1)
                    dve.wait_ge(br_taken_s, 8 * i + (2 * st + d + 1 + 4))
                    dve.wait_ge(br_sum_s, 8 * i + (2 * st + d + 1))
                    dve.tensor_tensor(Y[:, 2 * m + d, :], Y[:, 2 * m + d, :], bt[:, g, :], ALU.add).then_inc(br_sum_s, 1)

            for m in range(4):
                step(m, U0["branch"] + 3 * m, first=m == 0)
            with dve.Fori(1, 3) as i:
                for m in range(4):
                    step(m, U0["branch"] + 3 * m, i)

            dve.wait_ge(sums_done, 1 + BEFORE["sums_done"]["out"])
            dve.tensor_scalar(rstd[:], ps[:, 3, :], RMS_EPS, None, ALU.add).then_inc(var_made, 1)
            dve.wait_ge(rstd_made, 1 + BEFORE["rstd_made"]["out"])
            with dve.Fori(0, KB) as k:
                dve.scalar_tensor_tensor(out=Y[:, k, :], in0=Y[:, k, :], scalar=V("post", k), in1=rstd[:],
                                         op0=ALU.mult, op1=ALU.mult).then_inc(fin0_s, 1)
                dve.wait_ge(fin0_s, k + 1)
                dve.tensor_tensor(H[:, k, :], H[:, k, :], Y[:, k, :], ALU.add).then_inc(fin_s, 1)


_INS = ["w", "xT", "memT", "vec", "const", "small", "pool_count"]


def lay_out(i):
    def in_tiles(a):
        k, n = a.shape
        return a.reshape(k // P, P, n // P, P).transpose(2, 1, 0, 3).reshape(n // P, P, k)

    f = lambda a: np.asarray(a)
    sb = in_tiles(f(i["sb_win"])[0])
    sb = np.stack([sb[0:8], sb[8:16], sb[16:24]], 1).reshape(24, P, UNIT)
    up = in_tiles(f(i["ffn_up"])[0])
    up = np.stack([up[:FFB], up[FFB:]], 1).reshape(2 * FFB, P, UNIT)
    down = in_tiles(f(i["ffn_down"])[0])
    down = np.concatenate([down, np.zeros((KB, P, 2 * P), down.dtype)], 2)
    down = down.reshape(KB, P, DOWN_UNITS, UNIT).transpose(0, 2, 1, 3).reshape(KB * DOWN_UNITS, P, UNIT)
    win = f(i["w_in_2"])[0]
    rw = in_tiles(win[:, :2176])
    rw = np.concatenate([rw[16:], rw[:16]])
    cv = in_tiles(win[:, 2176:4224]).reshape(4, 4, P, UNIT).transpose(1, 0, 2, 3).reshape(16, P, UNIT)
    po = in_tiles(win[:, 4224:5248]).reshape(2, 4, P, UNIT).transpose(1, 0, 2, 3).reshape(8, P, UNIT)
    ga = in_tiles(win[:, 5248:]).reshape(3, 4, 2, P, UNIT)
    br = np.stack([in_tiles(b) for b in f(i["w_branch_2"])[0]])
    br = br.reshape(3, 4, 2, P, 512).transpose(0, 1, 3, 2, 4).reshape(3, 4, 1, P, UNIT)
    br = np.concatenate([ga, br], 2).reshape(36, P, UNIT)
    w = np.concatenate([in_tiles(f(i["xa_wkv"])[0]), sb, in_tiles(f(i["mix_wo"])[0]), in_tiles(f(i["xa_wq"])[0]),
                        in_tiles(f(i["xa_wo"])[0]), up, down, rw, cv, po, br, in_tiles(f(i["w_out_2"])[0])])
    assert w.shape == (UNITS, P, UNIT)
    col = lambda a: f(a).reshape(-1, P).T
    vec = np.concatenate([col(i[n]) for n in (
        "ln_g", "ln_b", "ffn_conv", "ffn_conv_b", "pre_norm_w_2", "post_norm_w_2", "mu_shift_2", "rwkv_w0_2",
        "rwkv_a0_2", "rwkv_k_k_2", "rwkv_k_a_2", "rwkv_r_k_2", "rwkv_gn_w_2", "rwkv_gn_b_2", "conv_w_2",
        "pool_scale_2")], 1)
    assert vec.shape == (P, VEC)
    small = np.concatenate([np.concatenate([f(i["rwkv_w_up_2"])[0], f(i["rwkv_a_up_2"])[0]]),
                            f(i["pool_w_2"])[0].transpose(1, 0, 2).reshape(P, 512)], 1)
    r, c = np.arange(P)[:, None], np.arange(P)[None]
    f32 = np.float32
    t = np.arange(SEQ)
    const = np.concatenate([
        np.eye(P, dtype=f32), np.full((P, P), 1.0 / D, f32), (r // HD_A == c // HD_A).astype(f32),
        -(r >= c).astype(f32), np.full((P, P), -1.0, f32), (r >= c) * f32(-2.0 ** 100), (r < c).astype(f32),
        *[((r // b % 2 == 0) & (c // b == r // b + 1)).astype(f32) for b in LEVELS],
        np.broadcast_to((t % CH != 0).astype(f32), (P, SEQ))], 1)
    count = np.stack([1.0 / np.minimum(t + 1, n) for n in POOL_WINDOWS]).astype(f32)
    count = np.ascontiguousarray(np.broadcast_to(count, (P, 4, SEQ)))
    act = lambda a: a.reshape(a.shape[0], KB, P).transpose(2, 1, 0)
    out = dict(w=w, xT=act(f(i["x"])[0]), memT=act(f(i["mem"])[0]), vec=vec, const=const, small=small, pool_count=count)
    return {k: np.ascontiguousarray(v) for k, v in out.items()}


def kernel(**inputs):
    import numpy as _np
    import concourse.bacc as _bacc
    from concourse import mybir as _mybir
    from concourse.bass_utils import run_bass_kernel_spmd as _run

    nc = _bacc.Bacc("TRN2", target_bir_lowering=False, num_devices=1)
    arrays = lay_out(inputs)
    args = [nc.dram_tensor(n, arrays[n].shape, _mybir.dt.float32, kind="ExternalInput").ap() for n in _INS]
    args.append(nc.dram_tensor("outT", (P, KB, SEQ), _mybir.dt.float32, kind="ExternalOutput").ap())
    build_block(nc, *args)
    got = _run(nc, [arrays], core_ids=[0]).results[0]["outT"]
    return _np.ascontiguousarray(_np.asarray(got).transpose(2, 1, 0).reshape(1, SEQ, D))
```

```python
import numpy as np
from contextlib import ExitStack

import concourse.bass as bass
from concourse import mybir

F32 = mybir.dt.float32
F32R = mybir.dt.float32r
ALU = mybir.AluOpType
ACT = mybir.ActivationFunctionType

P = 128
SEQ = 512
MEM = 256
D = 1024
KB = D // P
HD_A = 64
PAIRS = D // P
XA_HEADS = 4
D_FF = 2816
FFB = D_FF // P
NS = SEQ // P
CA = 4
CH = P
ALPHA = 2.0 ** 0.25
LN_EPS = 1e-5
RMS_EPS = 1e-6
GN_EPS = HD_A * 1e-5
DECAY = -float(np.exp(-0.5))

UNIT = 8 * P
STAGE_UNITS = [("mem_kv", 16), ("sb", 24), ("wo", 8), ("xq", 8), ("xo", 8), ("up", 44), ("down", 24),
               ("rwkv", 17), ("conv", 16), ("pool", 8), ("branch", 36), ("out", 8)]
U0, _u = {}, 0
for _name, _n in STAGE_UNITS:
    U0[_name] = _u
    _u += _n
UNITS = _u
DOWN_UNITS = 3

VEC_WIDTHS = [("ln_g", 24), ("ln_b", 24), ("ffn_conv", 3 * 2 * FFB), ("ffn_conv_b", 2 * FFB), ("pre", 8), ("post", 8),
              ("mu", 17), ("w0", 4), ("a0", 4), ("k_k", 4), ("k_a", 4), ("r_k", 4), ("gn_w", 4), ("gn_b", 4),
              ("conv_w", 12), ("pool_scale", 4)]
V0, _v = {}, 0
for _name, _n in VEC_WIDTHS:
    V0[_name] = _v
    _v += _n
VEC = _v

LEVELS = [1, 2, 4, 8, 16, 32, 64]
CONST_WIDTHS = [("ident", P), ("mean", P), ("heads", P), ("suffix", P), ("all", P), ("never", P), ("strict", P),
                ("levels", len(LEVELS) * P), ("scan", SEQ)]
C0, _c = {}, 0
for _name, _n in CONST_WIDTHS:
    C0[_name] = _c
    _c += _n
CONST = _c
POOL_WINDOWS = (2, 4, 8, 16)

REGION = {0: (0, 512), 1: (512, 384), 3: (896, 128), 2: (1024, 256)}
SCORES = 1280


def build_block(nc, w, xT, memT, vec, const, small, pool_count, outT):
    ctx = ExitStack()
    with ctx:
        def sem(name):
            return ctx.enter_context(nc.semaphore(name))

        def at(name, shape, kb, dt=F32):
            assert 0 <= kb and BASE + int(kb * 1024) + 4 * int(np.prod(shape[1:])) <= nc.sbuf_usable_end, name
            return nc.alloc_sbuf_tensor_at(name, shape, dt, offset=BASE + int(kb * 1024))

        BASE = 17408
        stage = at("stage", [P, 2, UNIT], 0)
        w_hi = at("w_hi", [P, 2, UNIT], 8, F32R)
        w_lo = at("w_lo", [P, 2, UNIT], 16, F32R)
        H = at("H", [P, KB, SEQ], 32)
        x_hi = at("x_hi", [P, KB, SEQ], 48, F32R)
        x_lo = at("x_lo", [P, KB, SEQ], 64, F32R)
        Y = at("Y", [P, KB, SEQ], 80)
        con = at("con", [P, C0["levels"]], 96)
        vcol = at("vcol", [P, VEC], 99.5)
        suffix = at("suffix", [P, P], 24, F32R)
        every = at("every", [P, P], 24.5, F32R)
        never = at("never", [P, P], 25, F32R)
        ident_r = at("ident_r", [P, P], 25.5, F32R)
        tmp = at("tmp", [P, 2, SEQ], 101.5)
        acc = at("acc", [P, SEQ], 105.5)
        acc2 = at("acc2", [P, SEQ], 107.5)
        square = at("square", [P, SEQ], 109.5)
        mean = at("mean", [P, SEQ], 111.5)
        rstd = at("rstd", [P, SEQ], 113.5)
        A0 = 115.5
        o_hi = at("o_hi", [P, KB, SEQ], A0, F32R)
        o_lo = at("o_lo", [P, KB, SEQ], A0 + 16, F32R)
        mem_k = at("mem_k", [P, KB, MEM], A0 + 32)
        mem_v = at("mem_v", [P, MEM // P, D], A0 + 40)
        m_hi = at("m_hi", [P, KB, MEM], A0 + 48, F32R)
        m_lo = at("m_lo", [P, KB, MEM], A0 + 56, F32R)
        mem = at("mem", [P, KB, MEM], A0 + 64)
        mem_vT = at("mem_vT", [P, 2, MEM], A0 + 72)
        q_sb = at("q_sb", [P, SEQ], A0 + 48)
        k_sb = at("k_sb", [P, SEQ], A0 + 50)
        vT_sb = at("vT_sb", [P, SEQ], A0 + 52)
        v_sb = at("v_sb", [P, NS, P], A0 + 54)
        soft = [at(f"soft{h}", [P, SCORES], 80 + 5 * h) for h in range(2)]
        keep = [at("keep0", [P, SCORES], 90), at("keep1", [P, SCORES], A0 + 56)]
        keep_hi = [at(f"keep_hi{h}", [P, SCORES], A0 + 61 + 5 * h, F32R) for h in range(2)]
        keep_lo = [at(f"keep_lo{h}", [P, SCORES], A0 + 71 + 5 * h, F32R) for h in range(2)]
        xq = at("xq", [P, KB, SEQ], A0 + 48)
        prob = at("prob", [P, 2, NS, MEM], A0 + 64)
        probT = at("probT", [P, 2, MEM // P, SEQ], A0 + 72)
        soft_max = at("soft_max", [P, XA_HEADS, NS], A0 + 80)
        soft_sum = at("soft_sum", [P, XA_HEADS, NS], A0 + 80.25)
        f_hi = at("f_hi", [P, FFB, SEQ], A0, F32R)
        f_lo = at("f_lo", [P, FFB, SEQ], A0 + 44, F32R)
        raw = at("raw", [P, 4, SEQ], 80)
        conv = at("conv", [P, 4, SEQ], 88)
        gate_t = at("gate_t", [P, 2, SEQ], 105.5)

        levels = at("levels", [P, len(LEVELS), P], 26)
        scan_keep = at("scan_keep", [P, SEQ], 29.5)
        sq2 = at("sq2", [P, 2, SEQ], 107.5)
        rw_a = at("rw_a", [P, CA, SEQ], A0)
        rw_rk = at("rw_rk", [P, 2 * CA, SEQ], A0 + 8)
        rw_r, rw_k = rw_rk[:, 0:CA, :], rw_rk[:, CA:2 * CA, :]
        rw_kk = at("rw_kk", [P, CA, SEQ], A0 + 24)
        rw_vz = at("rw_vz", [P, 2 * CA, SEQ], A0 + 32)
        rw_v, rw_z = rw_vz[:, 0:CA, :], rw_vz[:, CA:2 * CA, :]
        rw_L = at("rw_L", [P, CA, SEQ], A0 + 48)
        w_small = at("w_small", [P, 2, SEQ], A0 + 56)
        rw_e = at("rw_e", [P, CA, SEQ], A0 + 60)
        rw_t = at("rw_t", [P, CA, SEQ], A0 + 68)
        lora = at("lora", [P, SEQ], A0 + 84)
        rw_ld = at("rw_ld", [P, CA, SEQ], 80)
        rw_n = at("rw_n", [P, CA, SEQ], 88)
        omm = at("omm", [P, 17], A0 + 88.5)
        cen = at("cen", [P, CA, NS], A0 + 88.75)
        gfac = at("gfac", [P, CA, NS], A0 + 89)
        M = at("M", [P, 8, 4, P], 80)
        tok = at("tok", [P, 3, CA, P], 105.5)
        rh = at("rh", [P, SEQ], 111.5)
        sa = at("sa", [P, SEQ], 113.5)
        AR = at("AR", [P, CA, 2, P], A0 + 60)
        bkv = at("bkv", [P, 3, CA, P], A0 + 64)
        X = at("X", [P, 8, P], A0 + 70)
        Tt = at("Tt", [P, 8, P], A0 + 74)
        R1 = at("R1", [P, 8, P], A0 + 78)
        Mk = at("Mk", [P, 8, P], A0 + 82)
        Sz = at("Sz", [P, 8, HD_A], A0 + 86)
        scr = at("scr", [P, 12], A0 + 89.25)
        g_sq = at("g_sq", [P, CA, SEQ], A0 + 16)
        g_mu = at("g_mu", [P, CA, SEQ], A0 + 32)
        g_rs = at("g_rs", [P, CA, SEQ], A0 + 24)
        g_sz = at("g_sz", [P, CA, SEQ], A0 + 68)
        ys_hi = at("ys_hi", [P, 3 * CA, SEQ], A0, F32R)
        ys_lo = at("ys_lo", [P, 3 * CA, SEQ], A0 + 24, F32R)
        cb = at("cb", [P, 2, 4, SEQ], 80)
        sg = at("sg", [P, 2, SEQ], A0 + 60)
        pool_n = at("pool_n", [P, 4, SEQ], A0 + 64)
        pt = at("pt", [P, 2, SEQ], A0 + 72)
        pld = at("pld", [P, 2, SEQ], A0 + 76)
        mg_hi = at("mg_hi", [P, KB, SEQ], A0 + 48, F32R)
        mg_lo = at("mg_lo", [P, KB, SEQ], A0 + 64, F32R)
        gates = at("gates", [P, 4, SEQ], A0 + 80)
        bt = at("bt", [P, 4, SEQ], 105.5)

        ps = ctx.enter_context(nc.psum_tensor("ps", [P, 8, 512], F32))

        def scores(h):
            return ps[:, 2 + 3 * h:5 + 3 * h, :].rearrange("p b n -> p (b n)")

        def C(name, n=P):
            return con[:, C0[name]:C0[name] + n]

        def V(name, j=0):
            return vcol[:, bass.ds(V0[name] + j, 1)]

        ident = C("ident")

        landed = [sem(f"landed{j}") for j in range(2)]
        params_in = sem("params_in")
        x_in = sem("x_in")
        mem_in = [sem(f"mem_in{a}") for a in range(2)]
        whi_made = sem("whi_made")
        wlo_made = sem("wlo_made")
        unit_done = sem("unit_done")
        evac = sem("evac")
        mask_made = sem("mask_made")
        h_split = sem("h_split")
        m_hi_made = sem("m_hi_made")
        m_split = sem("m_split")
        mv_turned = sem("mv_turned")
        mv_taken = sem("mv_taken")
        out_sent = sem("out_sent")

        EV0 = {}
        n_ev = 0
        for name, n in (("mem_kv", 16), ("sb", 24), ("wo", 8), ("xq", 8), ("xo", 8), ("up", 44), ("down", 8),
                        ("rwkv", 17), ("conv", 16), ("pool", 8), ("branch", 24), ("out", 8)):
            EV0[name] = n_ev
            n_ev += n
        CREDIT = 2

        EACH = {"mean_made": dict(wo=1, xo=1, down=1), "msq_made": dict(wo=1, xo=1, down=1), "var_made0": dict(wo=1, xo=1, down=1),
                "centred": dict(wo=KB, xo=KB, down=KB), "h_made": dict(wo=KB, xo=KB, down=KB),
                "ln_made": dict(wo=1, xo=1, down=1, pre=1, out=1), "rstd_made": dict(wo=1, xo=1, down=1, pre=1, out=1),
                "var_made": dict(wo=1, xo=1, down=1, pre=1, out=1),
                "y_made": dict(wo=KB + CREDIT, xo=KB + CREDIT, down=KB + CREDIT),
                "acc_made": dict(wo=KB, xo=KB, down=KB),
                "acc2_made": dict(wo=KB, xo=KB, down=KB, out=KB),
                "sq_made": dict(wo=KB - 1, xo=KB - 1, down=KB - 1, pre=KB, out=KB - 1), "last_sq": dict(wo=1, xo=1, down=1, out=1),
                "sums_done": dict(wo=2, xo=2, down=2, pre=KB, out=1),
                "normed": dict(wo=KB, xo=KB, down=KB, pre=KB), "xhi_made": dict(wo=KB, xo=KB, pre=KB),
                "x_ready": dict(wo=KB, xo=KB, pre=KB)}
        BEFORE = {s: {n: sum(list(c.values())[:k]) for k, n in enumerate(c)} for s, c in EACH.items()}

        NORMS = {"wo": 0, "xo": 1, "down": 2}
        xin_hi = sem("xin_hi")
        mean_made = sem("mean_made")
        var_made0 = sem("var_made0")
        msq_made = sem("msq_made")
        last_sq = sem("last_sq")
        centred = sem("centred")
        ln_made = sem("ln_made")
        rstd_made = sem("rstd_made")
        y_made = sem("y_made")
        acc_made = sem("acc_made")
        sq_made = sem("sq_made")
        acc2_made = sem("acc2_made")
        sums_done = sem("sums_done")
        var_made = sem("var_made")
        normed = sem("normed")
        h_made = sem("h_made")
        xhi_made = sem("xhi_made")
        x_ready = sem("x_ready")

        sb_scored = sem("sb_scored")
        sb_abs = sem("sb_abs")
        sb_exp = sem("sb_exp")
        sb_ln = sem("sb_ln")
        sb_keep = sem("sb_keep")
        sb_khi = sem("sb_khi")
        sb_klo = sem("sb_klo")
        sb_summed = sem("sb_summed")
        sb_w = sem("sb_w")
        sb_vturn = sem("sb_vturn")
        sb_v = sem("sb_v")
        sb_pv = sem("sb_pv")
        sb_ohi = sem("sb_ohi")
        sb_o = sem("sb_o")

        xa_scored = sem("xa_scored")
        xa_max = sem("xa_max")
        xa_nmax = sem("xa_nmax")
        xa_exp = sem("xa_exp")
        xa_rec = sem("xa_rec")
        xa_prob = sem("xa_prob")
        xa_turned = sem("xa_turned")
        xa_pT0 = sem("xa_pT0")
        xa_pT1 = sem("xa_pT1")
        xa_pv = sem("xa_pv")
        xa_ohi = sem("xa_ohi")
        xa_o = sem("xa_o")

        ff_conv = sem("ff_conv")
        ff_tap = sem("ff_tap")
        ff_sq = sem("ff_sq")
        ff_poly = sem("ff_poly")
        ff_arg = sem("ff_arg")
        ff_sig = sem("ff_sig")
        ff_vg = sem("ff_vg")
        ff_f = sem("ff_f")
        ff_hi = sem("ff_hi")
        ff_made = sem("ff_made")

        rw_shift0_s = sem("rw_shift0")
        rw_shifted_s = sem("rw_shifted")
        rw_tanh_s = sem("rw_tanh")
        rw_lora_mm_s = sem("rw_lora_mm")
        rw_sig_s = sem("rw_sig")
        rw_scan_s = sem("rw_scan")
        rw_kksq_s = sem("rw_kksq")
        rw_ss_mm_s = sem("rw_ss_mm")
        rw_max_s = sem("rw_max")
        rw_sqrt_s = sem("rw_sqrt")
        rw_lc_s = sem("rw_lc")
        rw_e_s = sem("rw_e")
        rw_barg_s = sem("rw_barg")
        rw_bmm_s = sem("rw_bmm")
        rw_bonus_s = sem("rw_bonus")
        rw_prep_s = sem("rw_prep")
        rw_kt_s = sem("rw_kt")
        small_in_s = sem("small_in")
        levels_in_s = sem("levels_in")
        pooln_in_s = sem("pooln_in")
        ch_ar_s = sem("ch_ar")
        ch_bkv_s = sem("ch_bkv")
        ch_turned_s = sem("ch_turned")
        ch_b_s = sem("ch_b")
        ch_k_s = sem("ch_k")
        ch_vt_s = sem("ch_vt")
        ch_scored_s = sem("ch_scored")
        ch_ab_s = sem("ch_ab")
        ch_m_s = sem("ch_m")
        ch_mask_s = sem("ch_mask")
        ch_y1_s = sem("ch_y1")
        ch_t1_s = sem("ch_t1")
        ch_tt0_s = sem("ch_tt0")
        ch_x0_s = sem("ch_x0")
        ch_mk_s = sem("ch_mk")
        ch_r_s = sem("ch_r")
        ch_rb_s = sem("ch_rb")
        ch_xmm_s = sem("ch_xmm")
        ch_ymm_s = sem("ch_ymm")
        ch_xn_s = sem("ch_xn")
        ch_yn_s = sem("ch_yn")
        ch_rh_mm_s = sem("ch_rh_mm")
        ch_rh_s = sem("ch_rh")
        ch_sa_mm_s = sem("ch_sa_mm")
        ch_sa_s = sem("ch_sa")
        ch_y_mm_s = sem("ch_y_mm")
        ch_s_mm_s = sem("ch_s_mm")
        ch_y_s = sem("ch_y")
        ch_s0_s = sem("ch_s0")
        ch_s_s = sem("ch_s")
        ch_wait_s = sem("ch_wait")
        gn_sq_s = sem("gn_sq")
        gn_mm_s = sem("gn_mm")
        gn_mu_s = sem("gn_mu")
        gn_v_s = sem("gn_v")
        gn_v2_s = sem("gn_v2")
        gn_ln_s = sem("gn_ln")
        gn_rs_s = sem("gn_rs")
        gn_out_s = sem("gn_out")
        gn_hi_s = sem("gn_hi")
        gn_lo_s = sem("gn_lo")
        gn_sig_s = sem("gn_sig")
        cv_sig_s = sem("cv_sig")
        cv_out_s = sem("cv_out")
        cv_hi_s = sem("cv_hi")
        cv_lo_s = sem("cv_lo")
        cv_link_s = sem("cv_link")
        pl_sig_s = sem("pl_sig")
        pl_pooled_s = sem("pl_pooled")
        pl_mm_s = sem("pl_mm")
        pl_out_s = sem("pl_out")
        pl_hi_s = sem("pl_hi")
        pl_lo_s = sem("pl_lo")
        br_taken_s = sem("br_taken")
        br_sum_s = sem("br_sum")
        mg_hi_made_s = sem("mg_hi_made")
        mg_ready_s = sem("mg_ready")
        fin_s = sem("fin")
        fin0_s = sem("fin0")
        rw_link_s = sem("rw_link")

        block = ctx.enter_context(nc.Block())

        @block.sync
        def _(sp):
            sp.dma_start(stage[:, 0, :], w[0]).then_inc(landed[0], 16)
            for a in range(2):
                sp.dma_start(mem[:, 4 * a:4 * a + 4, :], memT[:, 4 * a:4 * a + 4, :]).then_inc(mem_in[a], 16)
            sp.dma_start(stage[:, 1, :], w[1]).then_inc(landed[1], 16)
            sp.dma_start(H[:], xT).then_inc(x_in, 16)
            with sp.Fori(1, UNITS // 2) as i:
                for j in range(2):
                    sp.wait_ge(wlo_made, 2 * i + (j - 1))
                    sp.dma_start(stage[:, j, :], w[2 * i + j]).then_inc(landed[j], 16)
            for u in range(UNITS // 2 * 2, UNITS):
                sp.wait_ge(wlo_made, u - 1)
                sp.dma_start(stage[:, u % 2, :], w[u]).then_inc(landed[u % 2], 16)
            with sp.Fori(0, KB) as k:
                sp.wait_ge(fin_s, k + 1)
                sp.dma_start(outT[:, k, :], H[:, k, :]).then_inc(out_sent, 16)
            sp.wait_ge(out_sent, 16 * KB)

        @block.tensor
        def _(pe):
            pe.sem_inc(unit_done, CREDIT)
            pe.sem_inc(mv_turned, CREDIT)

            def product(out, u, slot, hi, lo, ready=None, blocks=8, k0=0, last_k=None, done=True):
                pe.wait_ge(wlo_made, u + 1)
                for k in range(blocks):
                    if ready is not None:
                        pe.wait_ge(*ready(k))
                    wh, wl = w_hi[:, slot, k * P:(k + 1) * P], w_lo[:, slot, k * P:(k + 1) * P]
                    first = k0 + k == 0
                    end = k0 + k == (blocks - 1 if last_k is None else last_k)
                    pe.matmul(out, wl, hi(k), start=first, stop=False)
                    pe.matmul(out, wh, lo(k), start=False, stop=False)
                    mm = pe.matmul(out, wh, hi(k), start=False, stop=end)
                if done:
                    mm.then_inc(unit_done, 1)

            def two_products(u, hi, lo, ready):
                pe.wait_ge(wlo_made, u + 2)
                order = [(n, k) for k in range(4) for n in range(2)] + [(0, 4), (0, 5), (1, 4), (0, 6), (0, 7), (1, 5), (1, 6), (1, 7)]
                for n, k in order:
                    b = (u + n) % 2
                    if n == 0:
                        pe.wait_ge(*ready(k))
                    wh, wl = w_hi[:, b, k * P:(k + 1) * P], w_lo[:, b, k * P:(k + 1) * P]
                    pe.matmul(ps[:, b, :], wl, hi(k), start=(k == 0), stop=False)
                    pe.matmul(ps[:, b, :], wh, lo(k), start=False, stop=False)
                    mm = pe.matmul(ps[:, b, :], wh, hi(k), start=False, stop=(k == KB - 1))
                    if k == KB - 1:
                        mm.then_inc(unit_done, 1)

            def x_rows(k):
                return x_hi[:, k, :]

            def x_rows_lo(k):
                return x_lo[:, k, :]

            pe.wait_ge(m_split, 2)
            with pe.Fori(0, 2) as i:
                for j in range(4):
                    u = 4 * i + j
                    pe.wait_ge(evac, u + 1)
                    product(ps[:, j % 2, 0:MEM], u, j % 2, lambda k: m_hi[:, k, :], lambda k: m_lo[:, k, :])

            def turn_mem_v(n, b):
                pe.wait_ge(evac, n + (8 + CREDIT + 1))
                pe.wait_ge(mv_taken, n + 1)
                for t in range(MEM // P):
                    mm = pe.transpose(ps[:, 2 + b, t * P:(t + 1) * P], mem_vT[:, b, t * P:(t + 1) * P], ident)
                mm.then_inc(mv_turned, 1)

            pe.wait_ge(params_in, 32)
            def value_product(n, b):
                pe.wait_ge(evac, n + 9)
                product(ps[:, b, 0:MEM], n + 8, b, lambda k: m_hi[:, k, :], lambda k: m_lo[:, k, :])

            value_product(0, 0)
            with pe.Fori(0, 3) as i:
                for j in range(2):
                    value_product(2 * i + (j + 1), 1 - j)
                    turn_mem_v(2 * i + j, j)
            value_product(7, 1)
            for j in range(2):
                turn_mem_v(6 + j, j)

            E = EV0["sb"] + CREDIT
            pe.wait_ge(mask_made, 4)
            pe.wait_ge(mv_taken, 8 + CREDIT)
            pe.wait_ge(h_split, 1)

            def pv(g, h, bank=1):
                pe.wait_ge(sb_w, 2 * g + (h + 1))
                for i in range(NS):
                    o, n = REGION[i]
                    mm = pe.matmul(ps[64 * h:64 * h + 64, bank, SEQ - n:SEQ], v_sb[:, i, 64 * h:64 * h + 64],
                                   soft[h][:, o:o + n], start=(i == 0), stop=(i == NS - 1), skip_group_check=True)
                mm.then_inc(sb_pv, 1)

            def pair(g, b, base, first=False, second=None):
                u = base
                if second is not None:
                    pe.wait_ge(sb_o, second)
                product(ps[:, 1, :], u, b, x_rows, x_rows_lo)
                if not first:
                    pe.wait_ge(sb_v, g)
                product(ps[:, 0, :], u + 1, 1 - b, x_rows, x_rows_lo)
                if not first:
                    pe.wait_ge(evac, 3 * g + (E + 1))
                    pv(g - 1, 0)
                pe.wait_ge(evac, 3 * g + (E + 2))
                for h in range(2):
                    if h and not first:
                        pe.wait_ge(sb_w, 2 * g)
                    for i in (0, 1, 3, 2):
                        o, n = REGION[i]
                        pe.matmul(scores(h)[:, o:o + n], k_sb[64 * h:64 * h + 64, i * P:(i + 1) * P],
                                  q_sb[64 * h:64 * h + 64, SEQ - n:SEQ], start=(i != 3), stop=False,
                                  skip_group_check=True)
                        mm = pe.matmul(scores(h)[:, o:o + P], ident_r[:], never[:], start=False, stop=False,
                                       skip_group_check=True)
                    mm.then_inc(sb_scored, 1)
                if not first:
                    pv(g - 1, 1)
                product(ps[:, 0, :], u + 2, b, x_rows, x_rows_lo)
                for h in range(2):
                    pe.wait_ge(sb_klo, 2 * g + (h + 1))
                    for i in range(NS):
                        o, n = REGION[i]
                        for s in range(i, NS):
                            so, sn = REGION[s]
                            m = suffix if s == i else every
                            for part in (keep_hi, keep_lo):
                                mm = pe.matmul(scores(h)[:, o + n - sn:o + n], m[:], part[h][:, so:so + sn],
                                               start=False, stop=(s == NS - 1 and part is keep_lo),
                                               skip_group_check=True)
                    mm.then_inc(sb_summed, 1)
                    if h == 0:
                        pe.wait_ge(evac, 3 * g + (E + 3))
                        for i in range(NS):
                            mm = pe.transpose(ps[:, 0, i * P:(i + 1) * P], vT_sb[:, i * P:(i + 1) * P], ident)
                        mm.then_inc(sb_vturn, 1)

            pair(0, 0, U0["sb"], first=True)
            pair(1, 1, U0["sb"] + 3)
            with pe.Fori(1, PAIRS // 2) as i:
                pair(2 * i, 0, 6 * i + U0["sb"], second=2 * i - 1)
                pair(2 * i + 1, 1, 6 * i + (U0["sb"] + 3), second=2 * i)
            pe.wait_ge(sb_v, PAIRS)
            for h in range(2):
                pv(PAIRS - 1, h, 2)

            def sums(n, both=True):
                if both:
                    pe.wait_ge(acc_made, KB + BEFORE["acc_made"][n])
                    pe.matmul(ps[:, 2, :], C("mean"), acc[:], start=True, stop=False)
                pe.wait_ge(acc2_made, KB + BEFORE["acc2_made"][n])
                pe.matmul(ps[:, 3, :], C("mean"), acc2[:], start=True, stop=False)
                if both:
                    pe.wait_ge(y_made, KB + CREDIT + BEFORE["y_made"][n])
                    pe.matmul(ps[:, 2, :], C("mean"), Y[:, KB - 1, :], start=False, stop=True).then_inc(sums_done, 1)
                pe.wait_ge(last_sq, 1 + BEFORE["last_sq"][n])
                pe.matmul(ps[:, 3, :], C("mean"), rstd[:], start=False, stop=True).then_inc(sums_done, 1)

            def tiles(n, hi, lo, ready, free=None):
                pe.wait_ge(evac, EV0[n] + CREDIT)
                two_products(U0[n], hi, lo, ready)
                with pe.Fori(1, KB // 2) as i:
                    for j in range(2):
                        u = 2 * i + (U0[n] + j)
                        b = (U0[n] + j) % 2
                        pe.wait_ge(evac, 2 * i + (EV0[n] + j + CREDIT - 1))
                        product(ps[:, b, :], u, b, hi, lo)

            def o_rows(k):
                return o_hi[:, k, :]

            def o_rows_lo(k):
                return o_lo[:, k, :]

            pe.wait_ge(sb_o, PAIRS - 1)
            tiles("wo", o_rows, o_rows_lo, lambda k: (sb_o, k + 1))
            sums("wo")

            def xa_scores(h):
                if h >= 1:
                    pe.wait_ge(xa_exp, NS * h)
                pe.wait_ge(evac, EV0["xq"] + CREDIT + 2 * h + 2)
                for t in range(NS):
                    for d in range(2):
                        mm = pe.matmul(ps[:, 2 + t // 2, (t % 2) * MEM:(t % 2 + 1) * MEM],
                                       xq[:, 2 * h + d, t * P:(t + 1) * P], mem_k[:, 2 * h + d, :],
                                       start=(d == 0), stop=(d == 1))
                mm.then_inc(xa_scored, 1)

            def xa_out(h):
                pe.wait_ge(xa_prob, h + 1)
                if h >= 1:
                    pe.wait_ge(xa_pT0, h)
                    pe.wait_ge(xa_pT1, h)
                for m in range(MEM // P):
                    for t in range(NS):
                        mm = pe.transpose(ps[:, 4 + m, t * P:(t + 1) * P], prob[:, h % 2, t, m * P:(m + 1) * P], ident)
                    mm.then_inc(xa_turned, 1)
                pe.wait_ge(xa_pT0, h + 1)
                pe.wait_ge(xa_pT1, h + 1)
                if h >= 1:
                    pe.wait_ge(xa_o, 2 * h)
                for d in range(2):
                    for m in range(MEM // P):
                        mm = pe.matmul(ps[:, 6 + d, :], mem_v[:, m, (2 * h + d) * P:(2 * h + d + 1) * P],
                                       probT[:, h % 2, m, :], start=(m == 0), stop=(m == MEM // P - 1))
                    mm.then_inc(xa_pv, 1)

            pe.wait_ge(mv_taken, 8 + CREDIT)
            for h in range(XA_HEADS):
                if h == 0:
                    pe.wait_ge(evac, EV0["xq"] + CREDIT)
                    two_products(U0["xq"], x_rows, x_rows_lo, lambda k: (x_ready, k + 1 + BEFORE["x_ready"]["wo"]))
                for d in range(2 if h else 0):
                    u = U0["xq"] + 2 * h + d
                    pe.wait_ge(evac, EV0["xq"] + 2 * h + d + CREDIT - 1)
                    product(ps[:, u % 2, :], u, u % 2, x_rows, x_rows_lo)
                if h:
                    xa_out(h - 1)
                xa_scores(h)
            xa_out(XA_HEADS - 1)
            tiles("xo", o_rows, o_rows_lo, lambda k: (xa_o, k + 1))
            sums("xo")

            pe.wait_ge(evac, EV0["up"] + CREDIT)
            two_products(U0["up"], x_rows, x_rows_lo, lambda k: (x_ready, k + 1 + BEFORE["x_ready"]["xo"]))
            with pe.Fori(1, FFB) as i:
                for j in range(2):
                    u = 2 * i + (U0["up"] + j)
                    b = (U0["up"] + j) % 2
                    pe.wait_ge(evac, 2 * i + (EV0["up"] + j + CREDIT - 1))
                    product(ps[:, b, :], u, b, x_rows, x_rows_lo)
            with pe.Fori(0, 2) as i:
                for j in range(4):
                    pe.wait_ge(evac, 4 * i + (EV0["down"] + j + CREDIT - 1))
                    for c in range(DOWN_UNITS):
                        u = 12 * i + (U0["down"] + 3 * j + c)
                        product(ps[:, j % 2, :], u, (U0["down"] + 3 * j + c) % 2,
                                lambda k: f_hi[:, 8 * c + k, :], lambda k: f_lo[:, 8 * c + k, :],
                                (lambda k: (ff_made, 8 * c + k + 3)) if j == 0 else None,
                                blocks=min(8, FFB - 8 * c), k0=8 * c, last_k=FFB - 1)
            sums("down")

            for k in range(KB):
                pe.wait_ge(sq_made, k + 1 + BEFORE["sq_made"]["pre"])
                pe.matmul(ps[:, 4, :], C("mean"), sq2[:, k % 2, :], start=(k == 0),
                          stop=(k == KB - 1)).then_inc(sums_done, 1)

            def shifted(t0, n):
                with pe.Fori(0, n // 2) as i:
                    for j in range(2):
                        b = U0["rwkv"] + t0 + j
                        pe.wait_ge(evac, 2 * i + (EV0["rwkv"] + t0 + j + CREDIT - 1))
                        product(ps[:, b % 2, :], 2 * i + b, b % 2, x_rows, x_rows_lo)

            pe.wait_ge(evac, EV0["rwkv"] + CREDIT)
            two_products(U0["rwkv"], x_rows, x_rows_lo, lambda k: (x_ready, k + 1 + BEFORE["x_ready"]["pre"]))
            pe.wait_ge(evac, EV0["rwkv"] + 2 + CREDIT - 1)
            product(ps[:, (U0["rwkv"] + 2) % 2, :], U0["rwkv"] + 2, (U0["rwkv"] + 2) % 2, x_rows, x_rows_lo)
            shifted(3, 2)
            pe.wait_ge(small_in_s, 16)
            pe.wait_ge(rw_tanh_s, 1)
            for part in range(2):
                for j in range(CA):
                    if part and j >= 2:
                        pe.wait_ge(rw_sig_s, j - 1)
                    bank = 2 + (4 * part + j) % 6
                    pe.matmul(ps[:, bank, :], w_small[64 * part:64 * part + 64, 0, j * P:(j + 1) * P],
                              lora[64 * part:64 * part + 64, :], start=True, stop=True).then_inc(rw_lora_mm_s, 1)
            shifted(5, 4)
            shifted(9, 2)
            pe.wait_ge(rw_kksq_s, 1)
            pe.wait_ge(rw_sig_s, 8)
            for j in range(CA):
                pe.matmul(ps[:, 4 + j, :], C("heads"), rw_t[:, j, :], start=True, stop=True).then_inc(rw_ss_mm_s, 1)
            shifted(11, 2)
            shifted(13, 2)
            pe.wait_ge(rw_max_s, 1)
            for j in range(CA):
                pe.wait_ge(rw_barg_s, j + 1)
                pe.matmul(ps[:, 4 + j, :], C("heads"), rw_t[:, j, :], start=True, stop=True).then_inc(rw_bmm_s, 1)
            shifted(15, 2)

            pe.sem_inc(ch_scored_s, 1)
            pe.sem_inc(ch_r_s, 2)
            RB, XB, YB = (3, 4), (5, 6), (7, 0)

            def heads_of(q):
                return range(4 * q, 4 * q + 4)

            def bank_of(b, h):
                return ps[:, b, (h % 4) * P:(h % 4 + 1) * P]

            with pe.Fori(0, NS) as c:
                for n in range(3):
                    pe.wait_ge(ch_bkv_s, 3 * c + (n + 1))
                    for j in range(CA):
                        mm = pe.transpose(ps[:, n, j * P:(j + 1) * P], bkv[:, n, j, :], ident)
                    mm.then_inc(ch_turned_s, 1)
                pe.wait_ge(ch_ar_s, 2 * c + 2)
                pe.wait_ge(rw_bonus_s, CA)
                pe.wait_ge(ch_y_s, c + 1)
                pe.wait_ge(ch_s_s, 2 * c + 2)
                for p in range(4):
                    if p >= 2:
                        pe.wait_ge(ch_m_s, 8 * c + (2 * p - 2))
                    for n in range(2):
                        for h in (2 * p, 2 * p + 1):
                            r0 = 64 * (h % 2)
                            mm = pe.matmul(ps[:, 3 + h % 4, 256 * n:256 * n + 256], bkv[r0:r0 + 64, n, p, :],
                                           AR[r0:r0 + 64, p, :, :], start=True, stop=True)
                            if n:
                                mm.then_inc(ch_scored_s, 1)
                pe.wait_ge(ch_k_s, c + 1)
                pe.wait_ge(ch_vt_s, c + 1)
                for h in range(8):
                    pe.wait_ge(ch_mask_s, 8 * c + (h + 1))
                    o = ps[:, 1, h * HD_A:(h + 1) * HD_A]
                    pe.matmul(o, AR[:, h // 2, 0, :], Sz[:, h, :], start=True, stop=False)
                    mm = pe.matmul(o, M[:, h, 2, :], tok[:, 2, h // 2, 64 * (h % 2):64 * (h % 2) + 64],
                                   start=False, stop=True)
                mm.then_inc(ch_rh_mm_s, 1)
                pe.wait_ge(ch_m_s, 8 * c + 8)
                pe.wait_ge(ch_b_s, c + 1)
                for q in range(2):
                    pe.wait_ge(ch_y1_s, 2 * c + (q + 1))
                    for h in heads_of(q):
                        mm = pe.transpose(bank_of(XB[q], h), Tt[:, h, :], ident)
                    mm.then_inc(ch_t1_s, 1)

                def level(idx, x_idx, with_x):
                    for q in range(2):
                        pe.wait_ge(ch_mk_s, 2 * idx + (q + 1))
                        pe.wait_ge(ch_x0_s, 2 * c + (q + 1))
                        pe.wait_ge(ch_xn_s, 2 * x_idx + (q + 1))
                        for h in heads_of(q):
                            mm = pe.matmul(bank_of(RB[q], h), Mk[:, h, :], X[:, h, :], start=True, stop=True)
                        mm.then_inc(ch_r_s, 1)
                    for q in range(2):
                        pe.wait_ge(ch_rb_s, 2 * idx + (q + 1))
                        pe.wait_ge(ch_yn_s, 2 * idx + (q + 1))
                        if with_x:
                            for h in heads_of(q):
                                mm = pe.matmul(bank_of(XB[q], h), Tt[:, h, :], R1[:, h, :], start=True, stop=True)
                            mm.then_inc(ch_xmm_s, 1)
                        for h in heads_of(q):
                            mm = pe.matmul(bank_of(YB[q], h), R1[:, h, :], Tt[:, h, :], start=True, stop=True)
                        mm.then_inc(ch_ymm_s, 1)

                NL = len(LEVELS) - 1

                with pe.Fori(0, NL - 1) as lv:
                    level(NL * c + lv, (NL - 1) * c + lv, True)
                level(NL * c + (NL - 1), (NL - 1) * c + (NL - 1), False)
                pe.wait_ge(ch_rh_s, c + 1)
                pe.wait_ge(ch_vt_s, c + 1)
                pe.wait_ge(ch_yn_s, 2 * NL * (c + 1) + 2 * 1)
                for h in range(8):
                    mm = pe.matmul(ps[:, 2, h * HD_A:(h + 1) * HD_A], Tt[:, h, :], rh[:, h * HD_A:(h + 1) * HD_A],
                                   start=True, stop=True)
                mm.then_inc(ch_sa_mm_s, 1)
                pe.wait_ge(ch_sa_s, c + 1)
                for h in range(8):
                    r0 = 64 * (h % 2)
                    v_h = tok[:, 2, h // 2, r0:r0 + 64]
                    sa_h = sa[:, h * HD_A:(h + 1) * HD_A]
                    o = ps[r0:r0 + 64, 4, (h // 2) * HD_A:(h // 2 + 1) * HD_A]
                    pe.matmul(o, tok[:, 0, h // 2, r0:r0 + 64], sa_h, start=True, stop=False)
                    mm = pe.matmul(o, tok[:, 1, h // 2, r0:r0 + 64], v_h, start=False, stop=True)
                mm.then_inc(ch_s_mm_s, 1)
                for h in range(8):
                    r0 = 64 * (h % 2)
                    v_h = tok[:, 2, h // 2, r0:r0 + 64]
                    sa_h = sa[:, h * HD_A:(h + 1) * HD_A]
                    o = ps[r0:r0 + 64, 3, (h // 2) * P:(h // 2 + 1) * P]
                    pe.matmul(o, Sz[:, h, :], AR[:, h // 2, 1, :], start=True, stop=False)
                    pe.matmul(o, sa_h, M[:, h, 1, :], start=False, stop=False)
                    mm = pe.matmul(o, v_h, M[:, h, 3, :], start=False, stop=True)
                mm.then_inc(ch_y_mm_s, 1)

            pe.wait_ge(ch_y_s, NS + 1)
            pe.wait_ge(ch_s_s, 2 * NS + 2)
            for j in range(CA):
                pe.matmul(ps[:, j, :], C("heads"), rw_r[:, j, :], start=True, stop=True)
            pe.wait_ge(gn_sq_s, 1)
            for j in range(CA):
                mm = pe.matmul(ps[:, 4 + j, :], C("heads"), g_sq[:, j, :], start=True, stop=True)
            mm.then_inc(gn_mm_s, 1)
            pe.wait_ge(gn_mu_s, 1)
            with pe.Fori(0, 2) as i:
                for j in range(8):
                    b = U0["conv"] + j
                    pe.wait_ge(evac, 8 * i + (EV0["conv"] + j + CREDIT - 1))
                    product(ps[:, b % 2, :], 8 * i + b, b % 2, x_rows, x_rows_lo)

            def mix(j):
                pe.wait_ge(pl_pooled_s, j + 1)
                if j >= 2:
                    pe.wait_ge(pl_out_s, j - 1)
                pe.matmul(ps[:, 2 + j % 2, :], w_small[:, 1, j * P:(j + 1) * P], pld[:, j % 2, :],
                          start=True, stop=True).then_inc(pl_mm_s, 1)

            pe.wait_ge(gn_v_s, 1)
            for j in range(CA):
                for c in range(2):
                    b = U0["pool"] + 2 * j + c
                    pe.wait_ge(evac, EV0["pool"] + 2 * j + c + CREDIT - 1)
                    product(ps[:, b % 2, :], b, b % 2, x_rows, x_rows_lo)
                if j:
                    mix(j - 1)

            def step(n, m, b, i=0, first=False):
                for d in range(2):
                    pe.wait_ge(evac, 8 * i + (EV0["branch"] + 2 * ((b - U0["branch"]) // 3) + d + CREDIT - 1))
                    product(ps[:, (b + d) % 2, :], 12 * i + (b + d), (b + d) % 2, x_rows, x_rows_lo)
                if first:
                    mix_late()
                st = (b - U0["branch"]) // 3
                pe.wait_ge(br_taken_s, 8 * i + (2 * st + 1))
                pe.wait_ge(br_taken_s, 8 * i + (2 * st + 2))
                pe.wait_ge(wlo_made, 12 * i + (b + 3))
                slot = b % 2
                for d in range(2):
                    for k in range(4):
                        kk = 4 * d + k
                        wh, wl = w_hi[:, slot, kk * P:(kk + 1) * P], w_lo[:, slot, kk * P:(kk + 1) * P]
                        hi, lo = ys_hi[:, CA * n + k, :], ys_lo[:, CA * n + k, :]
                        o = ps[:, 4 + 2 * (m % 2) + d, :]
                        pe.matmul(o, wl, hi, start=(k == 0), stop=False)
                        pe.matmul(o, wh, lo, start=False, stop=False)
                        mm = pe.matmul(o, wh, hi, start=False, stop=(k == 3))
                mm.then_inc(unit_done, 1)

            def mix_late():
                mix(CA - 1)
                pe.wait_ge(pl_lo_s, CA)

            for m in range(4):
                step(0, m, U0["branch"] + 3 * m, first=m == 0)
            with pe.Fori(1, 3) as i:
                for m in range(4):
                    step(i, m, U0["branch"] + 3 * m, i)
            tiles("out", lambda k: mg_hi[:, k, :], lambda k: mg_lo[:, k, :], lambda k: (mg_ready_s, k + 1))
            sums("out", both=False)

        @block.scalar
        def _(act):
            act.dma_start(con[:], const[:, 0:C0["levels"]]).then_inc(params_in, 16)
            act.dma_start(vcol[:], vec).then_inc(params_in, 16)
            act.dma_start(levels[:], const[:, C0["levels"]:C0["scan"]].rearrange("p (l n) -> p l n", n=P)).then_inc(levels_in_s, 16)
            act.dma_start(scan_keep[:], const[:, C0["scan"]:CONST]).then_inc(levels_in_s, 16)
            act.preload_act_table_set("natural_log_exp_and_others")
            act.sem_inc(evac, CREDIT)

            def split_hi(b, i=0, step=0):
                act.wait_ge(landed[b % 2], 8 * step * i + 16 * (b // 2 + 1))
                act.activation(w_hi[:, b % 2, :], stage[:, b % 2, :], ACT.Copy).then_inc(whi_made, 1)

            def take(dst, bank, n, width=SEQ, scale=1.0):
                act.wait_ge(unit_done, n)
                act.activation(dst, ps[:, bank, 0:width], ACT.Copy, scale=scale).then_inc(evac, 1)

            split_hi(0)
            for a in range(2):
                act.wait_ge(mem_in[a], 16)
                act.activation(m_hi[:, 4 * a:4 * a + 4, :], mem[:, 4 * a:4 * a + 4, :], ACT.Copy).then_inc(m_hi_made, 1)
            split_hi(1)
            with act.Fori(0, 4) as i:
                for j in range(2):
                    act.wait_ge(unit_done, 2 * i + (j + CREDIT + 1))
                    split_hi(2 + j, i, 2)
                    take(mem_k[:, 2 * i + j, :], j, 2 * i + (j + CREDIT + 1), MEM)
            with act.Fori(0, 4) as i:
                for j in range(2):
                    act.wait_ge(unit_done, 2 * i + (8 + j + CREDIT + 1))
                    split_hi(10 + j, i, 2)
                    act.wait_ge(mv_turned, 2 * i + (j + 1))
                    take(mem_vT[:, j, :], j, 2 * i + (8 + j + CREDIT + 1), MEM)
            act.wait_ge(params_in, 32)
            act.activation(suffix[:], C("suffix"), ACT.Copy).then_inc(mask_made, 1)
            act.activation(every[:], C("all"), ACT.Copy).then_inc(mask_made, 1)
            act.activation(ident_r[:], ident, ACT.Copy).then_inc(mask_made, 1)
            act.activation(never[:], C("never"), ACT.Copy).then_inc(mask_made, 1)

            def pair(g, i, b, first=False):
                n = 6 * i + (b + CREDIT)
                if not first:
                    act.wait_ge(sb_scored, 2 * g)
                take(q_sb[:], 1, n + 1, scale=float(HD_A) ** -0.5)
                split_hi(b + 2, i, 6)
                take(k_sb[:], 0, n + 2)
                split_hi(b + 3, i, 6)
                for h in range(2):
                    act.wait_ge(sb_scored, 2 * g + (h + 1))
                    if not first:
                        act.wait_ge(sb_pv, 2 * g + (h - 1))
                    act.activation(soft[h][:], scores(h)[:, 0:SCORES], ACT.Abs).then_inc(sb_abs, 1)
                    act.wait_ge(sb_abs, 2 * g + (h + 1))
                    act.activation(soft[h][:], soft[h][:], ACT.Exp, scale=-1.0).then_inc(sb_exp, 1)
                    act.wait_ge(sb_exp, 2 * g + (h + 1))
                    act.activation(soft[h][:], soft[h][:], ACT.Ln, bias=1.0).then_inc(sb_ln, 1)
                if not first:
                    outputs(g - 1)
                    act.wait_ge(sb_vturn, g)
                take(vT_sb[:], 0, n + 3)
                split_hi(b + 4, i, 6)
                for h in range(2):
                    act.wait_ge(sb_summed, 2 * g + (h + 1))
                    act.activation(soft[h][:], scores(h)[:, 0:SCORES], ACT.Exp).then_inc(sb_w, 1)

            def outputs(g, bank=1):
                act.wait_ge(sb_pv, 2 * g + 2)
                act.activation(o_hi[:, g, :], ps[:, bank, :], ACT.Copy).then_inc(sb_ohi, 1)

            pair(0, 0, U0["sb"], first=True)
            pair(1, 0, U0["sb"] + 3)
            with act.Fori(1, PAIRS // 2) as i:
                pair(2 * i, i, U0["sb"])
                pair(2 * i + 1, i, U0["sb"] + 3)
            outputs(PAIRS - 1, 2)

            def tiles(n):
                with act.Fori(0, 4) as i:
                    for j in range(2):
                        act.wait_ge(y_made, 2 * i + (j + 1) + BEFORE["y_made"][n])
                        take(tmp[:, j, :], j, 2 * i + (U0[n] + j + CREDIT + 1))
                        split_hi(U0[n] + j + 2, i, 2)

            def statistics(n, both=True):
                if both:
                    act.wait_ge(y_made, KB + CREDIT + BEFORE["y_made"][n])
                    act.activation(rstd[:], Y[:, KB - 1, :], ACT.Square).then_inc(last_sq, 1)
                    act.wait_ge(sums_done, 1 + BEFORE["sums_done"][n])
                    act.activation(mean[:], ps[:, 2, :], ACT.Copy).then_inc(mean_made, 1)
                    act.activation(square[:], ps[:, 2, :], ACT.Square).then_inc(msq_made, 1)
                act.wait_ge(var_made, 1 + BEFORE["var_made"][n])
                act.activation(rstd[:], rstd[:], ACT.Ln).then_inc(ln_made, 1)
                act.wait_ge(ln_made, 1 + BEFORE["ln_made"][n])
                act.activation(rstd[:], rstd[:], ACT.Exp, scale=-0.5).then_inc(rstd_made, 1)

            def scale_shift(n):
                v = KB * NORMS[n]
                with act.Fori(0, KB) as k:
                    act.wait_ge(normed, k + 1 + BEFORE["normed"][n])
                    g, s = V("ln_g", v + k), V("ln_b", v + k)
                    act.activation(H[:, k, :], Y[:, k, :], ACT.Identity, bias=s, scale=g).then_inc(h_made, 1)
                    act.activation(x_hi[:, k, :], Y[:, k, :], ACT.Identity, bias=s, scale=g).then_inc(xhi_made, 1)

            tiles("wo")
            statistics("wo")
            scale_shift("wo")

            def xa_soft(h):
                act.wait_ge(xa_nmax, h + 1)
                if h >= 2:
                    act.wait_ge(xa_turned, 2 * (h - 1))
                for t in range(NS):
                    act.activation(prob[:, h % 2, t, :], ps[:, 2 + t // 2, (t % 2) * MEM:(t % 2 + 1) * MEM], ACT.Exp,
                                   bias=soft_max[:, h, t:t + 1], scale=float(D // XA_HEADS) ** -0.5,
                                   accum_out=soft_sum[:, h, t:t + 1]).then_inc(xa_exp, 1)

            def xa_take(h):
                act.wait_ge(xa_turned, 2 * h + 1)
                if h >= 2:
                    act.wait_ge(xa_pv, 2 * (h - 1))
                act.activation(probT[:, h % 2, 0, :], ps[:, 4, :], ACT.Copy).then_inc(xa_pT0, 1)
                for d in range(2):
                    act.wait_ge(xa_pv, 2 * h + d + 1)
                    act.activation(o_hi[:, 2 * h + d, :], ps[:, 6 + d, :], ACT.Copy).then_inc(xa_ohi, 1)

            for h in range(XA_HEADS):
                for d in range(2):
                    u = U0["xq"] + 2 * h + d
                    take(xq[:, 2 * h + d, :], u % 2, u + CREDIT + 1)
                    split_hi(u + 2)
                if h:
                    xa_take(h - 1)
                xa_soft(h)
            xa_take(XA_HEADS - 1)
            tiles("xo")
            statistics("xo")
            scale_shift("xo")

            act.preload_act_table_set("sigmoid_and_others")
            with act.Fori(0, FFB // 2) as i:
                for j in range(4):
                    p = 2 * i + j // 2
                    act.wait_ge(ff_conv, 4 * i + (j + 1))
                    take(raw[:, j, :], j % 2, 4 * i + (U0["up"] + j + CREDIT + 1))
                    split_hi(U0["up"] + j + 2, i, 4)
                    if j % 2:
                        act.wait_ge(ff_arg, p + 1)
                        act.activation(gate_t[:, j // 2, :], gate_t[:, j // 2, :], ACT.Sigmoid).then_inc(ff_sig, 1)
                        act.wait_ge(ff_f, p + 3)
                        act.activation(f_hi[:, p, :], conv[:, j - 1, :], ACT.Copy).then_inc(ff_hi, 1)
            act.preload_act_table_set("natural_log_exp_and_others")
            with act.Fori(0, 4) as i:
                for j in range(2):
                    for c in range(DOWN_UNITS):
                        b = U0["down"] + DOWN_UNITS * j + c
                        if c < DOWN_UNITS - 1:
                            act.wait_ge(unit_done, 6 * i + (b + CREDIT + 1))
                        else:
                            act.wait_ge(y_made, 2 * i + (j + 1) + BEFORE["y_made"]["down"])
                            take(tmp[:, j, :], j, 6 * i + (b + CREDIT + 1))
                        split_hi(b + 2, i, 6)
            act.dma_start(w_small[:], small.rearrange("p (a n) -> p a n", n=SEQ)).then_inc(small_in_s, 16)
            statistics("down")
            for k in range(KB):
                act.wait_ge(normed, k + 1 + BEFORE["normed"]["down"])
                g, t = V("ln_g", KB * NORMS["down"] + k), V("ln_b", KB * NORMS["down"] + k)
                if k >= 2:
                    act.wait_ge(sums_done, k - 1 + BEFORE["sums_done"]["pre"])
                act.activation(sq2[:, k % 2, :], Y[:, k, :], ACT.Square, bias=t, scale=g).then_inc(sq_made, 1)
                act.activation(H[:, k, :], Y[:, k, :], ACT.Identity, bias=t, scale=g).then_inc(h_made, 1)
            statistics("pre", both=False)
            with act.Fori(0, KB) as k:
                act.wait_ge(normed, k + 1 + BEFORE["normed"]["pre"])
                act.activation(x_hi[:, k, :], Y[:, k, :], ACT.Copy).then_inc(xhi_made, 1)

            u = U0["rwkv"]
            take(tmp[:, u % 2, :], u % 2, u + CREDIT + 1)
            split_hi(u + 2)
            act.wait_ge(rw_shifted_s, 1 + CREDIT)
            act.activation(lora[0:64, :], lora[0:64, :], ACT.Tanh).then_inc(rw_tanh_s, 1)

            def shifted(t0, n):
                with act.Fori(0, n // 2) as i:
                    for j in range(2):
                        b = U0["rwkv"] + t0 + j
                        act.wait_ge(rw_shifted_s, 2 * i + (t0 + j + 1))
                        take(tmp[:, b % 2, :], b % 2, 2 * i + (b + CREDIT + 1))
                        split_hi(b + 2, i, 2)

            shifted(1, 4)
            for part, (dst, bias) in enumerate(((rw_ld, "w0"), (rw_a, "a0"))):
                for j in range(CA):
                    act.wait_ge(rw_lora_mm_s, 4 * part + j + 1)
                    act.activation(dst[:, j, :], ps[:, 2 + (4 * part + j) % 6, :], ACT.Sigmoid,
                                   bias=V(bias, j)).then_inc(rw_sig_s, 1)
            shifted(5, 4)
            shifted(9, 2)
            act.wait_ge(rw_max_s, 1)
            act.activation(rw_n[:], rw_n[:], ACT.Ln).then_inc(rw_sqrt_s, 1)
            act.wait_ge(rw_sqrt_s, 1)
            act.activation(rw_n[:], rw_n[:], ACT.Exp, scale=-0.5).then_inc(rw_sqrt_s, 1)
            shifted(11, 2)
            act.wait_ge(rw_lc_s, 2)
            act.activation(rw_e[:], rw_L[:], ACT.Exp, scale=-1.0).then_inc(rw_e_s, 1)
            act.wait_ge(rw_e_s, 1)
            act.activation(rw_L[:], rw_L[:], ACT.Exp).then_inc(rw_e_s, 1)
            shifted(13, 2)
            act.activation(rw_ld[:], rw_ld[:], ACT.Exp).then_inc(rw_e_s, 1)
            act.activation(gfac[:], gfac[:], ACT.Exp).then_inc(rw_e_s, 1)
            shifted(15, 2)

            act.sem_inc(ch_y_s, 1)
            act.wait_ge(rw_prep_s, 2)
            act.wait_ge(rw_kt_s, CA)
            with act.Fori(0, NS) as c:
                act.wait_ge(ch_y_s, c + 1)
                act.activation(AR[:, :, 0, :], rw_kk[:, :, bass.ds(c * CH, CH)], ACT.Copy).then_inc(ch_ar_s, 1)
                act.activation(AR[:, :, 1, :], rw_r[:, :, bass.ds(c * CH, CH)], ACT.Copy).then_inc(ch_ar_s, 1)
                act.wait_ge(ch_turned_s, 3 * c + 1)
                act.activation(tok[:, 0, :, :], ps[:, 0, :].rearrange("p (j n) -> p j n", n=P), ACT.Copy).then_inc(ch_b_s, 1)
                act.wait_ge(ch_turned_s, 3 * c + 2)
                act.activation(tok[:, 1, :, :], ps[:, 1, :].rearrange("p (j n) -> p j n", n=P), ACT.Copy).then_inc(ch_k_s, 1)
                for h in range(8):
                    act.wait_ge(ch_ab_s, 8 * c + (h + 1))
                    act.activation(M[:, h, 1:4, :], ps[:, 3 + h % 4, P:4 * P].rearrange("p (a n) -> p a n", n=P),
                                   ACT.Copy).then_inc(ch_m_s, 1)
                act.wait_ge(ch_rh_mm_s, c + 1)
                act.activation(rh[:], ps[:, 1, :], ACT.Copy).then_inc(ch_rh_s, 1)
                NL = len(LEVELS) - 1
                for q in range(2):
                    act.wait_ge(ch_t1_s, 2 * c + (q + 1))
                    act.activation(X[:, 4 * q:4 * q + 4, :], ps[:, 5 + q, :].rearrange("p (h n) -> p h n", n=P),
                                   ACT.Copy).then_inc(ch_x0_s, 1)

                def level(idx):
                    for q in range(2):
                        act.wait_ge(ch_r_s, 2 * idx + (q + 3))
                        act.activation(R1[:, 4 * q:4 * q + 4, :], ps[:, 3 + q, :].rearrange("p (h n) -> p h n", n=P),
                                       ACT.Copy).then_inc(ch_rb_s, 1)

                with act.Fori(0, NL) as lv:
                    level(NL * c + lv)
                act.wait_ge(ch_sa_mm_s, c + 1)
                act.activation(sa[:], ps[:, 2, :], ACT.Copy).then_inc(ch_sa_s, 1)
                act.wait_ge(ch_y_mm_s, c + 1)
                act.activation(rw_r[:, :, bass.ds((c + 1) * CH - CH, CH)], ps[:, 3, :].rearrange("p (j n) -> p j n", n=P), ACT.Copy).then_inc(ch_y_s, 1)

            act.wait_ge(gn_mm_s, 1)
            act.activation(g_mu[:], ps[:, 0:4, :], ACT.Copy, scale=1.0 / HD_A).then_inc(gn_mu_s, 1)

            def group_norm(step):
                if step == 0:
                    act.wait_ge(gn_v2_s, 1)
                    act.activation(g_rs[:], g_rs[:], ACT.Ln).then_inc(gn_ln_s, 1)
                    act.wait_ge(gn_ln_s, 1)
                    act.activation(g_rs[:], g_rs[:], ACT.Exp, scale=-0.5).then_inc(gn_rs_s, 1)
                elif step == 1:
                    act.activation(g_sz[:], rw_z, ACT.Sigmoid).then_inc(gn_sig_s, 1)
                elif step == 4:
                    act.wait_ge(gn_out_s, 1)
                    act.activation(ys_hi[:, 0:CA, :], rw_r, ACT.Copy).then_inc(gn_hi_s, 1)

            def conv_hi(t):
                act.wait_ge(cv_out_s, t + 1)
                act.wait_ge(gn_lo_s, 1)
                act.activation(ys_hi[:, CA + t, :], cb[:, t % 2, 2, :], ACT.Copy).then_inc(cv_hi_s, 1)

            for j in range(16):
                t, c = j // 4, j % 4
                b = U0["conv"] + j
                if c == 0 and t >= 2:
                    act.wait_ge(cv_lo_s, t - 1)
                take(cb[:, t % 2, c, :], b % 2, b + CREDIT + 1)
                split_hi(b + 2)
                group_norm(j)
                if c == 1 and t:
                    conv_hi(t - 1)
                if c == 3:
                    act.wait_ge(evac, EV0["conv"] + j + CREDIT + 1)
                    act.activation(sg[:, t % 2, :], cb[:, t % 2, 3, :], ACT.Sigmoid).then_inc(cv_sig_s, 1)
            conv_hi(CA - 1)
            act.wait_ge(cv_lo_s, CA)
            act.dma_start(pool_n[:], pool_count).then_inc(pooln_in_s, 16)

            def pool_hi(j):
                act.wait_ge(pl_out_s, j + 1)
                act.activation(ys_hi[:, 2 * CA + j, :], cb[:, j % 2, 2, :], ACT.Copy).then_inc(pl_hi_s, 1)

            for j in range(CA):
                if j >= 2:
                    act.wait_ge(pl_lo_s, j - 1)
                for c in range(2):
                    b = U0["pool"] + 2 * j + c
                    take(cb[:, j % 2, c, :], b % 2, b + CREDIT + 1)
                    split_hi(b + 2)
                act.wait_ge(evac, EV0["pool"] + 2 * j + 2 + CREDIT)
                act.activation(sg[:, j % 2, :], cb[:, j % 2, 1, :], ACT.Sigmoid).then_inc(pl_sig_s, 1)
                if j:
                    pool_hi(j - 1)

            def step(m, b, i=0, first=False):
                st = (b - U0["branch"]) // 3
                for d in range(2):
                    act.wait_ge(br_taken_s, 8 * i + (2 * st + d + 1))
                    act.wait_ge(unit_done, 12 * i + (b + d + CREDIT + 1))
                    act.activation(gates[:, 2 * (m % 2) + d, :], ps[:, (b + d) % 2, :], ACT.Sigmoid).then_inc(evac, 1)
                    split_hi(b + d + 2, i, 12)
                if first:
                    pool_hi(CA - 1)
                act.wait_ge(unit_done, 12 * i + (b + 2 + CREDIT + 1))
                split_hi(b + 4, i, 12)

            for m in range(4):
                step(m, U0["branch"] + 3 * m, first=m == 0)
            for m in range(4):
                step(m, U0["branch"] + 12 + 3 * m)

            def merged_hi(k):
                act.wait_ge(br_sum_s, k + (2 * KB + 2))
                act.activation(mg_hi[:, k, :], Y[:, k, :], ACT.Copy).then_inc(mg_hi_made_s, 1)

            for m in range(4):
                step(m, U0["branch"] + 24 + 3 * m)
                for k in range(2 * m - 2, 2 * m):
                    if k >= 0:
                        merged_hi(k)
            for k in range(KB - 2, KB):
                merged_hi(k)
            for j in range(KB):
                b = U0["out"] + j
                take(Y[:, j, :], b % 2, b + CREDIT + 1)
                if b + 2 < UNITS:
                    split_hi(b + 2)
            act.activation(rstd[:], ps[:, (UNITS - 1) % 2, :], ACT.Square).then_inc(last_sq, 1)
            statistics("out", both=False)

        @block.gpsimd
        def _(pool):
            def split_lo(b, i=0, step=0):
                pool.wait_ge(whi_made, step * i + (b + 1))
                pool.tensor_tensor(w_lo[:, b % 2, :], stage[:, b % 2, :], w_hi[:, b % 2, :].bitcast(F32),
                                   ALU.subtract).then_inc(wlo_made, 1)

            split_lo(0)
            split_lo(1)
            with pool.Fori(0, 8) as i:
                for j in range(2):
                    split_lo(2 + j, i, 2)

            with pool.Fori(0, PAIRS // 2) as i:
                for c in range(6):
                    split_lo(U0["sb"] + 2 + c, i, 6)

            def squares(k, n, src):
                pool.wait_ge(acc2_made, k + 1 + BEFORE["acc2_made"][n])
                pool.tensor_tensor(square[:], src, src, ALU.mult).then_inc(sq_made, 1)
                pool.wait_ge(sq_made, k + 1 + BEFORE["sq_made"][n])
                pool.tensor_tensor(acc2[:], acc2[:], square[:], ALU.add).then_inc(acc2_made, 1)

            def tiles(n, units=1):
                pool.memset(acc2[:], 0.0).then_inc(acc2_made, 1)
                with pool.Fori(0, 3) as i:
                    for j in range(2):
                        for c in range(units):
                            split_lo(U0[n] + 2 + units * j + c, i, 2 * units)
                        pool.wait_ge(y_made, 2 * i + (j + 1 + CREDIT) + BEFORE["y_made"][n])
                        squares(2 * i + j, n, Y[:, 2 * i + j, :])
                for j in range(2):
                    for c in range(units):
                        split_lo(U0[n] + 2 + units * (KB - 2 + j) + c)
                    if j == 0:
                        pool.wait_ge(y_made, KB - 1 + CREDIT + BEFORE["y_made"][n])
                        squares(KB - 2, n, Y[:, KB - 2, :])

            def split_x(n):
                with pool.Fori(0, KB) as k:
                    pool.wait_ge(h_made, k + 1 + BEFORE["h_made"][n])
                    pool.wait_ge(xhi_made, k + 1 + BEFORE["xhi_made"][n])
                    pool.tensor_tensor(x_lo[:, k, :], H[:, k, :], x_hi[:, k, :].bitcast(F32),
                                       ALU.subtract).then_inc(x_ready, 1)

            tiles("wo")
            split_x("wo")
            with pool.Fori(0, 4) as i:
                for j in range(2):
                    split_lo(U0["xq"] + 2 + j, i, 2)
            tiles("xo")
            split_x("xo")
            pool.sem_inc(ff_made, 2)
            with pool.Fori(0, FFB // 2) as i:
                for j in range(4):
                    p = 2 * i + j // 2
                    split_lo(U0["up"] + 2 + j, i, 4)
                    if j % 2:
                        pool.wait_ge(ff_conv, 4 * i + (j + 1 + 4))
                        pool.tensor_tensor(conv[:, j, :], conv[:, j, :], conv[:, j - 1, :], ALU.mult).then_inc(ff_vg, 1)
                        pool.wait_ge(ff_hi, p + 1)
                        pool.tensor_tensor(f_lo[:, p, :], conv[:, j - 1, :], f_hi[:, p, :].bitcast(F32),
                                           ALU.subtract).then_inc(ff_made, 1)
            tiles("down", DOWN_UNITS)
            with pool.Fori(0, KB) as k:
                pool.wait_ge(xhi_made, k + 1 + BEFORE["xhi_made"]["pre"])
                pool.tensor_tensor(x_lo[:, k, :], Y[:, k, :], x_hi[:, k, :].bitcast(F32),
                                   ALU.subtract).then_inc(x_ready, 1)
            split_lo(U0["rwkv"] + 2)
            with pool.Fori(0, 6) as i:
                for j in range(2):
                    split_lo(U0["rwkv"] + 3 + j, i, 2)
            for j in range(CA):
                split_lo(U0["rwkv"] + 15 + j)
                pool.wait_ge(rw_barg_s, CA)
                pool.wait_ge(rw_e_s, 1)
                pool.tensor_tensor(rw_k[:, j, :], rw_k[:, j, :], rw_e[:, j, :], ALU.mult).then_inc(rw_kt_s, 1)
            pool.wait_ge(rw_prep_s, 1)
            pool.wait_ge(rw_kt_s, CA)
            pool.wait_ge(rw_bmm_s, CA)
            pool.memset(Sz[:], 0.0).then_inc(ch_s_s, 1)
            pool.sem_inc(ch_s_s, 1)
            pool.memset(scr[:], 0.0).then_inc(ch_wait_s, 1)
            pool.wait_ge(ch_wait_s, 1)
            pool.wait_ge(levels_in_s, 32)
            NL = len(LEVELS) - 1
            with pool.Fori(0, NS) as c:
                at_c = bass.ds(c * CH, CH)
                pool.wait_ge(ch_scored_s, 8 * c + 1)
                pool.tensor_tensor(scr[:, 9:10], scr[:, 0:1], scr[:, 0:1], ALU.mult)
                pool.tensor_copy(bkv[:, 0, :, :], rw_a[:, :, at_c]).then_inc(ch_bkv_s, 1)
                pool.tensor_copy(bkv[:, 1, :, :], rw_k[:, :, at_c]).then_inc(ch_bkv_s, 1)
                pool.tensor_copy(bkv[:, 2, :, :], rw_v[:, :, at_c]).then_inc(ch_bkv_s, 1)
                for h in range(8):
                    pool.wait_ge(ch_m_s, 8 * c + (h + 1))
                    pool.tensor_tensor(scr[:, h + 1:h + 2], scr[:, 0:1], scr[:, 0:1], ALU.mult)
                    pool.affine_select(M[:, h, 1, :], M[:, h, 1, :], pattern=[[1, P]], compare_op=ALU.is_ge,
                                       fill=0.0, base=0, channel_multiplier=-1)
                    pool.affine_select(M[:, h, 2:4, :], M[:, h, 2:4, :], pattern=[[1, 2], [1, P]], compare_op=ALU.is_gt,
                                       fill=0.0, base=0, channel_multiplier=-1).then_inc(ch_mask_s, 1)
                with pool.Fori(0, NL) as lv:
                    for q in range(2):
                        hs = slice(4 * q, 4 * q + 4)
                        pool.wait_ge(ch_ab_s, 8 * c + (4 * q + 4))
                        pool.wait_ge(ch_r_s, 2 * (NL * c + lv) + (q + 1))
                        pool.tensor_tensor(scr[:, 10 + q:11 + q], scr[:, 0:1], scr[:, 0:1], ALU.mult)
                        mask = levels[:, bass.ds(lv + 1, 1), :].to_broadcast([P, 4, P])
                        pool.tensor_tensor(Mk[:, hs, :], M[:, hs, 0, :], mask, ALU.mult).then_inc(ch_mk_s, 1)
            def conv_lo(t):
                pool.wait_ge(cv_hi_s, t + 1)
                pool.tensor_tensor(ys_lo[:, CA + t, :], cb[:, t % 2, 2, :], ys_hi[:, CA + t, :].bitcast(F32),
                                   ALU.subtract).then_inc(cv_lo_s, 1)

            for j in range(16):
                split_lo(U0["conv"] + 2 + j)
                if j == 4:
                    pool.wait_ge(gn_hi_s, 1)
                    pool.tensor_tensor(ys_lo[:, 0:CA, :], rw_r, ys_hi[:, 0:CA, :].bitcast(F32), ALU.subtract).then_inc(gn_lo_s, 1)
                if j % 4 == 1 and j > 4:
                    conv_lo(j // 4 - 1)
            conv_lo(CA - 1)

            def pool_lo(j):
                pool.wait_ge(pl_hi_s, j + 1)
                pool.tensor_tensor(ys_lo[:, 2 * CA + j, :], cb[:, j % 2, 2, :], ys_hi[:, 2 * CA + j, :].bitcast(F32),
                                   ALU.subtract).then_inc(pl_lo_s, 1)

            for j in range(CA):
                for c in range(2):
                    split_lo(U0["pool"] + 2 * j + c + 2)
                if j:
                    pool_lo(j - 1)
            for c in range(12):
                split_lo(U0["branch"] + 2 + c)
                if c == 1:
                    pool_lo(CA - 1)
            for c in range(12, 24):
                split_lo(U0["branch"] + 2 + c)

            def merged_lo(k):
                pool.wait_ge(mg_hi_made_s, k + 1)
                pool.tensor_tensor(mg_lo[:, k, :], Y[:, k, :], mg_hi[:, k, :].bitcast(F32),
                                   ALU.subtract).then_inc(mg_ready_s, 1)

            for m in range(4):
                for c in range(3):
                    split_lo(U0["branch"] + 24 + 3 * m + 2 + c)
                for k in range(2 * m - 2, 2 * m):
                    if k >= 0:
                        merged_lo(k)
            for k in range(KB - 2, KB):
                merged_lo(k)
            pool.wait_ge(mg_ready_s, KB)
            pool.memset(acc2[:], 0.0).then_inc(acc2_made, 1)
            for j in range(KB):
                if U0["out"] + j + 2 < UNITS:
                    split_lo(U0["out"] + j + 2)
                if j < KB - 1:
                    pool.wait_ge(evac, EV0["out"] + j + 1 + CREDIT)
                    squares(j, "out", Y[:, j, :])

        @block.vector
        def _(dve):
            dve.sem_inc(mv_taken, CREDIT)
            for a in range(2):
                at_a = slice(4 * a, 4 * a + 4)
                dve.wait_ge(m_hi_made, a + 1)
                dve.tensor_tensor(m_lo[:, at_a, :], mem[:, at_a, :], m_hi[:, at_a, :].bitcast(F32),
                                  ALU.subtract).then_inc(m_split, 1)
            dve.wait_ge(x_in, 16)
            dve.tensor_copy(x_hi[:], H[:]).then_inc(xin_hi, 1)
            dve.wait_ge(xin_hi, 1)
            dve.tensor_tensor(x_lo[:], H[:], x_hi[:].bitcast(F32), ALU.subtract).then_inc(h_split, 1)
            with dve.Fori(0, 4) as i:
                for j in range(2):
                    dve.wait_ge(mv_turned, 2 * i + (j + 1 + CREDIT))
                    dve.tensor_copy(mem_v[:, :, bass.ds((2 * i + j) * P, P)],
                                    ps[:, 2 + j, 0:MEM].rearrange("p (t n) -> p t n", t=2)).then_inc(mv_taken, 1)

            def pair(g, first=False):
                for h in range(2):
                    dve.wait_ge(sb_ln, 2 * g + (h + 1))
                    dve.scalar_tensor_tensor(out=keep[h][:], in0=scores(h)[:, 0:SCORES], scalar=0.0, in1=soft[h][:],
                                             op0=ALU.max, op1=ALU.add).then_inc(sb_keep, 1)
                    dve.wait_ge(sb_keep, 2 * g + (h + 1))
                    dve.tensor_copy(keep_hi[h][:], keep[h][:]).then_inc(sb_khi, 1)
                    dve.wait_ge(sb_khi, 2 * g + (h + 1))
                    dve.tensor_tensor(keep_lo[h][:], keep[h][:], keep_hi[h][:].bitcast(F32),
                                      ALU.subtract).then_inc(sb_klo, 1)
                dve.wait_ge(sb_vturn, g + 1)
                dve.tensor_copy(v_sb[:], ps[:, 0, :].rearrange("p (t n) -> p t n", t=NS)).then_inc(sb_v, 1)
                if not first:
                    outputs(g - 1)

            def outputs(g, bank=1):
                dve.wait_ge(sb_ohi, g + 1)
                dve.tensor_tensor(o_lo[:, g, :], ps[:, bank, :], o_hi[:, g, :].bitcast(F32), ALU.subtract).then_inc(sb_o, 1)

            pair(0, first=True)
            pair(1)
            with dve.Fori(1, PAIRS // 2) as i:
                pair(2 * i)
                pair(2 * i + 1)
            outputs(PAIRS - 1, 2)

            def tiles(n):
                dve.sem_inc(y_made, CREDIT)
                dve.memset(acc[:], 0.0).then_inc(acc_made, 1)
                with dve.Fori(0, KB // 2 - 1) as i:
                    for j in range(2):
                        tile(n, 2 * i + j, j)
                        add(n, 2 * i + j)
                tile(n, KB - 2, 0)
                add(n, KB - 2)
                tile(n, KB - 1, 1)

            def tile(n, k, j):
                dve.wait_ge(evac, k + (EV0[n] + CREDIT + 1))
                dve.scalar_tensor_tensor(out=Y[:, k, :], in0=H[:, k, :], scalar=ALPHA, in1=tmp[:, j, :],
                                         op0=ALU.mult, op1=ALU.add).then_inc(y_made, 1)

            def add(n, k):
                dve.wait_ge(y_made, k + (1 + CREDIT + BEFORE["y_made"][n]))
                dve.wait_ge(acc_made, k + (1 + BEFORE["acc_made"][n]))
                dve.tensor_tensor(acc[:], acc[:], Y[:, k, :], ALU.add).then_inc(acc_made, 1)

            def centre(n, k):
                dve.tensor_tensor(Y[:, k, :], Y[:, k, :], mean[:], ALU.subtract).then_inc(centred, 1)

            def scale(n, k):
                dve.wait_ge(centred, k + (1 + BEFORE["centred"][n]))
                dve.tensor_tensor(Y[:, k, :], Y[:, k, :], rstd[:], ALU.mult).then_inc(normed, 1)

            def norm(n):
                dve.wait_ge(mean_made, 1 + BEFORE["mean_made"][n])
                centre(n, 0)
                dve.wait_ge(msq_made, 1 + BEFORE["msq_made"][n])
                dve.wait_ge(sums_done, 2 + BEFORE["sums_done"][n])
                dve.scalar_tensor_tensor(out=rstd[:], in0=ps[:, 3, :], scalar=LN_EPS, in1=square[:], op0=ALU.add,
                                         op1=ALU.subtract).then_inc(var_made0, 1)
                dve.wait_ge(var_made0, 1 + BEFORE["var_made0"][n])
                dve.tensor_scalar(rstd[:], rstd[:], LN_EPS, None, ALU.max).then_inc(var_made, 1)
                for k in range(1, 4):
                    centre(n, k)
                dve.wait_ge(rstd_made, 1 + BEFORE["rstd_made"][n])
                for k in range(KB):
                    scale(n, k)
                    if k + 4 < KB:
                        centre(n, k + 4)

            tiles("wo")
            norm("wo")

            def xa_soft(h):
                dve.wait_ge(xa_scored, h + 1)
                for b in range(2):
                    dve.tensor_reduce(soft_max[:, h, 2 * b:2 * b + 2],
                                      ps[:, 2 + b, :].rearrange("p (t n) -> p t n", t=2), mybir.AxisListType.X,
                                      ALU.max).then_inc(xa_max, 1)
                dve.wait_ge(xa_max, 2 * h + 2)
                dve.tensor_scalar(soft_max[:, h, :], soft_max[:, h, :], -float(D // XA_HEADS) ** -0.5, None,
                                  ALU.mult).then_inc(xa_nmax, 1)
                dve.wait_ge(xa_exp, NS * (h + 1))
                dve.reciprocal(soft_sum[:, h, :], soft_sum[:, h, :]).then_inc(xa_rec, 1)
                dve.wait_ge(xa_rec, h + 1)
                dve.tensor_tensor(prob[:, h % 2, :, :], prob[:, h % 2, :, :],
                                  soft_sum[:, h, :].unsqueeze(2).to_broadcast([P, NS, MEM]), ALU.mult).then_inc(xa_prob, 1)

            def xa_take(h):
                dve.wait_ge(xa_turned, 2 * h + 2)
                if h >= 2:
                    dve.wait_ge(xa_pv, 2 * (h - 1))
                dve.tensor_copy(probT[:, h % 2, 1, :], ps[:, 5, :]).then_inc(xa_pT1, 1)
                for d in range(2):
                    dve.wait_ge(xa_ohi, 2 * h + d + 1)
                    dve.tensor_tensor(o_lo[:, 2 * h + d, :], ps[:, 6 + d, :], o_hi[:, 2 * h + d, :].bitcast(F32),
                                      ALU.subtract).then_inc(xa_o, 1)

            for h in range(XA_HEADS):
                if h:
                    xa_take(h - 1)
                xa_soft(h)
            xa_take(XA_HEADS - 1)
            tiles("xo")
            norm("xo")

            C_GELU = 2.0 * float(np.sqrt(2.0 / np.pi))
            dve.sem_inc(ff_conv, 4)
            dve.sem_inc(ff_f, 2)
            with dve.Fori(0, FFB // 2) as i:
                for j in range(4):
                    p = 2 * i + j // 2
                    tap = lambda c: V("ffn_conv", (2 * c + j % 2) * FFB + p)
                    dve.wait_ge(evac, 4 * i + (EV0["up"] + j + CREDIT + 1))
                    dve.wait_ge(ff_made, p + 1)
                    dve.tensor_scalar(conv[:, j, :], raw[:, j, :], tap(2), V("ffn_conv_b", (j % 2) * FFB + p),
                                      ALU.mult, ALU.add).then_inc(ff_tap, 1)
                    dve.wait_ge(ff_tap, 8 * i + (2 * j + 1))
                    dve.scalar_tensor_tensor(out=conv[:, j, 1:SEQ], in0=raw[:, j, 0:SEQ - 1], scalar=tap(1),
                                             in1=conv[:, j, 1:SEQ], op0=ALU.mult, op1=ALU.add).then_inc(ff_tap, 1)
                    dve.wait_ge(ff_tap, 8 * i + (2 * j + 2))
                    dve.scalar_tensor_tensor(out=conv[:, j, 2:SEQ], in0=raw[:, j, 0:SEQ - 2], scalar=tap(0),
                                             in1=conv[:, j, 2:SEQ], op0=ALU.mult, op1=ALU.add).then_inc(ff_conv, 1)
                    gt = gate_t[:, j // 2, :]
                    if j % 2 == 0:
                        dve.wait_ge(ff_conv, 4 * i + (j + 1 + 4))
                        dve.tensor_tensor(gt, conv[:, j, :], conv[:, j, :], ALU.mult).then_inc(ff_sq, 1)
                    else:
                        dve.wait_ge(ff_sq, p + 1)
                        dve.tensor_scalar(gt, gt, 0.044715 * C_GELU, C_GELU, ALU.mult, ALU.add).then_inc(ff_poly, 1)
                        dve.wait_ge(ff_poly, p + 1)
                        dve.tensor_tensor(gt, gt, conv[:, j - 1, :], ALU.mult).then_inc(ff_arg, 1)
                        dve.wait_ge(ff_sig, p + 1)
                        dve.wait_ge(ff_vg, p + 1)
                        dve.tensor_tensor(conv[:, j - 1, :], conv[:, j, :], gt, ALU.mult).then_inc(ff_f, 1)
            tiles("down")
            norm("down")
            chain = [0]

            def link(ins):
                chain[0] += 1
                ins.then_inc(rw_link_s, 1)
                dve.wait_ge(rw_link_s, chain[0])

            dve.wait_ge(sums_done, KB + BEFORE["sums_done"]["pre"])
            dve.tensor_scalar(rstd[:], ps[:, 4, :], RMS_EPS, None, ALU.add).then_inc(var_made, 1)
            dve.wait_ge(rstd_made, 1 + BEFORE["rstd_made"]["pre"])
            with dve.Fori(0, KB) as k:
                dve.scalar_tensor_tensor(out=Y[:, k, :], in0=H[:, k, :], scalar=V("pre", k), in1=rstd[:],
                                         op0=ALU.mult, op1=ALU.mult).then_inc(normed, 1)

            link(dve.tensor_scalar(omm[:], vcol[:, V0["mu"]:V0["mu"] + 17], -1.0, 1.0, ALU.mult, ALU.add))
            dve.sem_inc(rw_shifted_s, CREDIT)

            def shift(dst, t, m, n):
                dve.wait_ge(evac, t + (EV0["rwkv"] + CREDIT + 1))
                dve.tensor_scalar(dst, tmp[:, n, :], omm[:, bass.ds(m, 1)], None, ALU.mult).then_inc(rw_shift0_s, 1)
                dve.wait_ge(rw_shift0_s, t + 1)
                dve.scalar_tensor_tensor(out=dst[:, 1:SEQ], in0=tmp[:, n, 0:SEQ - 1], scalar=V("mu", m), in1=dst[:, 1:SEQ],
                                         op0=ALU.mult, op1=ALU.add).then_inc(rw_shifted_s, 1)

            def shifts(buf, first, t0, n):
                with dve.Fori(0, n // 2) as i:
                    for j in range(2):
                        shift(buf[:, 2 * i + (first + j), :], 2 * i + (t0 + j), 2 * i + (t0 + j - 1),
                              (U0["rwkv"] + t0 + j) % 2)

            shift(lora[:], 0, 16, U0["rwkv"] % 2)
            shifts(rw_rk, 0, 1, 4)
            dve.wait_ge(rw_sig_s, 4)
            link(dve.tensor_scalar(rw_ld[:], rw_ld[:], DECAY, None, ALU.mult))
            dve.wait_ge(levels_in_s, 32)
            for j in range(CA):
                dve.tensor_tensor_scan(rw_L[:, j, :], scan_keep[:], rw_ld[:, j, :], 0.0, ALU.mult, ALU.add).then_inc(rw_scan_s, 1)
            shifts(rw_rk, 4, 5, 4)
            dve.wait_ge(rw_shifted_s, 9 + CREDIT)
            for j in range(CA):
                link(dve.tensor_scalar(rw_kk[:, j, :], rw_k[:, j, :], V("k_k", j), None, ALU.mult))
            dve.tensor_tensor(rw_t[:], rw_kk[:], rw_kk[:], ALU.mult).then_inc(rw_kksq_s, 1)
            dve.wait_ge(rw_scan_s, CA)
            L = rw_L[:].rearrange("p j (c n) -> p j c n", n=CH)
            link(dve.tensor_scalar(cen[:], L[:, :, :, CH - 1], 0.5, None, ALU.mult))
            Lf = rw_L[:].rearrange("p j (c n) -> p (j c) n", n=CH)
            dve.tensor_tensor(Lf, Lf, cen[:].rearrange("p j c -> p (j c)").unsqueeze(2).to_broadcast([P, CA * NS, CH]),
                              ALU.subtract).then_inc(rw_lc_s, 1)
            dve.wait_ge(rw_lc_s, 1)
            shifts(rw_vz, 0, 9, 2)
            dve.wait_ge(rw_ss_mm_s, CA)
            dve.tensor_scalar(rw_n[:], ps[:, 4:8, :], 1e-24, None, ALU.max).then_inc(rw_max_s, 1)
            link(dve.tensor_tensor(gfac[:, :, 0:NS - 1], cen[:, :, 0:NS - 1], cen[:, :, 1:NS], ALU.add))
            link(dve.tensor_copy(gfac[:, :, NS - 1:NS], cen[:, :, NS - 1:NS]))
            dve.tensor_tensor(rw_ld[:], rw_L[:], rw_ld[:], ALU.subtract).then_inc(rw_lc_s, 1)
            dve.wait_ge(rw_sig_s, 8)
            for j in range(CA):
                link(dve.tensor_scalar(rw_t[:, j, :], rw_a[:, j, :], V("k_a", j), V("k_a", j), ALU.mult, ALU.subtract))
                link(dve.scalar_tensor_tensor(out=rw_k[:, j, :], in0=rw_t[:, j, :], scalar=1.0, in1=rw_k[:, j, :],
                                              op0=ALU.add, op1=ALU.mult))
            shifts(rw_vz, 2, 11, 2)
            for j in range(CA):
                dve.scalar_tensor_tensor(out=rw_t[:, j, :], in0=rw_r[:, j, :], scalar=V("r_k", j), in1=rw_k[:, j, :],
                                         op0=ALU.mult, op1=ALU.mult).then_inc(rw_barg_s, 1)
            dve.wait_ge(rw_sqrt_s, 2)
            link(dve.tensor_tensor(rw_kk[:], rw_kk[:], rw_n[:], ALU.mult))
            shifts(rw_vz, 4, 13, 2)
            dve.wait_ge(rw_barg_s, CA)
            link(dve.tensor_tensor(rw_a[:], rw_a[:], rw_kk[:], ALU.mult))
            dve.wait_ge(rw_e_s, 2)
            link(dve.tensor_tensor(rw_a[:], rw_a[:], rw_e[:], ALU.mult))
            dve.sem_inc(rw_prep_s, 1)
            shifts(rw_vz, 6, 15, 2)
            dve.wait_ge(rw_shifted_s, 17 + CREDIT)
            link(dve.tensor_tensor(rw_r, rw_r, rw_L[:], ALU.mult))
            dve.wait_ge(rw_e_s, 4)
            link(dve.scalar_tensor_tensor(out=rw_kk[:], in0=rw_kk[:], scalar=-1.0, in1=rw_ld[:], op0=ALU.mult, op1=ALU.mult))
            dve.sem_inc(rw_prep_s, 1)
            dve.wait_ge(rw_bmm_s, CA)
            for j in range(CA):
                dve.tensor_tensor(rw_L[:, j, :], ps[:, 4 + j, :], rw_v[:, j, :], ALU.mult).then_inc(rw_bonus_s, 1)

            dve.sem_inc(ch_xn_s, 2)
            dve.sem_inc(ch_yn_s, 2)
            NL = len(LEVELS) - 1
            strict = C("strict")
            by_head = lambda m: m.unsqueeze(1).to_broadcast([P, 4, P])
            with dve.Fori(0, NS) as c:
                dve.wait_ge(ch_turned_s, 3 * c + 3)
                dve.tensor_copy(tok[:, 2, :, :], ps[:, 2, :].rearrange("p (j n) -> p j n", n=P)).then_inc(ch_vt_s, 1)
                for h in range(8):
                    dve.wait_ge(ch_scored_s, 8 * c + (h + 2))
                    dve.tensor_tensor(M[:, h, 0, :], ps[:, 3 + h % 4, 0:P], strict, ALU.mult).then_inc(ch_ab_s, 1)
                for q in range(2):
                    hs = slice(4 * q, 4 * q + 4)
                    dve.wait_ge(ch_ab_s, 8 * c + 4 * q + 4)
                    dve.tensor_tensor(Tt[:, hs, :], M[:, hs, 0, :], by_head(levels[:, 0, :]), ALU.mult).then_inc(ch_tt0_s, 1)
                    dve.wait_ge(ch_tt0_s, 2 * c + (q + 1))
                    dve.tensor_tensor(Tt[:, hs, :], Tt[:, hs, :], by_head(ident), ALU.add).then_inc(ch_y1_s, 1)

                def update(idx, x_idx, with_x):
                    for q in range(2):
                        hs = slice(4 * q, 4 * q + 4)
                        view = lambda b: ps[:, b, :].rearrange("p (h n) -> p h n", n=P)
                        if with_x:
                            dve.wait_ge(ch_xmm_s, 2 * x_idx + (q + 1))
                            dve.tensor_tensor(X[:, hs, :], X[:, hs, :], view(5 + q), ALU.add).then_inc(ch_xn_s, 1)
                        dve.wait_ge(ch_ymm_s, 2 * idx + (q + 1))
                        dve.tensor_tensor(Tt[:, hs, :], Tt[:, hs, :], view((7, 0)[q]), ALU.add).then_inc(ch_yn_s, 1)

                with dve.Fori(0, NL - 1) as lv:
                    idx = NL * c + lv
                    update(idx, (NL - 1) * c + lv, True)
                update(NL * c + (NL - 1), None, False)
                dve.wait_ge(ch_s_mm_s, c + 1)
                for r in range(2):
                    rows = slice(64 * r, 64 * r + 64)
                    S = Sz[rows, r::2, :]
                    dve.wait_ge(ch_y_mm_s, c + 1)
                    dve.tensor_tensor(S, S, ps[rows, 4, 0:CA * HD_A].rearrange("p (j n) -> p j n", n=HD_A),
                                      ALU.add).then_inc(ch_s0_s, 1)
                    dve.wait_ge(ch_s0_s, 2 * c + (r + 1))
                    dve.tensor_tensor(S, S, gfac[rows, :, bass.ds(c, 1)].to_broadcast([64, CA, HD_A]),
                                      ALU.mult).then_inc(ch_s_s, 1)

            dve.wait_ge(ch_y_s, NS + 1)
            dve.tensor_tensor(g_sq[:], rw_r, rw_r, ALU.mult).then_inc(gn_sq_s, 1)
            dve.wait_ge(gn_mu_s, 1)
            dve.wait_ge(gn_sq_s, 1)
            link(dve.tensor_tensor(rw_r, rw_r, g_mu[:], ALU.subtract))
            link(dve.tensor_tensor(g_mu[:], g_mu[:], g_mu[:], ALU.mult))
            dve.scalar_tensor_tensor(out=g_rs[:], in0=ps[:, 4:8, :], scalar=1.0 / HD_A, in1=g_mu[:], op0=ALU.mult,
                                     op1=ALU.subtract).then_inc(gn_v_s, 1)
            dve.wait_ge(gn_v_s, 1)
            dve.tensor_scalar(g_rs[:], g_rs[:], 0.0, GN_EPS, ALU.max, ALU.add).then_inc(gn_v2_s, 1)
            dve.wait_ge(gn_rs_s, 1)
            link(dve.tensor_tensor(rw_r, rw_r, g_rs[:], ALU.mult))
            for j in range(CA):
                link(dve.tensor_scalar(rw_r[:, j, :], rw_r[:, j, :], V("gn_w", j), V("gn_b", j), ALU.mult, ALU.add))
            link(dve.tensor_tensor(rw_r, rw_r, rw_L[:], ALU.add))
            dve.wait_ge(gn_sig_s, 1)
            link(dve.tensor_tensor(rw_r, rw_r, rw_z, ALU.mult))
            dve.tensor_tensor(rw_r, rw_r, g_sz[:], ALU.mult).then_inc(gn_out_s, 1)

            with dve.Fori(0, 2) as i:
                for p in range(2):
                    B, Cc, Uu, Z = (cb[:, p, n, :] for n in range(4))
                    at_0 = 14 * i + 7 * p
                    n_link = [0]

                    def step(ins):
                        n_link[0] += 1
                        ins.then_inc(cv_link_s, 1)
                        dve.wait_ge(cv_link_s, 12 * i + (6 * p + n_link[0]))

                    tap = lambda n: V("conv_w", 2 * i + (n * CA + p))
                    dve.wait_ge(evac, 8 * i + (EV0["conv"] + 4 * p + 3 + CREDIT))
                    step(dve.tensor_tensor(Cc, Cc, Uu, ALU.mult))
                    step(dve.tensor_scalar(Uu, Cc, tap(2), None, ALU.mult))
                    step(dve.scalar_tensor_tensor(out=Uu[:, 1:SEQ], in0=Cc[:, 0:SEQ - 1], scalar=tap(1), in1=Uu[:, 1:SEQ],
                                                  op0=ALU.mult, op1=ALU.add))
                    step(dve.scalar_tensor_tensor(out=Uu[:, 2:SEQ], in0=Cc[:, 0:SEQ - 2], scalar=tap(0), in1=Uu[:, 2:SEQ],
                                                  op0=ALU.mult, op1=ALU.add))
                    step(dve.tensor_tensor(Uu, Uu, B, ALU.mult))
                    dve.wait_ge(evac, 8 * i + (EV0["conv"] + 4 * p + 4 + CREDIT))
                    dve.wait_ge(cv_sig_s, 2 * i + (p + 1))
                    step(dve.tensor_tensor(Uu, Uu, Z, ALU.mult))
                    dve.tensor_tensor(Uu, Uu, sg[:, p, :], ALU.mult).then_inc(cv_out_s, 1)

            dve.sem_inc(br_taken_s, 4)

            def pool_out(j):
                B = cb[:, j % 2, :, :]
                dve.wait_ge(pl_mm_s, j + 1)
                dve.wait_ge(pl_sig_s, j + 1)
                link(dve.scalar_tensor_tensor(out=B[:, 2, :], in0=ps[:, 2 + j % 2, :], scalar=V("pool_scale", j),
                                              in1=B[:, 1, :], op0=ALU.mult, op1=ALU.mult))
                dve.tensor_tensor(B[:, 2, :], B[:, 2, :], sg[:, j % 2, :], ALU.mult).then_inc(pl_out_s, 1)

            dve.wait_ge(pooln_in_s, 16)
            for j in range(CA):
                src = cb[:, j % 2, 0, :]
                dve.wait_ge(evac, EV0["pool"] + 2 * j + 1 + CREDIT)
                if j >= 2:
                    dve.wait_ge(pl_mm_s, j - 1)
                width, cur, n = 1, src, 0
                while width < POOL_WINDOWS[j]:
                    nxt = pt[:, n % 2, :]
                    link(dve.tensor_copy(nxt[:, 0:width], cur[:, 0:width]))
                    link(dve.tensor_tensor(nxt[:, width:SEQ], cur[:, width:SEQ], cur[:, 0:SEQ - width], ALU.add))
                    cur, width, n = nxt, 2 * width, n + 1
                link(dve.tensor_tensor(pld[:, j % 2, :], cur, pool_n[:, j, :], ALU.mult))
                dve.tensor_tensor(pld[:, j % 2, :], pld[:, j % 2, :], src, ALU.subtract).then_inc(pl_pooled_s, 1)
                if j:
                    pool_out(j - 1)
            pool_out(CA - 1)

            dve.wait_ge(pl_lo_s, CA)
            dve.memset(Y[:], 0.0).then_inc(br_sum_s, 1)

            def step(m, b, i=0, first=False):
                st = (b - U0["branch"]) // 3
                dve.wait_ge(unit_done, 12 * i + (b + 2 + CREDIT + 1))
                for d in range(2):
                    g = 2 * (m % 2) + d
                    dve.wait_ge(evac, 8 * i + (EV0["branch"] + 2 * st + d + 1 + CREDIT))
                    dve.tensor_tensor(bt[:, g, :], gates[:, g, :], ps[:, 4 + g, :], ALU.mult).then_inc(br_taken_s, 1)
                    dve.wait_ge(br_taken_s, 8 * i + (2 * st + d + 1 + 4))
                    dve.wait_ge(br_sum_s, 8 * i + (2 * st + d + 1))
                    dve.tensor_tensor(Y[:, 2 * m + d, :], Y[:, 2 * m + d, :], bt[:, g, :], ALU.add).then_inc(br_sum_s, 1)

            for m in range(4):
                step(m, U0["branch"] + 3 * m, first=m == 0)
            with dve.Fori(1, 3) as i:
                for m in range(4):
                    step(m, U0["branch"] + 3 * m, i)

            dve.wait_ge(sums_done, 1 + BEFORE["sums_done"]["out"])
            dve.tensor_scalar(rstd[:], ps[:, 3, :], RMS_EPS, None, ALU.add).then_inc(var_made, 1)
            dve.wait_ge(rstd_made, 1 + BEFORE["rstd_made"]["out"])
            with dve.Fori(0, KB) as k:
                dve.scalar_tensor_tensor(out=Y[:, k, :], in0=Y[:, k, :], scalar=V("post", k), in1=rstd[:],
                                         op0=ALU.mult, op1=ALU.mult).then_inc(fin0_s, 1)
                dve.wait_ge(fin0_s, k + 1)
                dve.tensor_tensor(H[:, k, :], H[:, k, :], Y[:, k, :], ALU.add).then_inc(fin_s, 1)


_INS = ["w", "xT", "memT", "vec", "const", "small", "pool_count"]


def lay_out(i):
    def in_tiles(a):
        k, n = a.shape
        return a.reshape(k // P, P, n // P, P).transpose(2, 1, 0, 3).reshape(n // P, P, k)

    f = lambda a: np.asarray(a)
    sb = in_tiles(f(i["sb_win"])[0])
    sb = np.stack([sb[0:8], sb[8:16], sb[16:24]], 1).reshape(24, P, UNIT)
    up = in_tiles(f(i["ffn_up"])[0])
    up = np.stack([up[:FFB], up[FFB:]], 1).reshape(2 * FFB, P, UNIT)
    down = in_tiles(f(i["ffn_down"])[0])
    down = np.concatenate([down, np.zeros((KB, P, 2 * P), down.dtype)], 2)
    down = down.reshape(KB, P, DOWN_UNITS, UNIT).transpose(0, 2, 1, 3).reshape(KB * DOWN_UNITS, P, UNIT)
    win = f(i["w_in_2"])[0]
    rw = in_tiles(win[:, :2176])
    rw = np.concatenate([rw[16:], rw[:16]])
    cv = in_tiles(win[:, 2176:4224]).reshape(4, 4, P, UNIT).transpose(1, 0, 2, 3).reshape(16, P, UNIT)
    po = in_tiles(win[:, 4224:5248]).reshape(2, 4, P, UNIT).transpose(1, 0, 2, 3).reshape(8, P, UNIT)
    ga = in_tiles(win[:, 5248:]).reshape(3, 4, 2, P, UNIT)
    br = np.stack([in_tiles(b) for b in f(i["w_branch_2"])[0]])
    br = br.reshape(3, 4, 2, P, 512).transpose(0, 1, 3, 2, 4).reshape(3, 4, 1, P, UNIT)
    br = np.concatenate([ga, br], 2).reshape(36, P, UNIT)
    w = np.concatenate([in_tiles(f(i["xa_wkv"])[0]), sb, in_tiles(f(i["mix_wo"])[0]), in_tiles(f(i["xa_wq"])[0]),
                        in_tiles(f(i["xa_wo"])[0]), up, down, rw, cv, po, br, in_tiles(f(i["w_out_2"])[0])])
    assert w.shape == (UNITS, P, UNIT)
    col = lambda a: f(a).reshape(-1, P).T
    vec = np.concatenate([col(i[n]) for n in (
        "ln_g", "ln_b", "ffn_conv", "ffn_conv_b", "pre_norm_w_2", "post_norm_w_2", "mu_shift_2", "rwkv_w0_2",
        "rwkv_a0_2", "rwkv_k_k_2", "rwkv_k_a_2", "rwkv_r_k_2", "rwkv_gn_w_2", "rwkv_gn_b_2", "conv_w_2",
        "pool_scale_2")], 1)
    assert vec.shape == (P, VEC)
    small = np.concatenate([np.concatenate([f(i["rwkv_w_up_2"])[0], f(i["rwkv_a_up_2"])[0]]),
                            f(i["pool_w_2"])[0].transpose(1, 0, 2).reshape(P, 512)], 1)
    r, c = np.arange(P)[:, None], np.arange(P)[None]
    f32 = np.float32
    t = np.arange(SEQ)
    const = np.concatenate([
        np.eye(P, dtype=f32), np.full((P, P), 1.0 / D, f32), (r // HD_A == c // HD_A).astype(f32),
        -(r >= c).astype(f32), np.full((P, P), -1.0, f32), (r >= c) * f32(-2.0 ** 100), (r < c).astype(f32),
        *[((r // b % 2 == 0) & (c // b == r // b + 1)).astype(f32) for b in LEVELS],
        np.broadcast_to((t % CH != 0).astype(f32), (P, SEQ))], 1)
    count = np.stack([1.0 / np.minimum(t + 1, n) for n in POOL_WINDOWS]).astype(f32)
    count = np.ascontiguousarray(np.broadcast_to(count, (P, 4, SEQ)))
    act = lambda a: a.reshape(a.shape[0], KB, P).transpose(2, 1, 0)
    out = dict(w=w, xT=act(f(i["x"])[0]), memT=act(f(i["mem"])[0]), vec=vec, const=const, small=small, pool_count=count)
    return {k: np.ascontiguousarray(v) for k, v in out.items()}


def kernel(**inputs):
    import numpy as _np
    import concourse.bacc as _bacc
    from concourse import mybir as _mybir
    from concourse.bass_utils import run_bass_kernel_spmd as _run

    nc = _bacc.Bacc("TRN2", target_bir_lowering=False, num_devices=1)
    arrays = lay_out(inputs)
    args = [nc.dram_tensor(n, arrays[n].shape, _mybir.dt.float32, kind="ExternalInput").ap() for n in _INS]
    args.append(nc.dram_tensor("outT", (P, KB, SEQ), _mybir.dt.float32, kind="ExternalOutput").ap())
    build_block(nc, *args)
    got = _run(nc, [arrays], core_ids=[0]).results[0]["outT"]
    return _np.ascontiguousarray(_np.asarray(got).transpose(2, 1, 0).reshape(1, SEQ, D))
```
